# Optimizing a Trainium2 kernel written in Bass

```python
import jax, jax.numpy as jnp
from jax import lax
import numpy as np
import math

D_MODEL = 1024
BATCH = 1
SEQ = 512
DEPTH = 1

CHUNK = 64
Q_BLOCK = 128
A_HEADS = 8
A_HEAD_DIM = D_MODEL // 16
A_WIDTH = A_HEADS * A_HEAD_DIM
POOL_WINDOWS = (2, 4, 8, 16)
POOL_GROUPS = len(POOL_WINDOWS)
POOL_WIDTH = D_MODEL // 4
POOL_GROUP_DIM = POOL_WIDTH // POOL_GROUPS
CONV_WIDTH = D_MODEL // 4
CONV_K = 3
N_BRANCH = 3
MIX_WIDTH = A_WIDTH + POOL_WIDTH + CONV_WIDTH
D_FF = 4 * D_MODEL
RMS_EPS = 1e-6
NEG_INF = -1e30
IN_COLS = 3 * A_WIDTH + A_HEADS + POOL_WIDTH + 3 * CONV_WIDTH + N_BRANCH * D_MODEL


def rmsnorm(x, g):
    xf = x.astype(jnp.float32)
    y = xf * lax.rsqrt(jnp.mean(xf * xf, axis=-1, keepdims=True) + RMS_EPS)
    return (y * g.astype(jnp.float32)).astype(x.dtype)

def forgetting_attention(q, k, v, f_logit):
    b, s, h, dh = q.shape
    q = q.transpose(0, 2, 1, 3)
    k = k.transpose(0, 2, 1, 3)
    v = v.transpose(0, 2, 1, 3)
    log_f = jax.nn.log_sigmoid(f_logit.astype(jnp.float32))
    cum_f = jnp.cumsum(log_f, axis=1).transpose(0, 2, 1)
    scale = dh ** -0.5
    outs = []
    for i in range(s // Q_BLOCK):
        qs, qe = i * Q_BLOCK, (i + 1) * Q_BLOCK
        qb = q[:, :, qs:qe]
        kb = k[:, :, :qe]
        vb = v[:, :, :qe]
        logits = jnp.einsum('bhqd,bhkd->bhqk', qb, kb).astype(jnp.float32) * scale
        logits = logits + cum_f[:, :, qs:qe, None] - cum_f[:, :, None, :qe]
        causal = jnp.arange(qs, qe)[:, None] >= jnp.arange(qe)[None, :]
        logits = jnp.where(causal[None, None], logits, NEG_INF)
        p = jax.nn.softmax(logits, axis=-1).astype(v.dtype)
        outs.append(jnp.einsum('bhqk,bhkd->bhqd', p, vb))
    o = jnp.concatenate(outs, axis=2)
    return o.transpose(0, 2, 1, 3).reshape(b, s, h * dh)

def pool_mixer(u, w_pool, pool_scale):
    b, s, _ = u.shape
    uf = u.astype(jnp.float32)
    cs = jnp.cumsum(uf, axis=1)
    groups = []
    for g, w in enumerate(POOL_WINDOWS):
        sl = slice(g * POOL_GROUP_DIM, (g + 1) * POOL_GROUP_DIM)
        cs_g = cs[..., sl]
        lagged = jnp.pad(cs_g, ((0, 0), (w, 0), (0, 0)))[:, :s]
        count = jnp.minimum(jnp.arange(1, s + 1, dtype=jnp.float32), float(w))
        groups.append((cs_g - lagged) / count[None, :, None] - uf[..., sl])
    p = jnp.stack(groups, axis=2).astype(u.dtype)
    y = jnp.einsum('bsgc,gcd->bsgd', p, w_pool).reshape(b, s, POOL_WIDTH)
    return y * pool_scale

def short_conv(h, b_gate, c_gate, conv_w):
    u = c_gate * h
    y = lax.conv_general_dilated(
        u, conv_w[:, None, :].astype(u.dtype), window_strides=(1,), padding=[(CONV_K - 1, 0)],
        dimension_numbers=('NWC', 'WIO', 'NWC'), feature_group_count=CONV_WIDTH)
    return b_gate * y

def hybrid_layer(x, c, w_ada, b_ada, g_mix_pre, g_mix_post, g_ff_pre, g_ff_post, w_in, b_f,
                 w_pool, pool_scale, conv_w, w_branch, w_out, w_ff1, w_ff2):
    b, s, d = x.shape
    mod = jax.nn.silu(c) @ w_ada + b_ada
    shift_m, scale_m, gate_m, shift_f, scale_f, gate_f = jnp.split(mod, 6, axis=-1)

    h = rmsnorm(x, g_mix_pre) * (1.0 + scale_m[:, None]) + shift_m[:, None]
    z = h @ w_in
    sizes = [A_WIDTH, A_WIDTH, A_WIDTH, A_HEADS, POOL_WIDTH, CONV_WIDTH, CONV_WIDTH, CONV_WIDTH]
    cuts = [int(v) for v in np.cumsum(sizes)]
    q, k, v, fl, pu, ch, cb, cc, gl = jnp.split(z, cuts, axis=-1)
    heads = (b, s, A_HEADS, A_HEAD_DIM)
    br_a = forgetting_attention(q.reshape(heads), k.reshape(heads), v.reshape(heads), fl + b_f)
    br_b = pool_mixer(pu, w_pool, pool_scale)
    br_c = short_conv(ch, cb, cc, conv_w)
    gates = jax.nn.sigmoid(gl).reshape(b, s, N_BRANCH, d)
    wa = w_branch[:A_WIDTH]
    wb = w_branch[A_WIDTH:A_WIDTH + POOL_WIDTH]
    wc = w_branch[A_WIDTH + POOL_WIDTH:]
    merged = gates[:, :, 0] * (br_a @ wa) + gates[:, :, 1] * (br_b @ wb) + gates[:, :, 2] * (br_c @ wc)
    y = merged @ w_out
    x = x + gate_m[:, None] * rmsnorm(y, g_mix_post)

    h2 = rmsnorm(x, g_ff_pre) * (1.0 + scale_f[:, None]) + shift_f[:, None]
    y2 = jnp.square(jax.nn.relu(h2 @ w_ff1)) @ w_ff2
    return x + gate_f[:, None] * rmsnorm(y2, g_ff_post)

def first_inputs(seed: int = 0) -> dict:
    key = jax.random.key(seed)
    ks = jax.random.split(key, 20)

    def nrm(k, shape, std):
        return jax.random.normal(k, shape, jnp.float32) * std

    d = D_MODEL
    branch_row_scale = jnp.concatenate([
        jnp.full((A_WIDTH,), A_WIDTH ** -0.5, jnp.float32),
        jnp.full((POOL_WIDTH,), POOL_WIDTH ** -0.5, jnp.float32),
        jnp.full((CONV_WIDTH,), CONV_WIDTH ** -0.5, jnp.float32)])
    return {
        'x': nrm(ks[0], (BATCH, SEQ, d), 1.0),
        'c': nrm(ks[1], (BATCH, d), 1.0),
        'w_ada': nrm(ks[2], (DEPTH, d, 6 * d), 0.5 * d ** -0.5),
        'b_ada': nrm(ks[3], (DEPTH, 6 * d), 0.02),
        'g_mix_pre': 1.0 + nrm(ks[4], (DEPTH, d), 0.05),
        'g_mix_post': 1.0 + nrm(ks[5], (DEPTH, d), 0.05),
        'g_ff_pre': 1.0 + nrm(ks[6], (DEPTH, d), 0.05),
        'g_ff_post': 1.0 + nrm(ks[7], (DEPTH, d), 0.05),
        'w_in': nrm(ks[8], (DEPTH, d, IN_COLS), d ** -0.5),
        'b_f': 3.0 + nrm(ks[9], (DEPTH, A_HEADS), 0.1),
        'w_pool': nrm(ks[10], (DEPTH, POOL_GROUPS, POOL_GROUP_DIM, POOL_GROUP_DIM), POOL_GROUP_DIM ** -0.5),
        'pool_scale': 1.0 + nrm(ks[11], (DEPTH, POOL_WIDTH), 0.1),
        'conv_w': nrm(ks[12], (DEPTH, CONV_K, CONV_WIDTH), CONV_K ** -0.5),
        'w_branch': nrm(ks[13], (DEPTH, MIX_WIDTH, d), 1.0) * branch_row_scale[None, :, None],
        'w_out': nrm(ks[14], (DEPTH, d, d), d ** -0.5),
        'w_ff1': nrm(ks[15], (DEPTH, d, D_FF), d ** -0.5),
        'w_ff2': nrm(ks[16], (DEPTH, D_FF, d), D_FF ** -0.5),
    }

def first_block(x, c, w_ada, b_ada, g_mix_pre, g_mix_post, g_ff_pre, g_ff_post, w_in, b_f,
              w_pool, pool_scale, conv_w, w_branch, w_out, w_ff1, w_ff2):
    for l in range(DEPTH):
        x = hybrid_layer(x, c, w_ada[l], b_ada[l], g_mix_pre[l], g_mix_post[l], g_ff_pre[l], g_ff_post[l],
                         w_in[l], b_f[l], w_pool[l], pool_scale[l], conv_w[l], w_branch[l], w_out[l],
                         w_ff1[l], w_ff2[l])
    return x


DEPTH_2 = 2

QBLOCK = 128
MAX_STREAM_OFFSET = 4096

D_SSD = D_MODEL
SSD_HEADDIM = 64
SSD_HEADS = D_SSD // SSD_HEADDIM
SSD_GROUPS = 4
D_STATE = 128
SSD_CONV = 4
SSD_CHUNK = CHUNK

D_CONV = D_MODEL
CONF_KERNEL = 31

DIFF_HEADS = 8
DIFF_DK = 64
DIFF_DV = 2 * DIFF_DK
D_ATTN = DIFF_HEADS * DIFF_DV
ROT_DIM = DIFF_DK // 4
ROPE_THETA = 500000.0

EPS = 1e-6
LN_EPS = 1e-5

N_EVEN = (DEPTH_2 + 1) // 2
N_ODD = DEPTH_2 // 2

XBC_DIM = D_SSD + 2 * SSD_GROUPS * D_STATE
EVEN_SPLITS = [D_SSD, XBC_DIM, SSD_HEADS, D_CONV, D_CONV, D_CONV]
EVEN_IN = sum(EVEN_SPLITS)
EVEN_MIX = D_SSD + D_CONV
ODD_IN = 4 * D_ATTN


def rmsnorm_2(x, w, eps=EPS):
    xf = x.astype(jnp.float32)
    y = xf * lax.rsqrt(jnp.mean(xf * xf, axis=-1, keepdims=True) + eps)
    return (y * w.astype(jnp.float32)).astype(x.dtype)

def layernorm(x, w, b, eps=LN_EPS):
    xf = x.astype(jnp.float32)
    mu = jnp.mean(xf, axis=-1, keepdims=True)
    var = jnp.mean(jnp.square(xf - mu), axis=-1, keepdims=True)
    y = (xf - mu) * lax.rsqrt(var + eps)
    return (y * w.astype(jnp.float32) + b.astype(jnp.float32)).astype(x.dtype)

def causal_dwconv(x, w, b):
    k = w.shape[0]
    out = lax.conv_general_dilated(
        x, w[:, None, :].astype(x.dtype), window_strides=(1,), padding=[(k - 1, 0)],
        dimension_numbers=("NWC", "WIO", "NWC"), feature_group_count=x.shape[-1])
    return out + b.astype(x.dtype)

def ssd_chunked(x, dt, a, bm, cm, d_skip):
    bsz, s, h, p = x.shape
    g, n = bm.shape[2], bm.shape[3]
    e = h // g
    l = SSD_CHUNK
    nc = s // l
    xd = (x * dt[..., None]).reshape(bsz, nc, l, g, e, p)
    da = (dt * a).reshape(bsz, nc, l, g, e).transpose(0, 3, 4, 1, 2)
    cs = jnp.cumsum(da, axis=-1)
    bm = bm.reshape(bsz, nc, l, g, n)
    cm = cm.reshape(bsz, nc, l, g, n)
    tril = jnp.tril(jnp.ones((l, l), dtype=bool))
    seg = cs[..., :, None] - cs[..., None, :]
    decay = jnp.exp(jnp.where(tril, seg, -jnp.inf))
    cb = jnp.einsum("bclgn,bcsgn->bcgls", cm, bm)
    y_diag = jnp.einsum("bcgls,bgecls,bcsgep->bclgep", cb, decay, xd)
    decay_states = jnp.exp(cs[..., -1:] - cs)
    states = jnp.einsum("bclgn,bgecl,bclgep->bcgepn", bm, decay_states, xd)
    chunk_decay = jnp.exp(cs[..., -1])

    def step(hstate, inp):
        st, dec = inp
        return hstate * dec[..., None, None] + st, hstate

    h0 = jnp.zeros((bsz, g, e, p, n), jnp.float32)
    _, prev = lax.scan(step, h0, (jnp.moveaxis(states, 1, 0), jnp.moveaxis(chunk_decay, -1, 0)))
    prev = jnp.moveaxis(prev, 0, 1)
    y_off = jnp.einsum("bclgn,bcgepn,bgecl->bclgep", cm, prev, jnp.exp(cs))
    y = (y_diag + y_off).reshape(bsz, s, h, p)
    return y + x * d_skip[:, None]

def partial_rotary(t, pos):
    half = ROT_DIM // 2
    inv = ROPE_THETA ** (-2.0 * jnp.arange(half, dtype=jnp.float32) / ROT_DIM)
    ang = pos.astype(jnp.float32)[..., None] * inv
    cos = jnp.cos(ang)[:, :, None, None, :]
    sin = jnp.sin(ang)[:, :, None, None, :]
    tf = t.astype(jnp.float32)
    t1, t2 = tf[..., :half], tf[..., half:ROT_DIM]
    out = jnp.concatenate([t1 * cos - t2 * sin, t2 * cos + t1 * sin, tf[..., ROT_DIM:]], axis=-1)
    return out.astype(t.dtype)

def diff_attention(q, k, v, lam):
    bsz, s, h, _, dk = q.shape
    nb = s // QBLOCK
    qb = q.reshape(bsz, nb, QBLOCK, h, 2, dk).swapaxes(0, 1)
    kf = k.astype(jnp.float32)
    key_chunk = jnp.arange(s) // CHUNK
    scale = dk ** -0.5

    def one_block(args):
        qblk, bi = args
        sc = jnp.einsum("bqhmd,bkhmd->bhmqk", qblk.astype(jnp.float32), kf) * scale
        q_chunk = (bi * QBLOCK + jnp.arange(QBLOCK)) // CHUNK
        allowed = key_chunk[None, :] <= q_chunk[:, None]
        sc = jnp.where(allowed, sc, -jnp.inf)
        pr = jax.nn.softmax(sc, axis=-1)
        wts = pr[:, :, 0] - lam * pr[:, :, 1]
        return jnp.einsum("bhqk,bkhe->bqhe", wts.astype(v.dtype), v)

    o = lax.map(one_block, (qb, jnp.arange(nb)))
    return o.swapaxes(0, 1).reshape(bsz, s, h, v.shape[-1])

def even_layer(x, norm_w, w_in, conv_w, conv_b, dt_bias, a_log, d_skip, ssd_norm_w,
               dw_w, dw_b, ln_w, ln_b, w_out):
    bsz, s, _ = x.shape
    hn = rmsnorm_2(x, norm_w)
    proj = hn @ w_in
    idx = list(np.cumsum(EVEN_SPLITS)[:-1])
    z_a, xbc, dt_raw, glu_v, glu_g, z_b = jnp.split(proj, idx, axis=-1)
    xbc = jax.nn.silu(causal_dwconv(xbc, conv_w, conv_b))
    xs, bs, cs = jnp.split(xbc, [D_SSD, D_SSD + SSD_GROUPS * D_STATE], axis=-1)
    xs = xs.reshape(bsz, s, SSD_HEADS, SSD_HEADDIM).astype(jnp.float32)
    bs = bs.reshape(bsz, s, SSD_GROUPS, D_STATE).astype(jnp.float32)
    cs = cs.reshape(bsz, s, SSD_GROUPS, D_STATE).astype(jnp.float32)
    dt = jax.nn.softplus(dt_raw.astype(jnp.float32) + dt_bias.astype(jnp.float32))
    a = -jnp.exp(a_log.astype(jnp.float32))
    y = ssd_chunked(xs, dt, a, bs, cs, d_skip.astype(jnp.float32)).reshape(bsz, s, D_SSD)
    y = y * jax.nn.silu(z_a.astype(jnp.float32))
    y_a = rmsnorm_2(y.reshape(bsz, s, SSD_GROUPS, D_SSD // SSD_GROUPS),
                  ssd_norm_w.reshape(SSD_GROUPS, D_SSD // SSD_GROUPS)).reshape(bsz, s, D_SSD)
    y_a = y_a.astype(x.dtype)
    u = glu_v * jax.nn.sigmoid(glu_g)
    u = causal_dwconv(u, dw_w, dw_b)
    u = jax.nn.silu(layernorm(u, ln_w, ln_b))
    y_b = (u * jax.nn.silu(z_b)).astype(x.dtype)
    return x + jnp.concatenate([y_a, y_b], axis=-1) @ w_out

def odd_layer(x, positions, layer_idx, norm_w, w_in, q_norm_w, k_norm_w,
              lq1, lk1, lq2, lk2, subln_w, w_out):
    bsz, s, _ = x.shape
    lam_init = 0.8 - 0.6 * math.exp(-0.3 * layer_idx)
    hn = rmsnorm_2(x, norm_w)
    proj = hn @ w_in
    q, k, v, gate = jnp.split(proj, 4, axis=-1)
    q = rmsnorm_2(q.reshape(bsz, s, DIFF_HEADS, 2, DIFF_DK), q_norm_w)
    k = rmsnorm_2(k.reshape(bsz, s, DIFF_HEADS, 2, DIFF_DK), k_norm_w)
    q = partial_rotary(q, positions)
    k = partial_rotary(k, positions)
    v = v.reshape(bsz, s, DIFF_HEADS, DIFF_DV)
    f32 = jnp.float32
    lam = (jnp.exp(jnp.sum(lq1.astype(f32) * lk1.astype(f32)))
           - jnp.exp(jnp.sum(lq2.astype(f32) * lk2.astype(f32))) + lam_init)
    o = diff_attention(q, k, v, lam)
    o = rmsnorm_2(o, subln_w) * (1.0 - lam_init)
    o = o.reshape(bsz, s, D_ATTN) * jax.nn.silu(gate)
    return x + o.astype(x.dtype) @ w_out

def second_inputs(seed: int = 0) -> dict:
    key = jax.random.key(seed)
    ks = iter(jax.random.split(key, 40))

    def nrm(shape, scale):
        return jax.random.normal(next(ks), shape, jnp.float32) * scale

    x = nrm((BATCH, SEQ, D_MODEL), 1.0)
    offset = jax.random.randint(next(ks), (BATCH, 1), 0, MAX_STREAM_OFFSET, dtype=jnp.int32)
    positions = (offset + jnp.arange(SEQ, dtype=jnp.int32)[None, :]).astype(jnp.int32)

    ne, no = N_EVEN, N_ODD
    u = jax.random.uniform(next(ks), (ne, SSD_HEADS), jnp.float32)
    dt0 = jnp.exp(u * (math.log(0.1) - math.log(0.001)) + math.log(0.001))
    a_dt_bias = dt0 + jnp.log(-jnp.expm1(-dt0))
    a_a_log = jnp.log(jax.random.uniform(next(ks), (ne, SSD_HEADS), jnp.float32, 1.0, 16.0))
    return {
        "x": x,
        "positions": positions,
        "a_norm_w": 1.0 + nrm((ne, D_MODEL), 0.05),
        "a_w_in": nrm((ne, D_MODEL, EVEN_IN), D_MODEL ** -0.5),
        "a_conv_w": nrm((ne, SSD_CONV, XBC_DIM), SSD_CONV ** -0.5),
        "a_conv_b": nrm((ne, XBC_DIM), 0.02),
        "a_dt_bias": a_dt_bias,
        "a_a_log": a_a_log,
        "a_d_skip": 1.0 + nrm((ne, SSD_HEADS), 0.05),
        "a_ssd_norm_w": 1.0 + nrm((ne, D_SSD), 0.05),
        "a_dw_w": nrm((ne, CONF_KERNEL, D_CONV), CONF_KERNEL ** -0.5),
        "a_dw_b": nrm((ne, D_CONV), 0.02),
        "a_ln_w": 1.0 + nrm((ne, D_CONV), 0.05),
        "a_ln_b": nrm((ne, D_CONV), 0.02),
        "a_w_out": nrm((ne, EVEN_MIX, D_MODEL), EVEN_MIX ** -0.5),
        "c_norm_w": 1.0 + nrm((no, D_MODEL), 0.05),
        "c_w_in": nrm((no, D_MODEL, ODD_IN), D_MODEL ** -0.5),
        "c_q_norm_w": 1.0 + nrm((no, DIFF_DK), 0.05),
        "c_k_norm_w": 1.0 + nrm((no, DIFF_DK), 0.05),
        "c_lq1": nrm((no, DIFF_DK), 0.1),
        "c_lk1": nrm((no, DIFF_DK), 0.1),
        "c_lq2": nrm((no, DIFF_DK), 0.1),
        "c_lk2": nrm((no, DIFF_DK), 0.1),
        "c_subln_w": 1.0 + nrm((no, DIFF_DV), 0.05),
        "c_w_out": nrm((no, D_ATTN, D_MODEL), D_ATTN ** -0.5),
    }

def second_block(x, positions, a_norm_w, a_w_in, a_conv_w, a_conv_b, a_dt_bias, a_a_log,
              a_d_skip, a_ssd_norm_w, a_dw_w, a_dw_b, a_ln_w, a_ln_b, a_w_out,
              c_norm_w, c_w_in, c_q_norm_w, c_k_norm_w, c_lq1, c_lk1, c_lq2, c_lk2,
              c_subln_w, c_w_out):
    for i in range(DEPTH_2):
        if i % 2 == 0:
            j = i // 2
            x = even_layer(x, a_norm_w[j], a_w_in[j], a_conv_w[j], a_conv_b[j], a_dt_bias[j],
                           a_a_log[j], a_d_skip[j], a_ssd_norm_w[j], a_dw_w[j], a_dw_b[j],
                           a_ln_w[j], a_ln_b[j], a_w_out[j])
        else:
            j = i // 2
            x = odd_layer(x, positions, i, c_norm_w[j], c_w_in[j], c_q_norm_w[j], c_k_norm_w[j],
                          c_lq1[j], c_lk1[j], c_lq2[j], c_lk2[j], c_subln_w[j], c_w_out[j])
    return x


def setup_inputs(seed=0):
    out = dict(first_inputs(seed))
    for name, value in second_inputs(seed + 1).items():
        if name != "x":
            out[name + "_2"] = value
    return out


def reference(
    x, c, w_ada, b_ada, g_mix_pre, g_mix_post, g_ff_pre, g_ff_post, w_in, b_f, w_pool,
    pool_scale, conv_w, w_branch, w_out, w_ff1, w_ff2, positions_2, a_norm_w_2, a_w_in_2,
    a_conv_w_2, a_conv_b_2, a_dt_bias_2, a_a_log_2, a_d_skip_2, a_ssd_norm_w_2, a_dw_w_2,
    a_dw_b_2, a_ln_w_2, a_ln_b_2, a_w_out_2, c_norm_w_2, c_w_in_2, c_q_norm_w_2, c_k_norm_w_2,
    c_lq1_2, c_lk1_2, c_lq2_2, c_lk2_2, c_subln_w_2, c_w_out_2,
):
    x = first_block(
        x, c, w_ada, b_ada, g_mix_pre, g_mix_post, g_ff_pre, g_ff_post, w_in, b_f, w_pool,
        pool_scale, conv_w, w_branch, w_out, w_ff1, w_ff2,
    )
    return second_block(
        x, positions_2, a_norm_w_2, a_w_in_2, a_conv_w_2, a_conv_b_2, a_dt_bias_2, a_a_log_2,
        a_d_skip_2, a_ssd_norm_w_2, a_dw_w_2, a_dw_b_2, a_ln_w_2, a_ln_b_2, a_w_out_2,
        c_norm_w_2, c_w_in_2, c_q_norm_w_2, c_k_norm_w_2, c_lq1_2, c_lk1_2, c_lq2_2, c_lk2_2,
        c_subln_w_2, c_w_out_2,
    )


_drawn_inputs = setup_inputs


def setup_inputs(seed=0):
    import zlib

    import numpy as np

    out = dict(_drawn_inputs(seed))
    spreads = {}
    factors = {'g_mix_post': 2.772,
     'g_ff_pre': 2.807,
     'g_ff_post': 2.988,
     'b_f': 64.0,
     'pool_scale': 2.783,
     'a_conv_b_2': 3.073,
     'a_d_skip_2': 3.163,
     'a_dw_b_2': 5.842,
     'a_ln_w_2': 4.495,
     'a_ln_b_2': 8.0,
     'c_q_norm_w_2': 5.778,
     'c_k_norm_w_2': 5.145,
     'c_lq1_2': 4.558,
     'c_lk1_2': 8.0,
     'c_lk2_2': 8.0,
     'c_subln_w_2': 4.233}
    for name, (base, spread) in spreads.items():
        noise = np.random.default_rng([zlib.crc32(name.encode()), seed]).standard_normal(out[name].shape)
        drawn = base * np.exp(spread * noise) if base else spread * noise
        out[name] = __import__('jax').numpy.asarray(drawn.astype(out[name].dtype))
    for name, factor in factors.items():
        out[name] = (out[name] * factor).astype(out[name].dtype)
    return out
```

```python
from contextlib import ExitStack

import concourse.bass as bass
import numpy as np
from concourse import mybir

ALU = mybir.AluOpType
ACT = mybir.ActivationFunctionType
F32 = mybir.dt.float32
F32R = mybir.dt.float32r
I32 = mybir.dt.int32
AX_X = mybir.AxisListType.X

P = 128
S = 512
D = 1024
KT = D // P
NB = S // P
CONSTS = 5
SMALL_DMAS = 8
PARAM_DMAS = 18
PCOL = 256
EPS = 1e-6
LN_EPS = 1e-5
NEG = -1e30
HEADS = 8
DH = 64
WINDOWS = (2, 4, 8, 16)
SSD_HEADS = 16
SSD_GROUPS = 4
SSD_TAPS = 4
DW_TAPS = 31
ROT_HALF = 8
GLU_W = S + DW_TAPS - 1
ROPE_THETA = 500000.0
LAM_INIT = 0.8 - 0.6 * float(np.exp(-0.3))
CHUNK = 64
TWO_PI = 2.0 * np.pi
TWO_PI_PARTS = (6.28125, 0.0019350051879882812, float(TWO_PI - 6.28125 - 0.0019350051879882812))
ROUNDER = 1.5 * 2.0 ** 23
SIN_MAX = 3.1415925

Q_OFF = {3: 0, 2: 512, 0: 896, 1: 1024}
K_OFF = {0: 0, 1: 512, 3: 896, 2: 1024}
PACKED = 1280

PAR = {}
PAR_ROWS = [
    ("c", 8), ("b_ada", 48), ("g_mix_pre", 8), ("g_mix_post", 8), ("g_ff_pre", 8), ("g_ff_post", 8),
    ("pool_scale", 2), ("conv_w", 6), ("a_norm_w_2", 8), ("a_ln_w_2", 8), ("a_ln_b_2", 8), ("a_ssd_norm_w_2", 8),
    ("a_conv_w_2", 64), ("a_conv_b_2", 16), ("a_dw_b_2", 8), ("c_norm_w_2", 8), ("pad", 32),
    ("a_dw_w_2", 248),
]
at_row = 0
for row_name, row_count in PAR_ROWS:
    PAR[row_name] = at_row
    at_row += row_count
PAR_GROUPS = [(0, 128), (128, 96), (256, 128), (384, 120)]

SEGMENTS = [("fl", 1), ("mix", 4), ("qk", 4), ("v", 2), ("gates", 16), ("wout", 4), ("ff", 32),
            ("dt", 1), ("glu", 8), ("xbc", 8), ("z", 8), ("out_a", 4), ("out_b", 4),
            ("dqk", 8), ("dv", 4), ("dgate", 4), ("dout", 4)]
PANEL = {}
panels_so_far = 0
for seg_name, seg_count in SEGMENTS:
    PANEL[seg_name] = panels_so_far
    panels_so_far += seg_count
N_PANELS = panels_so_far

FILLS = [("par", 1), ("x", 16), ("fl", 1), ("mix", 8), ("qk", 8), ("v", 4), ("pool", 2),
         ("attn", 40), ("gates", 32), ("wout", 8), ("ff", 64),
         ("dt", 1), ("glu", 16), ("xbc", 16), ("dtt", 2), ("btok", 3), ("xtok", 8), ("ssd", 48),
         ("out_a", 8), ("out_b", 8), ("dqk", 16), ("dv", 8),
         ("dattn", 64), ("dout", 8)]
FILL = {}
fills_so_far = 0
for fill_name, fill_count in FILLS:
    FILL[fill_name] = fills_so_far
    fills_so_far += fill_count

SPLITS = [("h1", 8), ("conv", 2), ("pool", 2), ("attn", 8), ("merged", 8), ("h_ff", 8), ("hidden", 32),
          ("h2", 8), ("ya", 8), ("yb", 8), ("h3", 8), ("o", 8)]
SPLIT = {}
splits_so_far = 0
for split_name, split_count in SPLITS:
    SPLIT[split_name] = splits_so_far
    splits_so_far += split_count

NOT_BY_DVE = ("pool", "attn", "merged", "hidden")


def dve_source(q):
    return sum(min(max(q + 1 - SPLIT[name], 0), n) for name, n in SPLITS if name not in NOT_BY_DVE)


NORM = {"mix_post": 0, "ff_pre": 1, "ff_post": 2, "a_norm": 3, "c_norm": 6}
SQ = {"ya": 32, "ln": 40}
RMS = {"ya": 4, "ln": 8, "c_norm": 9}


def attn_bc(h):
    return FILL["attn"] + (0 if h == 0 else 1 + 5 * (h - 1))


def attn_pt(h, j):
    return FILL["attn"] + 1 + 5 * h + (1 if h < HEADS - 1 else 0) + j


def attn_o(h):
    return attn_pt(h, 3)



def ssd_cum(h):
    return FILL["ssd"] + max(3 * h - 2, 0)


def ssd_y(h):
    return FILL["ssd"] + min(2 + 3 * h, 45)


def ssd_z(h):
    return FILL["ssd"] + (3 + 3 * h if h < 14 else 32 + h)


def diff_t(h, j):
    return FILL["dattn"] + (0 if h == 0 else 2 + 8 * (h - 1)) + j


def diff_wt(h, j):
    return FILL["dattn"] + 2 + 8 * h + (2 if h < HEADS - 1 else 0) + j


def diff_o(h):
    return diff_wt(h, 3)


def diff_gate(h):
    return diff_wt(h, 4)


def diff_sum(h):
    return diff_wt(h, 5)


class Tally:

    def __init__(self, sem):
        self.sem, self.n = sem, 0

    def mark(self, instruction):
        instruction.then_inc(self.sem, 1)
        self.n = self.n + 1

    def last(self, engine):
        engine.wait_ge(self.sem, self.n)

    def enter(self, turn, per_turn):
        self.before, self.per_turn = self.n, per_turn
        self.n = turn * per_turn + self.before

    def leave(self, turns):
        self.n = self.before + turns * self.per_turn


def hybrid_program(nc, t, out):
    ctx = ExitStack()
    with ctx:
        def sb(name, shape, dtype=F32):
            return ctx.enter_context(nc.sbuf_tensor(name, shape, dtype))

        def sem(name):
            return ctx.enter_context(nc.semaphore(name))

        def row(ap):
            return ap.rearrange("a n -> (a n)").unsqueeze(0) if len(ap.shape) == 2 else ap.unsqueeze(0)

        raw = [sb(f"raw{i}", [P, KT * PCOL]) for i in range(2)]
        w_hi = [sb(f"w_hi{i}", [P, KT * PCOL], F32R) for i in range(2)]
        w_lo = [sb(f"w_lo{i}", [P, KT * PCOL], F32R) for i in range(2)]
        h_hi = sb("h_hi", [P, KT * S], F32R)
        h_lo = sb("h_lo", [P, KT * S], F32R)
        b_offset = nc.sbuf_base
        b_hi = sb("b_hi", [P, KT * S], F32R)
        b_lo = sb("b_lo", [P, KT * S], F32R)
        b_mem = nc.alloc_sbuf_tensor_at("b_mem", [P, 2 * KT * S], F32, offset=b_offset)
        x = sb("resid", [P, KT * S])
        par = sb("par", [P, 512])
        ident = sb("ident", [P, P])
        ones = sb("ones", [P, P])
        causal_qk = sb("causal_qk", [P, P])
        causal_kq = sb("causal_kq", [P, P])
        tmp = [sb(f"tmp{i}", [P, S]) for i in range(2)]
        sq = [sb(f"sq{i}", [P, S]) for i in range(2)]
        rb = sb("rb", [P, S])
        small = sb("small", [P, 672])
        arena = sb("arena", [P, 18176])

        small_at = [0]

        def little(n):
            small_at[0] += n
            assert small_at[0] <= 672
            return small[:, small_at[0] - n:small_at[0]]

        def place(at, n):
            assert at + n <= 18176, (at, n)
            return arena[:, at:at + n]

        silu_c, mod = little(8), little(48)
        a_mix, g_mix, a_ff, g_ff = little(8), little(8), little(8), little(8)
        ss_x, r_x = little(4), little(4)
        lmax, lneg, lsum, linv = little(4 * HEADS), little(4 * HEADS), little(4 * HEADS), little(4 * HEADS)
        bias_f = little(1)
        eps_t = little(2)
        win_n, win_inv = little(32), little(32)
        win_i = little(16).bitcast(I32)

        xbc = place(0, 16 * S)
        glu = place(8192, KT * GLU_W)
        z_b = place(12528, 4096)
        z_a = [place(16624, 512), place(17136, 512)]
        cum = place(17648, 512)
        taps = [tmp[0][:], tmp[1][:]]
        padded = [b_mem[:, 0:515], b_mem[:, 520:1035]]
        dt_tmp = [b_mem[:, 1040 + 512 * i:1552 + 512 * i] for i in range(5)]
        xd = b_mem[:, 0:4096]
        b_tok = b_mem[:, 4096:5632]
        xdu = b_mem[:, 5632:6400]
        state = b_mem[:, 6400:7168]
        c_scaled = b_mem[:, 7168:7680]
        masked = tmp[0][:]
        csb = tmp[1][:]
        decay = sq
        from_start = [rb[:], b_mem[:, 7680:8192]]
        y_rms = [place(4096 + 512 * g, 512) for g in range(SSD_GROUPS)]
        out_a = place(0, 4096)
        dw_acc = [sq[0][:], sq[1][:]]
        dw_acc_late = place(8 * S, S)
        dt_bias, a_log, a_rate = little(1), little(1), little(1)
        d_all, d_skip = little(16), little(8)
        dt_tok, ncum_tok, to_end, end_decay = little(64), little(64), little(64), little(64)

        qkv = place(0, 12 * 1024)
        qk_sq = place(12288, 1024)
        qk_w = place(13312, 128)
        lam_in = place(13440, 256)
        position = place(13696, 4)
        pos_f, turns, angle = place(13700, 4), place(13704, 32), place(13736, 32)
        cosines, sines, qk_ms = place(13768, 32), place(13800, 32), place(13832, 16)
        rot = [place(13848 + 128 * j, 128) for j in range(4)]
        lam_prod = place(14360, 128)
        d_gate = [place(12288, 512), place(12800, 512)]
        weights = [place(13312, PACKED), place(14592, PACKED)]
        probs_1 = place(15872, PACKED)
        weights_tr = [place(17152, 512), place(17664, 512), par[:, 0:256]]
        half_q, half_k = par[0:1, 256:384], par[0:1, 384:512]
        q_t, k_t = sq
        final = place(0, 8 * S)
        lam_e, neg_lam, sub_w = little(2), little(1), little(1)

        def glu_tile(k):
            return glu[:, k * GLU_W + DW_TAPS - 1:(k + 1) * GLU_W]

        psum = ctx.enter_context(nc.psum_tensor("psum", [P, 8 * 512], F32))

        def bank(b, n=512, at=0):
            return psum[:, b * 512 + at:b * 512 + at + n]

        landed = [sem("landed0"), sem("landed1")]
        hi_done = sem("hi_done")
        lo_done = sem("lo_done")
        fill_done = sem("fill_done")
        ring_free = [sem("ring_free0"), sem("ring_free1")]
        split_hi = sem("split_hi")
        split_lo = sem("split_lo")
        split_src = sem("split_src")
        param_rows = sem("param_rows")
        small_landed = sem("small_landed")
        consts_done = sem("consts_done")
        pool_step = sem("pool_step")
        x_landed = sem("x_landed")
        ada_landed = [sem(f"ada_landed{i}") for i in range(3)]
        ada_acc_done = sem("ada_acc_done")
        act_step = sem("act_step")
        dve_step = sem("dve_step")
        par_done = sem("par_done")
        x_sumsq = sem("x_sumsq")
        x_rms = sem("x_rms")
        x_diag = sem("x_diag")
        silu_t = sem("silu_t")
        mod_a = sem("mod_a")
        f_logit = sem("f_logit")
        f_exp_in = sem("f_exp_in")
        f_exp = sem("f_exp")
        f_ln = sem("f_ln")
        cum_done = sem("cum_done")
        scores_done = sem("scores_done")
        scores_read = sem("scores_read")
        cum_row = sem("cum_row")
        neg_max = sem("neg_max")
        exp_done = sem("exp_done")
        probs_done = sem("probs_done")
        probs_t = sem("probs_t")
        branch_done = sem("branch_done")
        branch_read = sem("branch_read")
        pooled = sem("pooled")
        sq_done = sem("sq_done")
        sq_read = sem("sq_read")
        rms_done = sem("rms_done")
        rinv_done = sem("rinv_done")
        x_ready = sem("x_ready")
        eps_done = sem("eps_done")
        silu_c_done = sem("silu_c_done")
        mod_rows = sem("mod_rows")
        mod_columns = sem("mod_columns")
        out_landed = sem("out_landed")
        rate_exp = sem("rate_exp")
        cum_chunks = sem("cum_chunks")
        taps_done = sem("taps_done")
        xbc_done = sem("xbc_done")
        ends_done = sem("ends_done")
        ends_exp = sem("ends_exp")
        xdu_done = sem("xdu_done")
        states_summed = sem("states_summed")
        states_done = sem("states_done")
        cb_done = sem("cb_done")
        decay_in = sem("decay_in")
        decay_done = sem("decay_done")
        from_start_done = sem("from_start_done")
        masked_scores = sem("masked_scores")
        gated_y = sem("gated_y")
        dw_in_done = sem("dw_in_done")
        dw_done = sem("dw_done")
        ln_summed = sem("ln_summed")
        ln_mean = sem("ln_mean")
        centred = sem("centred")
        ln_scaled = sem("ln_scaled")
        ln_silu = sem("ln_silu")

        diff_landed = sem("diff_landed")
        halves_done = sem("halves_done")
        angle_in = sem("angle_in")
        lam_in_done = sem("lam_in_done")
        sin_done = sem("sin_done")
        lam_exp = sem("lam_exp")
        qk_squared = sem("qk_squared")
        qk_rms = sem("qk_rms")
        qk_prepared = sem("qk_prepared")
        diff_scores = sem("diff_scores")
        diff_neg_max = sem("diff_neg_max")
        diff_exp = sem("diff_exp")
        diff_weights = sem("diff_weights")
        o_squared = sem("o_squared")
        o_rms = sem("o_rms")
        o_rinv = sem("o_rinv")
        o_normed = sem("o_normed")

        hi = h_hi, b_hi
        lo = h_lo, b_lo

        def tile_of(buffer, k):
            return buffer[:, k * S:(k + 1) * S]

        x_tok, xn = place(4096, 4096), place(8192, 4096)
        x_junk, diag = place(12288, 1024), place(13312, 512)
        ada = [place(0, 2048), place(2048, 2048), raw[1][:]]
        w_pool = place(15616, 256)
        ada_acc = [place(15936, 256), place(16192, 256)]
        par_rows = place(13824, 512)
        mod_row = [rb[:], sq[0][:], sq[1][:], tmp[1][:]]
        u = place(0, 4096)
        qk, v = place(4096, 4096), place(8192, 2048)
        scores = [place(10240, PACKED), place(11520, PACKED)]
        probs_tr = place(12800, PACKED)
        cum_bc, cum_bcm = place(14080, 512), place(14592, 512)
        flog = [place(15104, 512), place(10240, 512), place(10752, 512), place(11264, 512), place(11776, 512)]
        pool_sum = [sq[0][:], sq[1][:]]
        gate = place(4096, 3072)
        merged, gate_tmp = place(7168, 4096), place(11264, 512)
        y = place(0, 4096)
        relu = [place(4096, 512), place(4608, 512)]
        relu_sq = [place(5120, 512), place(5632, 512)]

        def wait_fill(engine, f, d=0):
            engine.wait_ge(fill_done, f + 1 + 2 * d)

        def wait_ring_free(pe, f, d=0):
            if isinstance(d, int) and f // 2 + d == 0:
                return
            pe.wait_ge(ring_free[f % 2], f // 2 + d)

        def wait_ring_read(engine, f, d=0):
            engine.wait_ge(ring_free[f % 2], f // 2 + 1 + d)

        def split_weights_hi(act, n, filled, slot, landings):
            act.wait_ge(landed[slot], landings)
            if filled is not None:
                act.wait_ge(fill_done, filled)
            nc.scalar.activation(w_hi[slot][:], raw[slot][:], ACT.Copy).then_inc(hi_done, 1)

        def panel_hi(act, n, d, filled):
            split_weights_hi(act, n, filled, n % 2, 16 * (n // 2 + 1) + 16 * d)

        def wait_panel(pe, n, d=0):
            pe.wait_ge(lo_done, n + 1 + 2 * d)

        def product(out_ap, slot, c, src, k_range, need=None, n_done=None, start=True, stop=True):
            ks = list(k_range)
            a_hi, a_lo = hi[src], lo[src]
            last = None
            for k in ks:
                if need is not None:
                    nc.tensor.wait_ge(split_lo, need + k + 1)
                wh = w_hi[slot][:, k * PCOL + c * P:k * PCOL + (c + 1) * P]
                wl = w_lo[slot][:, k * PCOL + c * P:k * PCOL + (c + 1) * P]
                nc.tensor.matmul(out_ap, wh, tile_of(a_hi, k), start=start and k == ks[0], stop=False)
                nc.tensor.matmul(out_ap, wh, tile_of(a_lo, k), start=False, stop=False)
                last = nc.tensor.matmul(out_ap, wl, tile_of(a_hi, k), start=False, stop=stop and k == ks[-1])
            return last

        def linear(pe, seg, src, split, count=None, fill=None):
            n0, f0 = PANEL[seg], FILL[fill or seg]
            with pe.Fori(0, (count or dict(SEGMENTS)[seg]) // 2) as i:
                for s in range(2):
                    wait_panel(pe, n0 + s, i)
                    for c in range(2):
                        f = f0 + 2 * s + c
                        wait_ring_free(pe, f, 2 * i)
                        product(bank(f % 2), (n0 + s) % 2, c, src, range(KT),
                                need=split if s == 0 and c == 0 else None).then_inc(fill_done, 1)

        def panel_load(sp, n, d, source):
            sp.dma_start(raw[n % 2][:].rearrange("p (t n) -> p t n", t=KT), source)\
              .then_inc(landed[n % 2], 16)

        def wait_slot(sp, n, d=0):
            if isinstance(d, int) and n + 2 * d < 2:
                return
            sp.wait_ge(lo_done, n - 1 + 2 * d)

        def load_segment(sp, seg, weight, col0, count=None, first=0):
            w = weight.rearrange("(t p) n -> p t n", p=P)
            n0 = PANEL[seg] + first
            count = count or dict(SEGMENTS)[seg]
            if count == 1:
                wait_slot(sp, n0)
                panel_load(sp, n0, 0, w[:, :, col0:col0 + PCOL])
                return
            for s in range(2):
                wait_slot(sp, n0 + s)
                panel_load(sp, n0 + s, 0, w[:, :, col0 + s * PCOL:col0 + (s + 1) * PCOL])
            if count > 2:
                with sp.Fori(1, count // 2) as i:
                    for s in range(2):
                        wait_slot(sp, n0 + s, i)
                        panel_load(sp, n0 + s, i, w[:, :, bass.ds(i * 2 * PCOL + (col0 + s * PCOL), PCOL)])

        w_ada = t["w_ada"][0].rearrange("(t p) n -> p t n", p=P)

        def ada_load(sp, slot, col):
            sp.dma_start(ada[slot].rearrange("p (t n) -> p t n", t=KT), w_ada[:, :, col])\
              .then_inc(ada_landed[slot], 16)

        block = ctx.enter_context(nc.Block())

        @block.sync
        def _(sp):
            sp.dma_start(x_tok.rearrange("p (b d) -> p b d", b=NB),
                         t["x"][0].rearrange("(b p) d -> p b d", p=P)).then_inc(x_landed, 16)
            for a in range(8):
                if a >= 3:
                    sp.wait_ge(ada_acc_done, a - 2)
                ada_load(sp, a % 3, slice(a * PCOL, (a + 1) * PCOL))
                if a == 3:
                    load_segment(sp, "fl", t["w_in"][0], 1536)
            sp.wait_ge(ada_acc_done, 6)
            load_segment(sp, "mix", t["w_in"][0], 1544)
            load_segment(sp, "qk", t["w_in"][0], 0)
            load_segment(sp, "v", t["w_in"][0], 1024)

            w_in = t["w_in"][0].rearrange("(t p) n -> p t n", p=P)
            w_branch = t["w_branch"][0].rearrange("(t p) n -> p t n", p=P)
            n0 = PANEL["gates"]
            with sp.Fori(1, 5) as i:
                for s in range(4):
                    sp.wait_ge(lo_done, n0 + s - 5 + 4 * i)
                    if s < 3:
                        panel_load(sp, n0 + s, 0, w_in[:, :, bass.ds(i * PCOL + (2568 - PCOL + s * D), PCOL)])
                    else:
                        panel_load(sp, n0 + s, 0, w_branch[:, :, bass.ds(i * PCOL - PCOL, PCOL)])
                    if s == 1:
                        sp.wait_ge(split_lo, SPLIT["attn"])
                        for a in range(2):
                            sp.wait_ge(ada_acc_done, 3 + a + 4 * i)
                            ada_load(sp, a % 2, bass.ds(i * 4 * PCOL + (4 + a) * PCOL, PCOL))
                for a in range(2, 4):
                    sp.wait_ge(ada_acc_done, 3 + a + 4 * i)
                    ada_load(sp, a % 2, bass.ds(i * 4 * PCOL + (4 + a) * PCOL, PCOL))
            load_segment(sp, "wout", t["w_out"][0], 0)

            w1 = t["w_ff1"][0].rearrange("(t p) n -> p t n", p=P)
            w2 = t["w_ff2"][0].rearrange("(q t p) n -> p (q t) n", p=P, t=KT)
            n0 = PANEL["ff"]
            with sp.Fori(0, 4) as q:
                for s in range(4):
                    sp.wait_ge(lo_done, n0 + s - 1 + 8 * q)
                    panel_load(sp, n0 + s, 4 * q, w1[:, :, bass.ds(q * D + s * PCOL, PCOL)])
                for s in range(4, 8):
                    sp.wait_ge(lo_done, n0 + s - 1 + 8 * q)
                    panel_load(sp, n0 + s, 4 * q, w2[:, bass.ds(q * KT, KT), (s - 4) * PCOL:(s - 3) * PCOL])
            w2in = t["a_w_in_2"][0]
            load_segment(sp, "dt", w2in, 3072)
            w2v = w2in.rearrange("(t p) n -> p t n", p=P)
            n0 = PANEL["glu"]
            with sp.Fori(0, 4) as i:
                for s in range(2):
                    sp.wait_ge(lo_done, n0 + s - 1 + 2 * i)
                    panel_load(sp, n0 + s, i, w2v[:, :, bass.ds(i * PCOL + (3088 + s * D), PCOL)])
            load_segment(sp, "xbc", w2in, 1024)
            n0 = PANEL["z"]
            with sp.Fori(0, 4) as i:
                for s, col in enumerate((0, 5136)):
                    sp.wait_ge(lo_done, n0 + s - 1 + 2 * i)
                    panel_load(sp, n0 + s, i, w2v[:, :, bass.ds(i * PCOL + col, PCOL)])
            load_segment(sp, "out_a", t["a_w_out_2"][0][0:D], 0)
            load_segment(sp, "out_b", t["a_w_out_2"][0][D:2 * D], 0)
            w_c = t["c_w_in_2"][0]
            w_cv = w_c.rearrange("(t p) n -> p t n", p=P)
            n0 = PANEL["dqk"]
            with sp.Fori(0, 4) as i:
                for s in range(2):
                    sp.wait_ge(lo_done, n0 + s - 1 + 2 * i)
                    panel_load(sp, n0 + s, i, w_cv[:, :, bass.ds(i * PCOL + s * D, PCOL)])
            load_segment(sp, "dv", w_c, 2 * D)
            load_segment(sp, "dgate", w_c, 3 * D)
            load_segment(sp, "dout", t["c_w_out_2"][0], 0)
            out_v = out[0].rearrange("(b p) d -> p b d", p=P)
            for j in range(8):
                s, g = j // 2, j % 2
                wait_ring_read(sp, FILL["dout"] + j)
                sp.dma_start(out_v[:, 2 * g:2 * g + 2, s * PCOL:(s + 1) * PCOL],
                             tile_of(final, j).rearrange("p (b n) -> p b n", b=2)).then_inc(out_landed, 16)
            sp.wait_ge(out_landed, 16 * 8)

        @block.gpsimd
        def _(pool):
            step = Tally(pool_step)
            step.mark(nc.gpsimd.memset(ones[:], 1.0))
            step.mark(nc.gpsimd.memset(ident[:], 0.0))
            step.mark(nc.gpsimd.memset(causal_qk[:], 0.0))
            step.mark(nc.gpsimd.memset(causal_kq[:], 0.0))
            step.last(pool)
            nc.gpsimd.affine_select(out=ident[:], in_=ident[:], compare_op=ALU.not_equal, fill=1.0, base=0,
                                    pattern=[[-1, P]], channel_multiplier=1).then_inc(consts_done, 1)
            nc.gpsimd.affine_select(out=causal_qk[:], in_=causal_qk[:], compare_op=ALU.is_ge, fill=NEG * 8, base=0,
                                    pattern=[[-1, P]], channel_multiplier=1).then_inc(consts_done, 1)
            nc.gpsimd.affine_select(out=causal_kq[:], in_=causal_kq[:], compare_op=ALU.is_ge, fill=NEG, base=0,
                                    pattern=[[1, P]], channel_multiplier=-1).then_inc(consts_done, 1)
            nc.gpsimd.memset(w_pool, 0.0).then_inc(consts_done, 1)
            nc.gpsimd.iota(win_i, pattern=[[1, 16]], base=1, channel_multiplier=0).then_inc(consts_done, 1)

            def panel_lo(n, d):
                pool.wait_ge(hi_done, n + 1 + 2 * d)
                nc.gpsimd.tensor_tensor(w_lo[n % 2][:], raw[n % 2][:], w_hi[n % 2][:].bitcast(F32), ALU.subtract)\
                  .then_inc(lo_done, 1)

            with pool.Fori(0, N_PANELS // 2) as i:
                for s in range(2):
                    panel_lo(s, i)

        @block.scalar
        def _(act):
            step = Tally(act_step)

            def rows_of(name):
                ap = t[name]
                flat = ap.rearrange("a n -> (a n)") if len(ap.shape) == 2 else ap.rearrange("a k n -> (a k n)")
                return flat.rearrange("(r p) -> r p", p=P)

            n_rows = [0]

            def load_rows(name, at, r0, r1):
                g, r = at // P, at % P
                act.dma_start(par_rows[r:r + r1 - r0, g * P:(g + 1) * P], rows_of(name)[r0:r1]).then_inc(param_rows, 16)
                n_rows[0] += 16

            for name, count in PAR_ROWS:
                if name == "pad":
                    continue
                if name == "a_dw_w_2":
                    load_rows(name, 256, 0, 128)
                    load_rows(name, 384, 128, 248)
                    continue
                at, done = PAR[name], 0
                while done < count:
                    k = min(count - done, P - (at + done) % P)
                    load_rows(name, at + done, done, done + k)
                    done += k
            assert n_rows[0] == PARAM_DMAS * 16
            with nc.allow_non_contiguous_dma(reason="eight biases"):
                act.dma_start(bias_f[0:HEADS, :], t["b_f"].rearrange("a n -> n a")).then_inc(small_landed, 16)
            act.wait_ge(consts_done, CONSTS)
            for g in range(len(WINDOWS)):
                r = slice(DH * (g % 2), DH * (g % 2) + DH)
                act.dma_start(w_pool[r, (g // 2) * P + DH * (g % 2):(g // 2) * P + DH * (g % 2) + DH],
                              t["w_pool"][0][g]).then_inc(small_landed, 16)
            with nc.allow_non_contiguous_dma(reason="sixteen biases and rates"):
                act.dma_start(dt_bias[0:SSD_HEADS, :], t["a_dt_bias_2"].rearrange("a n -> n a")).then_inc(small_landed, 16)
                act.dma_start(a_log[0:SSD_HEADS, :], t["a_a_log_2"].rearrange("a n -> n a")).then_inc(small_landed, 16)
            act.dma_start(d_all, t["a_d_skip_2"].to_broadcast([P, SSD_HEADS])).then_inc(small_landed, 16)

            act.wait_ge(fill_done, FILL["par"] + 1)
            for at, n in PAR_GROUPS:
                ins = nc.scalar.activation(par[:, at:at + n], bank(0, n, at), ACT.Copy)
                if at == PAR_GROUPS[-1][0]:
                    ins.then_inc(ring_free[0], 1)
            wait_ring_read(act, FILL["par"])
            nc.scalar.activation(silu_c, par[:, 0:8], ACT.Tanh, scale=0.5).then_inc(silu_t, 1)
            act.wait_ge(eps_done, 1)
            act.wait_ge(x_landed, 16)
            for b in range(NB):
                nc.scalar.activation(x_junk, x_tok[:, b * D:(b + 1) * D], ACT.Square,
                                     accum_out=ss_x[:, b:b + 1]).then_inc(x_sumsq, 1)
                act.wait_ge(x_sumsq, b + 1)
            nc.scalar.activation(r_x, ss_x, ACT.Sqrt, bias=eps_t[:, 0:1], scale=1.0 / D).then_inc(x_rms, 1)
            for k in range(KT):
                f = FILL["x"] + 2 * k
                wait_fill(act, f)
                nc.scalar.activation(tile_of(x, k), bank(f % 2), ACT.Copy).then_inc(ring_free[f % 2], 1)
            act.wait_ge(ada_acc_done, 8)
            for j in range(4):
                nc.scalar.activation(mod_row[j][0:1], bank(2 + j)[0:1], ACT.Copy).then_inc(mod_rows, 1)
            panel_hi(act, 0, 0, None)

            def hi_of_tmp(q, dest, k, scale=1.0, bias=None):
                act.wait_ge(split_src, dve_source(q))
                if bias is None:
                    nc.scalar.activation(tile_of(dest, k), tmp[q % 2][:], ACT.Copy).then_inc(split_hi, 1)
                else:
                    nc.scalar.activation(tile_of(dest, k), tmp[q % 2][:], ACT.Identity, bias=bias).then_inc(split_hi, 1)

            for k in range(KT):
                hi_of_tmp(SPLIT["h1"] + k, h_hi, k)

            def evacuate(seg, emit, count=None, fill=None, first=None):
                n0, f0 = PANEL[seg], FILL[fill or seg]
                with act.Fori(0, (count or dict(SEGMENTS)[seg]) // 2) as i:
                    for s in range(2):
                        panel_hi(act, n0 + s + 1, i, f0 + 2 * s + 4 * i)
                        for c in range(2):
                            f = f0 + 2 * s + c
                            wait_fill(act, f, 2 * i)
                            emit(i, 2 * s + c, f)

            def to(dest):
                def emit(i, j, f):
                    nc.scalar.activation(dest[:, bass.ds(i * 4 * S + j * S, S)], bank(f % 2), ACT.Copy)\
                      .then_inc(ring_free[f % 2], 1)
                return emit

            f = FILL["fl"]
            panel_hi(act, PANEL["fl"] + 1, 0, None)
            wait_fill(act, f)
            act.wait_ge(small_landed, SMALL_DMAS * 16)
            nc.scalar.activation(flog[0][0:HEADS], bank(f % 2)[0:HEADS], ACT.Identity, bias=bias_f[0:HEADS, 0:1])\
              .then_inc(ring_free[f % 2], 1)
            act.wait_ge(f_exp_in, 1)
            nc.scalar.activation(flog[1][0:HEADS], flog[1][0:HEADS], ACT.Exp, scale=-1.0).then_inc(f_exp, 1)
            act.wait_ge(f_exp_in, 2)
            nc.scalar.activation(flog[3][0:HEADS], flog[2][0:HEADS], ACT.Ln).then_inc(f_ln, 1)
            evacuate("mix", to(u))
            evacuate("qk", to(qk))
            n0, f0 = PANEL["v"], FILL["v"]
            for s in range(2):
                panel_hi(act, n0 + s + 1, 0, f0 + 2 * s)
                for g in range(2):
                    f = f0 + 2 * s + g
                    wait_fill(act, f)
                    nc.scalar.activation(
                        v.rearrange("p (b n) -> p b n", b=NB)[:, 2 * g:2 * g + 2, s * PCOL:(s + 1) * PCOL],
                        bank(f % 2).rearrange("p (b n) -> p b n", b=2), ACT.Copy).then_inc(ring_free[f % 2], 1)

            for j in range(2):
                hi_of_tmp(SPLIT["conv"] + j, b_hi, 6 + j)

            def from_psum(q, f, dest, k, rows=slice(0, P), scale=1.0):
                wait_fill(act, f)
                act.wait_ge(split_lo, q - 1)
                nc.scalar.activation(tmp[q % 2][rows], bank(f % 2)[rows], ACT.Copy, scale=scale)\
                  .then_inc(ring_free[f % 2], 1)
                wait_ring_read(act, f)
                nc.scalar.activation(tile_of(dest, k)[rows], tmp[q % 2][rows], ACT.Copy).then_inc(split_hi, 1)

            for j in range(2):
                from_psum(SPLIT["pool"] + j, FILL["pool"] + j, b_hi, 4 + j,
                          scale=par[:, PAR["pool_scale"] + j:PAR["pool_scale"] + j + 1])
            def cum_copy(h):
                wait_fill(act, attn_bc(h))
                if h >= 1:
                    act.wait_ge(scores_read, h)
                nc.scalar.activation(cum_bc, bank(attn_bc(h) % 2), ACT.Copy).then_inc(ring_free[attn_bc(h) % 2], 1)

            cum_copy(0)
            for h in range(HEADS):
                if h + 1 < HEADS:
                    cum_copy(h + 1)
                act.wait_ge(neg_max, h + 1)
                for i in range(NB):
                    sc = scores[h % 2][:, Q_OFF[i]:Q_OFF[i] + (i + 1) * P]
                    nc.scalar.activation(sc, sc, ACT.Exp, bias=lneg[:, 4 * h + i:4 * h + i + 1], scale=DH ** -0.5,
                                         accum_out=lsum[:, 4 * h + i:4 * h + i + 1]).then_inc(exp_done, 1)
                for j in range(3):
                    f = attn_pt(h, j)
                    wait_fill(act, f)
                    if j == 0 and h >= 1:
                        wait_fill(act, attn_o(h - 1))
                    n = 256 if j == 2 else 512
                    nc.scalar.activation(probs_tr[:, j * 512:j * 512 + n], bank(f % 2, n), ACT.Copy)\
                      .then_inc(ring_free[f % 2], 1)
                from_psum(SPLIT["attn"] + h, attn_o(h), b_hi, h // 2, slice(DH * (h % 2), DH * (h % 2) + DH))

            n0, f0 = PANEL["gates"], FILL["gates"]
            with act.Fori(0, 4) as i:
                for s in range(4):
                    if s == 0:
                        act.wait_ge(branch_done, 2 * i + 1)
                    panel_hi(act, n0 + s + 1, 2 * i, f0 + (0, 2, 5, 8)[s] + 8 * i)
                    if s == 3:
                        continue
                    for c in range(2):
                        f = f0 + 3 * s + c
                        wait_fill(act, f, 4 * i)
                        if s == 0 and c == 0:
                            act.wait_ge(branch_read, 2 * i + 1)
                        nc.scalar.activation(gate[:, (2 * s + c) * S:(2 * s + c + 1) * S], bank(f % 2), ACT.Tanh,
                                             scale=0.5).then_inc(ring_free[f % 2], 1)
            for k in range(KT):
                q = SPLIT["merged"] + k
                act.wait_ge(branch_read, k + 2)
                wait_fill(act, FILL["wout"] - 1)
                nc.scalar.activation(tile_of(h_hi, k), tile_of(merged, k), ACT.Copy, scale=0.5).then_inc(split_hi, 1)
            evacuate("wout", to(y))

            def squares(norm, source, ready=None):
                for k in range(KT):
                    q = 8 * NORM[norm] + k
                    if ready is not None:
                        act.wait_ge(*ready(k))
                    if q >= 2:
                        act.wait_ge(sq_read, q - 1)
                    nc.scalar.activation(sq[q % 2][:], tile_of(source, k), ACT.Square).then_inc(sq_done, 1)
                act.wait_ge(sq_read, 8 * NORM[norm] + 8)
                nc.scalar.activation(rb[:], bank(7), ACT.Sqrt, bias=eps_t[:, 0:1], scale=1.0 / D).then_inc(rms_done, 1)

            for b in range(2):
                wait_ring_read(act, FILL["wout"] + 6 + b)
            squares("mix_post", y)
            squares("ff_pre", x, lambda k: (x_ready, k + 1))
            for k in range(KT):
                hi_of_tmp(SPLIT["h_ff"] + k, h_hi, k, bias=mod[:, 24 + k:25 + k])

            n0, f0 = PANEL["ff"], FILL["ff"]
            with act.Fori(0, 4) as q:
                for s in range(8):
                    panel_hi(act, n0 + s + 1, 4 * q, f0 + 2 * s + 16 * q)
                    if s >= 4:
                        continue
                    for c in range(2):
                        j = 2 * s + c
                        f = f0 + j
                        wait_fill(act, f, 8 * q)
                        act.wait_ge(split_lo, SPLIT["hidden"] + j - 1 + 8 * q)
                        nc.scalar.activation(relu[j % 2], bank(f % 2), ACT.Relu).then_inc(ring_free[f % 2], 1)
                        wait_ring_read(act, f, 8 * q)
                        nc.scalar.activation(tile_of(b_hi, j), relu[j % 2], ACT.Square).then_inc(split_hi, 1)
            squares("ff_post", y, lambda k: (ring_free[(f0 + 56 + k) % 2], (f0 + 56 + k) // 2 + 1))
            squares("a_norm", x, lambda k: (x_ready, KT + k + 1))
            for k in range(KT):
                hi_of_tmp(SPLIT["h2"] + k, h_hi, k)
            f = FILL["dt"]
            panel_hi(act, PANEL["dt"] + 1, 0, f)
            wait_fill(act, f)
            nc.scalar.activation(dt_tmp[0][0:SSD_HEADS], bank(f % 2)[0:SSD_HEADS], ACT.Identity,
                                 bias=dt_bias[0:SSD_HEADS, 0:1]).then_inc(ring_free[f % 2], 1)
            nc.scalar.activation(a_rate[0:SSD_HEADS], a_log[0:SSD_HEADS], ACT.Exp).then_inc(rate_exp, 1)
            act.wait_ge(f_exp_in, 3)
            nc.scalar.activation(dt_tmp[1][0:SSD_HEADS], dt_tmp[1][0:SSD_HEADS], ACT.Exp, scale=-1.0).then_inc(f_exp, 1)
            act.wait_ge(f_exp_in, 4)
            nc.scalar.activation(dt_tmp[3][0:SSD_HEADS], dt_tmp[2][0:SSD_HEADS], ACT.Ln).then_inc(f_ln, 1)

            n0, f0 = PANEL["glu"], FILL["glu"]
            with act.Fori(0, 4) as i:
                for s in range(2):
                    panel_hi(act, n0 + s + 1, i, f0 + 2 * s + 4 * i)
                    for c in range(2):
                        f = f0 + 2 * s + c
                        wait_fill(act, f, 2 * i)
                        if s == 0:
                            nc.scalar.activation(glu[:, bass.ds(i * 2 * GLU_W + (c * GLU_W + DW_TAPS - 1), S)], bank(f % 2),
                                                 ACT.Copy).then_inc(ring_free[f % 2], 1)
                        else:
                            nc.scalar.activation(z_b[:, bass.ds(i * 2 * S + c * S, S)], bank(f % 2), ACT.Sigmoid)\
                              .then_inc(ring_free[f % 2], 1)
            n0, f0 = PANEL["xbc"], FILL["xbc"]
            with act.Fori(0, 4) as i:
                for j in range(5):
                    if j < 4:
                        if j % 2 == 0:
                            panel_hi(act, n0 + j // 2 + 1, i, f0 + j + 4 * i)
                        f = f0 + j
                        wait_fill(act, f, 2 * i)
                        act.wait_ge(taps_done, 4 * i + max(j, 1))
                        nc.scalar.activation(padded[j % 2][:, 3:3 + S], bank(f % 2), ACT.Copy)\
                          .then_inc(ring_free[f % 2], 1)
                    if j >= 1:
                        act.wait_ge(taps_done, 4 * i + j + 1)
                        nc.scalar.activation(xbc[:, bass.ds(i * 4 * S + (j - 1) * S, S)], taps[(j - 1) % 2], ACT.Silu,
                                             bias=par[:, bass.ds(i * 4 + (PAR["a_conv_b_2"] + j - 1), 1)])\
                          .then_inc(xbc_done, 1)
            act.wait_ge(ends_done, 1)
            nc.scalar.activation(to_end, to_end, ACT.Exp).then_inc(ends_exp, 1)
            nc.scalar.activation(end_decay, end_decay, ACT.Exp).then_inc(ends_exp, 1)
            for b in range(3):
                f = FILL["btok"] + b
                wait_fill(act, f)
                nc.scalar.activation(b_tok[:, b * S:(b + 1) * S], bank(f % 2), ACT.Copy).then_inc(ring_free[f % 2], 1)

            def head_decay(h):
                f = ssd_cum(h)
                wait_fill(act, f)
                if h >= 1:
                    act.wait_ge(decay_in, h)
                    act.wait_ge(from_start_done, h)
                nc.scalar.activation(csb, bank(f % 2), ACT.Copy).then_inc(ring_free[f % 2], 1)
                wait_ring_read(act, f)
                if h >= 2:
                    act.wait_ge(masked_scores, h - 1)
                nc.scalar.activation(from_start[h % 2], csb, ACT.Exp).then_inc(from_start_done, 1)

            def decay_exp(h):
                act.wait_ge(decay_in, h + 1)
                nc.scalar.activation(decay[h % 2][:], decay[h % 2][:], ACT.Exp).then_inc(decay_done, 1)

            def z_silu(h):
                f, k = ssd_z(h), 2 * (h // 4) + h % 2
                wait_fill(act, f)
                if h % 4 < 2 and k >= 2:
                    act.wait_ge(gated_y, k - 1)
                if h == 2:
                    act.wait_ge(dw_in_done, 8)
                nc.scalar.activation(z_a[k % 2] if h % 4 < 2 else tile_of(z_b, k), bank(f % 2), ACT.Silu)\
                  .then_inc(ring_free[f % 2], 1)

            head_decay(0)
            decay_exp(0)
            for h in range(SSD_HEADS):
                if h + 1 < SSD_HEADS:
                    head_decay(h + 1)
                    decay_exp(h + 1)
                if h % 2 == 0:
                    panel_hi(act, PANEL["z"] + h // 2 + 1, 0, ssd_z(h - 1) + 1 if h else FILL["xbc"] + 16)
                if h < 14:
                    z_silu(h)

            for g in range(SSD_GROUPS):
                for j in range(2):
                    q = SQ["ya"] + 2 * g + j
                    act.wait_ge(gated_y, 2 * g + j + 1)
                    act.wait_ge(masked_scores, SSD_HEADS)
                    act.wait_ge(sq_read, q - 1)
                    nc.scalar.activation(sq[q % 2][:], tile_of(xbc, 2 * g + j), ACT.Square).then_inc(sq_done, 1)
            z_silu(14)
            for g in range(SSD_GROUPS):
                act.wait_ge(sq_read, SQ["ya"] + 2 * g + 2)
                nc.scalar.activation(y_rms[g], bank(2 + g), ACT.Sqrt, bias=eps_t[:, 0:1], scale=1.0 / 256)\
                  .then_inc(rms_done, 1)
            for k in range(KT):
                hi_of_tmp(SPLIT["ya"] + k, b_hi, k)
                if k == 3:
                    z_silu(15)
            act.wait_ge(ln_summed, 1)
            nc.scalar.activation(rb[:], bank(6), ACT.Copy, scale=1.0 / D).then_inc(ln_mean, 1)

            def ln_activation(k):
                act.wait_ge(ln_scaled, k + 1)
                nc.scalar.activation(glu_tile(k), glu_tile(k), ACT.Silu, bias=par[:, PAR["a_ln_b_2"] + k:PAR["a_ln_b_2"] + k + 1],
                                     scale=par[:, PAR["a_ln_w_2"] + k:PAR["a_ln_w_2"] + k + 1]).then_inc(ln_silu, 1)

            n0, f0 = PANEL["out_a"], FILL["out_a"]
            for s in range(4):
                panel_hi(act, n0 + s + 1, 0, f0 + 2 * s)
                for c in range(2):
                    f = f0 + 2 * s + c
                    wait_fill(act, f)
                    nc.scalar.activation(tile_of(out_a, 2 * s + c), bank(f % 2), ACT.Copy).then_inc(ring_free[f % 2], 1)
                if s == 0:
                    for k in range(KT):
                        q = SQ["ln"] + k
                        act.wait_ge(centred, k + 1)
                        act.wait_ge(sq_read, q - 1)
                        nc.scalar.activation(sq[q % 2][:], glu_tile(k), ACT.Square).then_inc(sq_done, 1)
                    act.wait_ge(sq_read, SQ["ln"] + 8)
                    nc.scalar.activation(rb[:], bank(7), ACT.Sqrt, bias=eps_t[:, 1:2], scale=1.0 / D).then_inc(rms_done, 1)
                if s in (1, 2):
                    for k in range(4 * s - 4, 4 * s):
                        ln_activation(k)
            for k in range(KT):
                hi_of_tmp(SPLIT["yb"] + k, h_hi, k)
            panel_hi(act, PANEL["out_b"] + 1, 0, FILL["out_b"])
            act.wait_ge(split_lo, SPLIT["yb"] + KT)
            with nc.allow_non_contiguous_dma(reason="positions and a weight column"):
                act.dma_start(position.bitcast(I32), t["positions_2"].rearrange("a (b p) -> p (a b)", p=P))\
                  .then_inc(diff_landed, 16)
                act.dma_start(sub_w, t["c_subln_w_2"].rearrange("a n -> n a")).then_inc(diff_landed, 16)
            for j, name in enumerate(("c_lq1_2", "c_lq2_2", "c_lk1_2", "c_lk2_2")):
                act.dma_start(lam_in[:, 64 * j:64 * j + 64], t[name].to_broadcast([P, DH])).then_inc(diff_landed, 16)
            for j, name in enumerate(("c_q_norm_w_2", "c_k_norm_w_2")):
                act.dma_start(qk_w[:, 64 * j:64 * j + 64], t[name].to_broadcast([P, DH])).then_inc(diff_landed, 16)
            n0, f0 = PANEL["out_b"], FILL["out_b"]
            for s in range(1, 4):
                panel_hi(act, n0 + s + 1, 0, f0 + 2 * s)
            act.wait_ge(angle_in, 2)
            nc.scalar.activation(sines, sines, ACT.Sin).then_inc(sin_done, 1)
            nc.scalar.activation(cosines, cosines, ACT.Sin).then_inc(sin_done, 1)
            act.wait_ge(lam_in_done, 1)
            nc.scalar.activation(lam_e, lam_e, ACT.Exp).then_inc(lam_exp, 1)
            squares("c_norm", x, lambda k: (ring_free[(f0 + k) % 2], (f0 + k) // 2 + 1))
            for k in range(KT):
                hi_of_tmp(SPLIT["h3"] + k, h_hi, k)
            n0, f0 = PANEL["dqk"], FILL["dqk"]
            with act.Fori(0, 4) as i:
                for s in range(2):
                    panel_hi(act, n0 + s + 1, i, f0 + 2 * s + 4 * i)
                    for c in range(2):
                        f = f0 + 2 * s + c
                        wait_fill(act, f, 2 * i)
                        nc.scalar.activation(qkv[:, bass.ds(i * 2 * S + (s * 8 + c) * S, S)], bank(f % 2), ACT.Copy)\
                          .then_inc(ring_free[f % 2], 1)
                    act.wait_ge(qk_squared, 2 * i + s + 1)
                    nc.scalar.activation(qk_ms, qk_ms, ACT.Sqrt, bias=eps_t[:, 0:1], scale=1.0 / DH).then_inc(qk_rms, 1)
            evacuate("dv", to(qkv[:, 8192:12288]))

            def copy_q_t(h):
                f = diff_t(h, 0)
                wait_fill(act, f)
                nc.scalar.activation(q_t[:], bank(f % 2), ACT.Copy).then_inc(ring_free[f % 2], 1)

            def diff_root(h):
                f = diff_sum(h)
                wait_fill(act, f)
                nc.scalar.activation(rb[:], bank(f % 2), ACT.Sqrt, bias=eps_t[:, 0:1], scale=1.0 / P)\
                  .then_inc(ring_free[f % 2], 1)

            copy_q_t(0)
            for h in range(HEADS):
                if h + 1 < HEADS:
                    copy_q_t(h + 1)
                for m in range(2):
                    act.wait_ge(diff_neg_max, 2 * h + m + 1)
                    if m == 1 and h:
                        act.wait_ge(diff_weights, 4 * h)
                    if m == 0 and h >= 2:
                        wait_fill(act, diff_wt(h - 2, 2))
                    for i in range(NB):
                        o, n, col = Q_OFF[i], (i + 1) * P, 8 * (h % 2) + 4 * m + i
                        dest = (weights[h % 2], probs_1)[m]
                        nc.scalar.activation(dest[:, o:o + n], psum[:, (2 + 3 * m) * 512 + o:(2 + 3 * m) * 512 + o + n],
                                             ACT.Exp, bias=lneg[:, col:col + 1], scale=DH ** -0.5,
                                             accum_out=lsum[:, col:col + 1]).then_inc(diff_exp, 1)
                if h:
                    diff_root(h - 1)
                if h % 2 == 0:
                    panel_hi(act, PANEL["dgate"] + h // 2 + 1, 0, diff_gate(h - 1) + 1 if h else FILL["dattn"])
                for j in range(3):
                    f, n = diff_wt(h, j), 256 if j == 2 else 512
                    wait_fill(act, f)
                    if j == 0 and h:
                        wait_fill(act, diff_o(h - 1))
                    nc.scalar.activation(weights_tr[j], bank(f % 2, n), ACT.Copy).then_inc(ring_free[f % 2], 1)
                if h:
                    hi_of_tmp(SPLIT["o"] + h - 1, b_hi, h - 1)
                q, f = SPLIT["o"] + h, diff_o(h)
                wait_fill(act, f)
                act.wait_ge(split_lo, q - 1)
                if h:
                    act.wait_ge(o_normed, h)
                step.mark(nc.scalar.activation(tmp[q % 2][:], bank(f % 2), ACT.Copy))
                nc.scalar.activation(rb[:], bank(f % 2), ACT.Square).then_inc(ring_free[f % 2], 1)
                f = diff_gate(h)
                wait_fill(act, f)
                if h >= 2:
                    act.wait_ge(split_src, dve_source(q - 2))
                nc.scalar.activation(d_gate[h % 2], bank(f % 2), ACT.Silu).then_inc(ring_free[f % 2], 1)
            diff_root(HEADS - 1)
            hi_of_tmp(SPLIT["o"] + 7, b_hi, 7)
            n0, f0 = PANEL["dout"], FILL["dout"]
            for s in range(4):
                if s < 3:
                    panel_hi(act, n0 + s + 1, 0, f0 + 2 * s if s else diff_gate(HEADS - 1) + 1)
                for g in range(2):
                    f = f0 + 2 * s + g
                    wait_fill(act, f)
                    nc.scalar.activation(tile_of(final, 2 * s + g), bank(f % 2), ACT.Copy)\
                      .then_inc(ring_free[f % 2], 1)

        @block.vector
        def _(dve):
            step = Tally(dve_step)

            def alone(instruction):
                step.mark(instruction)
                step.last(dve)

            def ada_panel(a, d, buf):
                for k in range(KT):
                    w = ada[a % 2][:, k * PCOL:(k + 1) * PCOL]
                    if k == 0:
                        ins = nc.vector.tensor_scalar(ada_acc[buf], w, silu_c[:, 0:1], None, ALU.mult)
                    else:
                        ins = nc.vector.scalar_tensor_tensor(out=ada_acc[buf], in0=w, scalar=silu_c[:, k:k + 1],
                                                             in1=ada_acc[buf], op0=ALU.mult, op1=ALU.add)
                    if k == KT - 1:
                        ins.then_inc(ada_acc_done, 1)
                    else:
                        ins.then_inc(dve_step, 1)
                        dve.wait_ge(dve_step, step.n + k + 1)
                step.n = step.n + KT - 1

            alone(nc.vector.memset(eps_t[:, 0:1], EPS))
            nc.vector.memset(eps_t[:, 1:2], LN_EPS).then_inc(eps_done, 1)
            dve.wait_ge(silu_t, 1)
            alone(nc.vector.scalar_tensor_tensor(out=silu_c, in0=silu_c, scalar=1.0, in1=par[:, 0:8],
                                                 op0=ALU.add, op1=ALU.mult))
            nc.vector.tensor_scalar(silu_c, silu_c, 0.5, None, ALU.mult).then_inc(silu_c_done, 1)
            dve.wait_ge(silu_c_done, 1)
            dve.wait_ge(consts_done, CONSTS)
            dve.wait_ge(x_rms, 1)
            alone(nc.vector.reciprocal(r_x, r_x))
            for b in range(NB):
                nc.vector.tensor_scalar(diag[:, b * P:(b + 1) * P], ident[:], r_x[:, b:b + 1], None, ALU.mult)\
                  .then_inc(x_diag, 1)
            for k in range(KT):
                f = FILL["x"] + 2 * k + 1
                wait_fill(dve, f)
                nc.vector.tensor_copy(tile_of(xn, k), bank(f % 2)).then_inc(ring_free[f % 2], 1)
            dve.wait_ge(mod_columns, 1)
            alone(nc.vector.tensor_tensor(mod[:, 0:16], bank(6, 16), par[:, PAR["b_ada"]:PAR["b_ada"] + 16], ALU.add))
            alone(nc.vector.scalar_tensor_tensor(out=a_mix, in0=mod[:, 8:16], scalar=1.0,
                                                 in1=par[:, PAR["g_mix_pre"]:PAR["g_mix_pre"] + 8],
                                                 op0=ALU.add, op1=ALU.mult))

            def lo_of_tmp(q, dest, k, bias=None):
                dve.wait_ge(split_hi, q + 1)
                if bias is None:
                    nc.vector.tensor_tensor(tile_of(dest[1], k), tmp[q % 2][:], tile_of(dest[0], k).bitcast(F32),
                                            ALU.subtract).then_inc(split_lo, 1)
                else:
                    nc.vector.scalar_tensor_tensor(out=tile_of(dest[1], k), in0=tmp[q % 2][:], scalar=bias,
                                                   in1=tile_of(dest[0], k).bitcast(F32),
                                                   op0=ALU.add, op1=ALU.subtract).then_inc(split_lo, 1)

            def split_tiles(q0, dest, source, bias=lambda k: None):
                def src(k):
                    if q0 + k >= 2:
                        dve.wait_ge(split_lo, q0 + k - 1)
                    source(k, tmp[(q0 + k) % 2][:]).then_inc(split_src, 1)
                src(0)
                for k in range(KT):
                    if k + 1 < KT:
                        src(k + 1)
                    lo_of_tmp(q0 + k, dest, k, bias(k))

            split_tiles(SPLIT["h1"], (h_hi, h_lo),
                        lambda k, o: nc.vector.tensor_scalar(o, tile_of(xn, k), a_mix[:, k:k + 1], mod[:, k:k + 1],
                                                             ALU.mult, ALU.add))

            z, e, w, l, d = (b[0:HEADS] for b in flog)
            f = FILL["fl"]
            wait_ring_read(dve, f)
            nc.vector.scalar_tensor_tensor(out=e, in0=z, scalar=-1.0, in1=z, op0=ALU.mult, op1=ALU.max)\
              .then_inc(f_exp_in, 1)
            dve.wait_ge(f_exp, 1)
            nc.vector.tensor_scalar(w, e, 1.0, None, ALU.add).then_inc(f_exp_in, 1)
            dve.wait_ge(f_ln, 1)
            log1p(dve, alone, e, w, l, d)
            alone(nc.vector.scalar_tensor_tensor(out=l, in0=z, scalar=0.0, in1=l, op0=ALU.min, op1=ALU.subtract))
            alone(nc.vector.memset(w, 1.0))
            alone(nc.vector.tensor_tensor_scan(z, w, l, 0.0, ALU.mult, ALU.add))
            nc.vector.tensor_scalar(z, z, -float(DH ** 0.5), None, ALU.mult).then_inc(cum_done, 1)

            f0 = FILL["mix"]
            for b in range(2):
                wait_ring_read(dve, f0 + 6 + b)
            alone(nc.vector.memset(win_n, 2.0))
            for j in range(2):
                for half in range(2):
                    r = slice(DH * half, DH * half + DH)
                    win = float(WINDOWS[2 * j + half])
                    alone(nc.vector.tensor_scalar(win_n[r, 16 * j:16 * j + 16], win_i[r], win, None, ALU.min))
            alone(nc.vector.reciprocal(win_inv, win_n))
            for j in range(2):
                value = tile_of(u, j)
                have, reach = value, 1
                for level in range(2 * j + 2):
                    rows = slice(DH, P) if level == 2 * j + 1 else slice(0, P)
                    o = pool_sum[level % 2] if have is not pool_sum[level % 2] else pool_sum[1 - level % 2]
                    if level == 2 * j + 1:
                        alone(nc.vector.tensor_copy(o[0:DH], have[0:DH]))
                    alone(nc.vector.tensor_copy(o[rows, 0:reach], have[rows, 0:reach]))
                    alone(nc.vector.tensor_tensor(o[rows, reach:S], have[rows, reach:S], have[rows, 0:S - reach],
                                                  ALU.add))
                    have, reach = o, 2 * reach
                first = win_n[:, 16 * j:16 * j + 16]
                alone(nc.vector.tensor_tensor(first, have[:, 0:16], win_inv[:, 16 * j:16 * j + 16], ALU.mult))
                alone(nc.vector.tensor_tensor(first, first, value[:, 0:16], ALU.subtract))
                alone(nc.vector.scalar_tensor_tensor(out=value, in0=have, scalar=win_inv[:, 16 * j + 15:16 * j + 16],
                                                     in1=value, op0=ALU.mult, op1=ALU.subtract))
                nc.vector.tensor_copy(value[:, 0:16], first).then_inc(pooled, 1)
            ch, cb, cc = 2, 4, 6
            conv_w = PAR["conv_w"]
            for j in range(2):
                q = SPLIT["conv"] + j
                value, o = tile_of(u, ch + j), tmp[q % 2][:]
                alone(nc.vector.tensor_tensor(value, value, tile_of(u, cc + j), ALU.mult))
                alone(nc.vector.tensor_scalar(o, value, par[:, conv_w + 4 + j:conv_w + 5 + j], None, ALU.mult))
                for lag in (1, 2):
                    col = conv_w + 2 * (2 - lag) + j
                    alone(nc.vector.scalar_tensor_tensor(out=o[:, lag:S], in0=value[:, 0:S - lag],
                                                         scalar=par[:, col:col + 1], in1=o[:, lag:S],
                                                         op0=ALU.mult, op1=ALU.add))
                nc.vector.tensor_tensor(o, o, tile_of(u, cb + j), ALU.mult).then_inc(split_src, 1)
            for j in range(2):
                lo_of_tmp(SPLIT["conv"] + j, (b_hi, b_lo), 6 + j)
            for j in range(2):
                lo_of_tmp(SPLIT["pool"] + j, (b_hi, b_lo), 4 + j)

            def add_bias(h):
                wait_ring_read(dve, attn_bc(h))
                alone(nc.vector.tensor_tensor(cum_bcm.rearrange("p (b n) -> p b n", b=NB),
                                              cum_bc.rearrange("p (b n) -> p b n", b=NB),
                                              causal_qk[:].unsqueeze(1).to_broadcast([P, NB, P]), ALU.add))
                dve.wait_ge(scores_done, h + 1)
                if h >= 2:
                    wait_fill(dve, attn_pt(h - 2, 2))
                sc = scores[h % 2]
                base = (2 + 3 * (h % 2)) * 512
                for i in (3, 2, 0, 1):
                    o = Q_OFF[i]
                    if i:
                        nc.vector.tensor_tensor(sc[:, o:o + i * P], psum[:, base + o:base + o + i * P],
                                                cum_bc[:, 0:i * P], ALU.add).then_inc(dve_step, 1)
                        step.n = step.n + 1
                    o += i * P
                    ins = nc.vector.tensor_tensor(sc[:, o:o + P], psum[:, base + o:base + o + P],
                                                  cum_bcm[:, i * P:(i + 1) * P], ALU.add)
                    if i == 1:
                        step.last(dve)
                        ins.then_inc(scores_read, 1)
                    else:
                        step.mark(ins)
                dve.wait_ge(scores_read, h + 1)
                for i in range(NB):
                    step.mark(nc.vector.tensor_reduce(lmax[:, 4 * h + i:4 * h + i + 1],
                                                      sc[:, Q_OFF[i]:Q_OFF[i] + (i + 1) * P], AX_X, ALU.max))
                step.last(dve)
                nc.vector.tensor_scalar(lneg[:, 4 * h:4 * h + 4], lmax[:, 4 * h:4 * h + 4], -(DH ** -0.5), None,
                                        ALU.mult).then_inc(neg_max, 1)

            add_bias(0)
            for h in range(HEADS):
                dve.wait_ge(exp_done, 4 * h + 4)
                alone(nc.vector.reciprocal(linv[:, 4 * h:4 * h + 4], lsum[:, 4 * h:4 * h + 4]))
                for i in range(NB):
                    sc = scores[h % 2][:, Q_OFF[i]:Q_OFF[i] + (i + 1) * P]
                    nc.vector.tensor_scalar(sc, sc, linv[:, 4 * h + i:4 * h + i + 1], None, ALU.mult)\
                      .then_inc(probs_done, 1)
                if h + 1 < HEADS:
                    add_bias(h + 1)
                p0, q = DH * (h % 2), SPLIT["attn"] + h
                dve.wait_ge(split_hi, q + 1)
                nc.vector.tensor_tensor(tile_of(b_lo, h // 2)[p0:p0 + DH], tmp[q % 2][p0:p0 + DH],
                                        tile_of(b_hi, h // 2)[p0:p0 + DH].bitcast(F32), ALU.subtract)\
                  .then_inc(split_lo, 1)

            nc.vector.memset(gate_tmp, 0.0).then_inc(branch_read, 1)
            per_turn = 4 * (KT - 1) + 2 * 4
            f0 = FILL["gates"]
            with dve.Fori(0, 4) as i:
                step.enter(i, per_turn)
                for g in range(2):
                    for a in (2 * g, 2 * g + 1):
                        dve.wait_ge(ada_landed[a % 2], 16 * (4 + a // 2) + 32 * i)
                        dve.wait_ge(fill_done, f0 + 8 * i + (0 if g == 0 else 3))
                        ada_panel(a, i, a % 2)
                    f = f0 + 2 + 3 * g
                    wait_fill(dve, f, 4 * i)
                    nc.vector.tensor_tensor(mod[:, bass.ds(i * 8 + (16 + 4 * g), 4)], bank(f % 2, 4),
                                            par[:, bass.ds(i * 8 + (PAR["b_ada"] + 16 + 4 * g), 4)], ALU.add)\
                      .then_inc(ring_free[f % 2], 1)
                for c in range(2):
                    wait_ring_read(dve, f0 + 6 + c, 4 * i)
                for c in range(2):
                    dve.wait_ge(branch_done, 2 * i + c + 2)
                    total = merged[:, bass.ds(i * 2 * S + c * S, S)]

                    def gated(b, o):
                        return nc.vector.scalar_tensor_tensor(
                            out=o, in0=gate[:, (2 * b + c) * S:(2 * b + c + 1) * S], scalar=1.0,
                            in1=bank(2 + 3 * c + b), op0=ALU.add, op1=ALU.mult)
                    alone(gated(0, total))
                    alone(gated(1, gate_tmp))
                    alone(nc.vector.tensor_tensor(total, total, gate_tmp, ALU.add))
                    alone(gated(2, gate_tmp))
                    nc.vector.tensor_tensor(total, total, gate_tmp, ALU.add).then_inc(branch_read, 1)
            step.leave(4)
            wait_ring_read(dve, f0 + 26)
            wait_ring_read(dve, f0 + 29)
            alone(nc.vector.tensor_tensor(g_mix, mod[:, 16:24], par[:, PAR["g_mix_post"]:PAR["g_mix_post"] + 8], ALU.mult))
            alone(nc.vector.scalar_tensor_tensor(out=a_ff, in0=mod[:, 32:40], scalar=1.0,
                                                 in1=par[:, PAR["g_ff_pre"]:PAR["g_ff_pre"] + 8],
                                                 op0=ALU.add, op1=ALU.mult))
            alone(nc.vector.tensor_tensor(g_ff, mod[:, 40:48], par[:, PAR["g_ff_post"]:PAR["g_ff_post"] + 8], ALU.mult))
            for k in range(KT):
                q = SPLIT["merged"] + k
                dve.wait_ge(split_hi, q + 1)
                nc.vector.scalar_tensor_tensor(out=tile_of(h_lo, k), in0=tile_of(merged, k), scalar=0.5,
                                               in1=tile_of(h_hi, k).bitcast(F32), op0=ALU.mult, op1=ALU.subtract)\
                  .then_inc(split_lo, 1)

            def reciprocal_rms(norm):
                n = RMS.get(norm, NORM[norm]) + 1
                dve.wait_ge(rms_done, n)
                nc.vector.reciprocal(rb[:], rb[:]).then_inc(rinv_done, 1)
                dve.wait_ge(rinv_done, n)

            def add_normed(gain):
                for k in range(KT):
                    step.mark(nc.vector.tensor_tensor(tile_of(y, k), tile_of(y, k), rb[:], ALU.mult))
                step.last(dve)
                for k in range(KT):
                    nc.vector.scalar_tensor_tensor(out=tile_of(x, k), in0=tile_of(y, k), scalar=gain[:, k:k + 1],
                                                   in1=tile_of(x, k), op0=ALU.mult, op1=ALU.add).then_inc(x_ready, 1)

            def normed(gain):
                return lambda k, o: nc.vector.scalar_tensor_tensor(out=o, in0=tile_of(x, k), scalar=gain[:, k:k + 1],
                                                                   in1=rb[:], op0=ALU.mult, op1=ALU.mult)

            reciprocal_rms("mix_post")
            add_normed(g_mix)
            reciprocal_rms("ff_pre")
            split_tiles(SPLIT["h_ff"], (h_hi, h_lo), normed(a_ff), lambda k: mod[:, 24 + k:25 + k])
            alone(nc.vector.memset(y, 0.0))

            f0 = FILL["ff"]
            with dve.Fori(0, 4) as q:
                step.enter(q, 8)
                for j in range(KT):
                    f = f0 + j
                    wait_ring_read(dve, f, 8 * q)
                    alone(nc.vector.tensor_tensor(relu_sq[j % 2], relu[j % 2], relu[j % 2], ALU.mult))
                    dve.wait_ge(split_hi, SPLIT["hidden"] + j + 1 + 8 * q)
                    nc.vector.tensor_tensor(tile_of(b_lo, j), relu_sq[j % 2], tile_of(b_hi, j).bitcast(F32),
                                            ALU.subtract).then_inc(split_lo, 1)
                for j in range(KT):
                    f = f0 + 8 + j
                    wait_fill(dve, f, 8 * q)
                    nc.vector.tensor_tensor(tile_of(y, j), tile_of(y, j), bank(f % 2), ALU.add)\
                      .then_inc(ring_free[f % 2], 1)
            step.leave(4)
            reciprocal_rms("ff_post")
            add_normed(g_ff)
            reciprocal_rms("a_norm")
            split_tiles(SPLIT["h2"], (h_hi, h_lo), normed(par[:, PAR["a_norm_w_2"]:PAR["a_norm_w_2"] + 8]))
            alone(nc.vector.memset(padded[0][:, 0:3], 0.0))
            nc.vector.memset(padded[1][:, 0:3], 0.0).then_inc(taps_done, 1)
            for half in range(2):
                r = slice(DH * half, DH * half + DH)
                alone(nc.vector.tensor_copy(d_skip[r], d_all[r].rearrange("p (j b) -> p b j", b=2)[:, half]))
            dt, e, w, l, d = (b[0:SSD_HEADS] for b in dt_tmp)
            f = FILL["dt"]
            wait_ring_read(dve, f)
            nc.vector.scalar_tensor_tensor(out=e, in0=dt, scalar=-1.0, in1=dt, op0=ALU.mult, op1=ALU.max)\
              .then_inc(f_exp_in, 1)
            dve.wait_ge(f_exp, 2)
            nc.vector.tensor_scalar(w, e, 1.0, None, ALU.add).then_inc(f_exp_in, 1)
            dve.wait_ge(f_ln, 2)
            log1p(dve, alone, e, w, l, d)
            alone(nc.vector.scalar_tensor_tensor(out=dt, in0=dt, scalar=0.0, in1=l, op0=ALU.max, op1=ALU.add))
            dve.wait_ge(rate_exp, 1)
            alone(nc.vector.tensor_scalar(l, dt, a_rate[0:SSD_HEADS], -1.0, ALU.mult, ALU.mult))
            alone(nc.vector.memset(w, 1.0))
            for b in range(NB):
                nc.vector.tensor_tensor_scan(cum[0:SSD_HEADS, b * P:(b + 1) * P], w[:, b * P:(b + 1) * P],
                                             l[:, b * P:(b + 1) * P], 0.0, ALU.mult, ALU.add).then_inc(cum_chunks, 1)

            nc.vector.memset(glu.rearrange("p (k n) -> p k n", k=KT)[:, :, 0:DW_TAPS - 1], 0.0).then_inc(dw_done, 1)
            f0 = FILL["glu"]
            with dve.Fori(0, 2) as i:
                step.enter(i, 2 * (DW_TAPS - 1))
                dve.wait_ge(dw_done, 2 * i + 1)
                for c in range(2):
                    wait_ring_read(dve, f0 + c, 2 * i)
                    wait_ring_read(dve, f0 + 2 + c, 2 * i)
                    value = glu[:, bass.ds(i * 2 * GLU_W + (c * GLU_W + DW_TAPS - 1), S)]
                    nc.vector.tensor_tensor(value, value, z_b[:, bass.ds(i * 2 * S + c * S, S)], ALU.mult)\
                      .then_inc(dw_in_done, 1)
                dve.wait_ge(dw_in_done, 2 * i + 2)
                for tap in range(DW_TAPS):
                    last = tap == DW_TAPS - 1
                    for c in range(2):
                        if tap:
                            dve.wait_ge(dve_step, step.n - (0 if last and c else 1))
                        src = glu[:, bass.ds(i * 2 * GLU_W + (c * GLU_W + tap), S)]
                        w_tap = par[:, bass.ds(i * 2 + (PAR["a_dw_w_2"] + 8 * tap + c), 1)]
                        if tap == 0:
                            ins = nc.vector.tensor_scalar(dw_acc[c], src, w_tap,
                                                          par[:, bass.ds(i * 2 + (PAR["a_dw_b_2"] + c), 1)],
                                                          ALU.mult, ALU.add)
                        else:
                            ins = nc.vector.scalar_tensor_tensor(out=src if last else dw_acc[c], in0=src, scalar=w_tap,
                                                                 in1=dw_acc[c], op0=ALU.mult, op1=ALU.add)
                        if last:
                            ins.then_inc(dw_done, 1)
                        else:
                            step.mark(ins)
            step.leave(2)
            for k in range(4, KT):
                wait_ring_read(dve, f0 + 4 * (k // 2) + k % 2)
                wait_ring_read(dve, f0 + 4 * (k // 2) + 2 + k % 2)
                nc.vector.tensor_tensor(glu_tile(k), glu_tile(k), tile_of(z_b, k), ALU.mult).then_inc(dw_in_done, 1)
            dve.wait_ge(dw_in_done, KT)
            dve.wait_ge(dw_done, 5)

            def dw_taps(k, t0, t1, acc):
                for tap in range(t0, min(t1, DW_TAPS)):
                    src = glu[:, k * GLU_W + tap:k * GLU_W + tap + S]
                    w_tap = par[:, PAR["a_dw_w_2"] + 8 * tap + k:PAR["a_dw_w_2"] + 8 * tap + k + 1]
                    if tap == 0:
                        dve.wait_ge(dw_done, k + 1)
                        alone(nc.vector.tensor_scalar(acc, src, w_tap, par[:, PAR["a_dw_b_2"] + k:PAR["a_dw_b_2"] + k + 1],
                                                      ALU.mult, ALU.add))
                    elif tap < DW_TAPS - 1:
                        alone(nc.vector.scalar_tensor_tensor(out=acc, in0=src, scalar=w_tap, in1=acc,
                                                             op0=ALU.mult, op1=ALU.add))
                    else:
                        nc.vector.scalar_tensor_tensor(out=src, in0=src, scalar=w_tap, in1=acc,
                                                       op0=ALU.mult, op1=ALU.add).then_inc(dw_done, 1)

            dw_taps(4, 0, 1, dw_acc[0])
            f0 = FILL["xbc"]
            with dve.Fori(0, 4) as i:
                step.enter(i, 4 * (SSD_TAPS - 1) + 7)
                for tap in range(7):
                    alone(nc.vector.scalar_tensor_tensor(
                        out=dw_acc[0], in0=glu[:, bass.ds(i * 7 + (4 * GLU_W + 1 + tap), S)],
                        scalar=par[:, bass.ds(i * 56 + (PAR["a_dw_w_2"] + 8 * (1 + tap) + 4), 1)], in1=dw_acc[0],
                        op0=ALU.mult, op1=ALU.add))
                for j in range(4):
                    f = f0 + j
                    wait_ring_read(dve, f, 2 * i)
                    for tap in range(SSD_TAPS):
                        src = padded[j % 2][:, tap:tap + S]
                        w_tap = par[:, bass.ds(i * 4 + (PAR["a_conv_w_2"] + 16 * tap + j), 1)]
                        if tap == 0:
                            alone(nc.vector.tensor_scalar(taps[j % 2], src, w_tap, None, ALU.mult))
                            continue
                        ins = nc.vector.scalar_tensor_tensor(out=taps[j % 2], in0=src, scalar=w_tap, in1=taps[j % 2],
                                                             op0=ALU.mult, op1=ALU.add)
                        if tap == SSD_TAPS - 1:
                            ins.then_inc(taps_done, 1)
                        else:
                            alone(ins)
            step.leave(4)

            dw_taps(4, 29, 31, dw_acc[0])

            f = FILL["dtt"]
            wait_fill(dve, f)
            step.mark(nc.vector.tensor_copy(dt_tok, bank(f % 2, 64)))
            nc.vector.tensor_scalar(ncum_tok, bank(f % 2, 64, 64), -1.0, None, ALU.mult).then_inc(ring_free[f % 2], 1)
            wait_ring_read(dve, f)
            f = FILL["dtt"] + 1
            wait_fill(dve, f)
            step.mark(nc.vector.tensor_scalar(end_decay, bank(f % 2, 64), -1.0, None, ALU.mult))
            step.last(dve)
            nc.vector.tensor_copy(to_end, bank(f % 2, 64)).then_inc(ring_free[f % 2], 1)
            wait_ring_read(dve, f)
            nc.vector.tensor_tensor(to_end, ncum_tok, to_end, ALU.subtract).then_inc(ends_done, 1)
            for b in range(NB):
                for half in range(2):
                    f = FILL["xtok"] + 2 * b + half
                    wait_fill(dve, f)
                    nc.vector.tensor_tensor(
                        xd[:, b * D + half * S:b * D + (half + 1) * S].rearrange("p (h c) -> p h c", h=8),
                        bank(f % 2).rearrange("p (h c) -> p h c", h=8),
                        dt_tok[:, b * 16 + half * 8:b * 16 + half * 8 + 8].unsqueeze(2).to_broadcast([P, 8, DH]),
                        ALU.mult).then_inc(ring_free[f % 2], 1)
            for b in range(2):
                wait_ring_read(dve, FILL["xtok"] + 6 + b)
            dve.wait_ge(ends_exp, 2)

            def end_weighted(g):
                nc.vector.tensor_tensor(
                    xdu.rearrange("p (b h c) -> p b h c", b=3, h=4),
                    xd.rearrange("p (b g h c) -> p b g h c", b=NB, g=SSD_GROUPS, h=4)[:, 0:3, g],
                    to_end.rearrange("p (b g h) -> p b g h", b=NB, g=SSD_GROUPS)[:, 0:3, g].unsqueeze(3)
                    .to_broadcast([P, 3, 4, DH]), ALU.mult).then_inc(xdu_done, 1)

            def states(g):
                dve.wait_ge(states_summed, g + 1)
                if g:
                    wait_fill(dve, ssd_y(4 * g - 1))
                base = (4 + 2 * (g % 2)) * 512
                alone(nc.vector.tensor_copy(state[:, 0:256], psum[:, base:base + 256]))
                for b in (1, 2):
                    here = state[:, b * 256:(b + 1) * 256]
                    alone(nc.vector.tensor_tensor(
                        here.rearrange("p (h c) -> p h c", h=4),
                        state[:, (b - 1) * 256:b * 256].rearrange("p (h c) -> p h c", h=4),
                        end_decay[:, b * 16 + 4 * g:b * 16 + 4 * g + 4].unsqueeze(2).to_broadcast([P, 4, DH]), ALU.mult))
                    ins = nc.vector.tensor_tensor(here, here, psum[:, base + b * 256:base + (b + 1) * 256], ALU.add)
                    if b == 1:
                        alone(ins)
                    else:
                        ins.then_inc(states_done, 1)

            def decay_exponent(h):
                wait_ring_read(dve, ssd_cum(h))
                for b in range(NB):
                    ins = nc.vector.scalar_tensor_tensor(out=decay[h % 2][:, b * P:(b + 1) * P], in0=csb[:, b * P:(b + 1) * P],
                                                         scalar=ncum_tok[:, b * 16 + h:b * 16 + h + 1], in1=causal_kq[:],
                                                         op0=ALU.add, op1=ALU.add)
                    if b < NB - 1:
                        step.mark(ins)
                    else:
                        ins.then_inc(decay_in, 1)

            def head_out(h):
                f, r = ssd_y(h), slice(DH * (h % 2), DH * (h % 2) + DH)
                wait_fill(dve, f)
                part = tile_of(xbc, h // 2)[r]
                nc.vector.scalar_tensor_tensor(out=part, in0=part, scalar=d_skip[r, h // 2:h // 2 + 1], in1=bank(f % 2)[r],
                                               op0=ALU.mult, op1=ALU.add).then_inc(ring_free[f % 2], 1)

            end_weighted(0)
            decay_exponent(0)
            for h in range(SSD_HEADS):
                g = h // 4
                if h % 4 == 0:
                    states(g)
                    if g + 1 < SSD_GROUPS:
                        end_weighted(g + 1)
                if h >= 1:
                    wait_fill(dve, ssd_y(h - 1))
                dve.wait_ge(from_start_done, h + 1)
                step.mark(nc.vector.tensor_tensor(c_scaled[:, P:S], tile_of(xbc, 12 + g)[:, P:S], from_start[h % 2][:, P:S],
                                                  ALU.mult))
                dve.wait_ge(decay_done, h + 1)
                dve.wait_ge(cb_done, g + 1)
                step.last(dve)
                nc.vector.tensor_tensor(masked, bank(2 + g % 2), decay[h % 2][:], ALU.mult).then_inc(masked_scores, 1)
                if h + 1 < SSD_HEADS:
                    decay_exponent(h + 1)
                first, end = 6 * h, 6 * h + 6
                for k in range(5, KT):
                    base = DW_TAPS * (k - 5)
                    if first < base + DW_TAPS and end > base:
                        dw_taps(k, max(first - base, 0), end - base, dw_acc_late)
                head_out(h)
                if h % 2:
                    k = h // 2
                    wait_ring_read(dve, ssd_z(4 * (k // 2) + k % 2))
                    wait_ring_read(dve, ssd_y(h))
                    wait_ring_read(dve, ssd_y(h - 1))
                    nc.vector.tensor_tensor(tile_of(xbc, k), tile_of(xbc, k), z_a[k % 2], ALU.mult).then_inc(gated_y, 1)

            def ya_src(k):
                g, q, w = k // 2, SPLIT["ya"] + k, PAR["a_ssd_norm_w_2"] + k
                if k % 2 == 0:
                    dve.wait_ge(rms_done, RMS["ya"] + g + 1)
                    nc.vector.reciprocal(y_rms[g], y_rms[g]).then_inc(rinv_done, 1)
                    dve.wait_ge(rinv_done, RMS["ya"] + g + 1)
                dve.wait_ge(split_lo, q - 1)
                nc.vector.scalar_tensor_tensor(out=tmp[q % 2][:], in0=tile_of(xbc, k), scalar=par[:, w:w + 1], in1=y_rms[g],
                                               op0=ALU.mult, op1=ALU.mult).then_inc(split_src, 1)

            ya_src(0)
            for k in range(KT):
                if k + 1 < KT:
                    ya_src(k + 1)
                lo_of_tmp(SPLIT["ya"] + k, (b_hi, b_lo), k)
            dve.wait_ge(ln_mean, 1)
            for k in range(KT):
                nc.vector.tensor_tensor(glu_tile(k), glu_tile(k), rb[:], ALU.subtract).then_inc(centred, 1)
            dve.wait_ge(rms_done, RMS["ln"] + 1)
            nc.vector.reciprocal(rb[:], rb[:]).then_inc(rinv_done, 1)
            dve.wait_ge(rinv_done, RMS["ln"] + 1)
            for k in range(KT):
                nc.vector.tensor_tensor(glu_tile(k), glu_tile(k), rb[:], ALU.mult).then_inc(ln_scaled, 1)

            def yb_src(k):
                q = SPLIT["yb"] + k
                dve.wait_ge(ln_silu, k + 1)
                dve.wait_ge(split_lo, q - 1)
                nc.vector.tensor_tensor(tmp[q % 2][:], glu_tile(k), tile_of(z_b, k), ALU.mult).then_inc(split_src, 1)

            yb_src(0)
            for k in range(KT):
                if k + 1 < KT:
                    yb_src(k + 1)
                lo_of_tmp(SPLIT["yb"] + k, (h_hi, h_lo), k)
            for b in range(2):
                wait_ring_read(dve, FILL["out_a"] + 6 + b)
            for k in range(KT):
                step.mark(nc.vector.tensor_tensor(tile_of(x, k), tile_of(x, k), tile_of(out_a, k), ALU.add))
            dve.wait_ge(diff_landed, 16 * 8)
            alone(nc.vector.tensor_copy(pos_f, position.bitcast(I32)))
            angle_v = angle.rearrange("p (b j) -> p b j", b=NB)
            for j in range(ROT_HALF):
                rate = float(np.float32(ROPE_THETA ** (-2.0 * j / (2 * ROT_HALF))))
                step.mark(nc.vector.tensor_scalar(angle_v[:, :, j], pos_f, rate, None, ALU.mult))
            step.last(dve)
            alone(nc.vector.tensor_scalar(turns, angle, 1.0 / TWO_PI, ROUNDER, ALU.mult, ALU.add))
            alone(nc.vector.tensor_scalar(turns, turns, -ROUNDER, None, ALU.add))
            for part in TWO_PI_PARTS:
                alone(nc.vector.scalar_tensor_tensor(out=angle, in0=turns, scalar=-part, in1=angle,
                                                     op0=ALU.mult, op1=ALU.add))
            alone(nc.vector.tensor_scalar(angle, angle, SIN_MAX, -SIN_MAX, ALU.min, ALU.max))
            nc.vector.tensor_copy(sines, angle).then_inc(angle_in, 1)
            alone(nc.vector.scalar_tensor_tensor(out=turns, in0=angle, scalar=-1.0, in1=angle, op0=ALU.mult, op1=ALU.max))
            nc.vector.tensor_scalar(cosines, turns, -1.0, TWO_PI / 4, ALU.mult, ALU.add).then_inc(angle_in, 1)
            alone(nc.vector.tensor_tensor(lam_prod, lam_in[:, 0:128], lam_in[:, 128:256], ALU.mult))
            nc.vector.tensor_reduce(lam_e, lam_prod.rearrange("p (g c) -> p g c", g=2), AX_X, ALU.add)\
              .then_inc(lam_in_done, 1)
            for k in range(KT):
                f = FILL["out_b"] + k
                wait_fill(dve, f)
                nc.vector.tensor_tensor(tile_of(x, k), tile_of(x, k), bank(f % 2), ALU.add).then_inc(ring_free[f % 2], 1)
            for b in range(2):
                wait_ring_read(dve, FILL["out_b"] + 6 + b)
            reciprocal_rms("c_norm")
            split_tiles(SPLIT["h3"], (h_hi, h_lo), normed(par[:, PAR["c_norm_w_2"]:PAR["c_norm_w_2"] + 8]))
            for part in (half_q, half_k):
                alone(nc.vector.memset(part, 0.0))
            alone(nc.vector.memset(half_q[:, 0:CHUNK], 1.0))
            nc.vector.memset(half_k[:, CHUNK:P], 8 * NEG).then_inc(halves_done, 1)

            f0 = FILL["dqk"]
            dve.wait_ge(sin_done, 2)
            dve.wait_ge(lam_exp, 1)
            alone(nc.vector.tensor_tensor(neg_lam, lam_e[:, 1:2], lam_e[:, 0:1], ALU.subtract))
            alone(nc.vector.tensor_scalar(neg_lam, neg_lam, -LAM_INIT, None, ALU.add))
            by_head = "p (b h c) -> p b h c"
            cos_b = cosines.rearrange("p (b j) -> p b j", b=NB).unsqueeze(2).to_broadcast([P, NB, 4, ROT_HALF])
            sin_b = sines.rearrange("p (b j) -> p b j", b=NB).unsqueeze(2).to_broadcast([P, NB, 4, ROT_HALF])
            rot_v = [r.rearrange(by_head, b=NB, h=4) for r in rot]
            with dve.Fori(0, 4) as i:
                step.enter(i, 2 * 9)
                for s in range(2):
                    panel = qkv[:, bass.ds(i * 2 * S + s * 8 * S, 2 * S)]
                    for c in range(2):
                        wait_ring_read(dve, f0 + 2 * s + c, 2 * i)
                    alone(nc.vector.tensor_tensor(qk_sq, panel, panel, ALU.mult))
                    nc.vector.tensor_reduce(qk_ms, qk_sq.rearrange("p (g c) -> p g c", c=DH), AX_X, ALU.add)\
                      .then_inc(qk_squared, 1)
                    dve.wait_ge(qk_rms, 2 * i + s + 1)
                    alone(nc.vector.reciprocal(qk_ms, qk_ms))
                    v3 = panel.rearrange("p (g c) -> p g c", c=DH)
                    alone(nc.vector.tensor_tensor(v3, v3, qk_ms.unsqueeze(2).to_broadcast([P, 16, DH]), ALU.mult))
                    alone(nc.vector.tensor_tensor(v3, v3, qk_w[:, 64 * s:64 * s + 64].unsqueeze(1)
                                                  .to_broadcast([P, 16, DH]), ALU.mult))
                    v4 = panel.rearrange(by_head, b=NB, h=4)
                    t1, t2 = v4[:, :, :, 0:ROT_HALF], v4[:, :, :, ROT_HALF:2 * ROT_HALF]
                    for r, (part, turn) in enumerate(((t1, cos_b), (t2, sin_b), (t2, cos_b), (t1, sin_b))):
                        step.mark(nc.vector.tensor_tensor(rot_v[r], part, turn, ALU.mult))
                    step.last(dve)
                    step.mark(nc.vector.tensor_tensor(t1, rot_v[0], rot_v[1], ALU.subtract))
                    nc.vector.tensor_tensor(t2, rot_v[2], rot_v[3], ALU.add).then_inc(qk_prepared, 1)
                    dve.wait_ge(qk_prepared, 2 * i + s + 1)
            step.leave(4)
            dve.wait_ge(diff_landed, 16 * 8)
            alone(nc.vector.tensor_scalar(sub_w, sub_w, 1.0 - LAM_INIT, None, ALU.mult))

            def copy_k_t(h):
                f = diff_t(h, 1)
                wait_fill(dve, f)
                nc.vector.tensor_copy(k_t[:], bank(f % 2)).then_inc(ring_free[f % 2], 1)

            def row_maxima(h):
                for m in range(2):
                    dve.wait_ge(diff_scores, 2 * h + m + 1)
                    c0, base = 8 * (h % 2) + 4 * m, (2 + 3 * m) * 512
                    for i in range(NB):
                        o = base + Q_OFF[i]
                        step.mark(nc.vector.tensor_reduce(lmax[:, c0 + i:c0 + i + 1], psum[:, o:o + (i + 1) * P],
                                                          AX_X, ALU.max))
                    step.last(dve)
                    nc.vector.tensor_scalar(lneg[:, c0:c0 + 4], lmax[:, c0:c0 + 4], -(DH ** -0.5), None, ALU.mult)\
                      .then_inc(diff_neg_max, 1)

            def subln(h):
                q = SPLIT["o"] + h
                wait_ring_read(dve, diff_sum(h))
                alone(nc.vector.reciprocal(rb[:], rb[:]))
                nc.vector.scalar_tensor_tensor(out=tmp[q % 2][:], in0=tmp[q % 2][:], scalar=sub_w, in1=rb[:],
                                               op0=ALU.mult, op1=ALU.mult).then_inc(o_normed, 1)
                wait_ring_read(dve, diff_gate(h))
                dve.wait_ge(o_normed, h + 1)
                nc.vector.tensor_tensor(tmp[q % 2][:], tmp[q % 2][:], d_gate[h % 2], ALU.mult).then_inc(split_src, 1)

            copy_k_t(0)
            row_maxima(0)
            for h in range(HEADS):
                if h + 1 < HEADS:
                    copy_k_t(h + 1)
                dve.wait_ge(diff_exp, 8 * h + 8)
                c0 = 8 * (h % 2)
                alone(nc.vector.reciprocal(linv[:, c0:c0 + 8], lsum[:, c0:c0 + 8]))
                alone(nc.vector.tensor_scalar(linv[:, c0 + 4:c0 + 8], linv[:, c0 + 4:c0 + 8], neg_lam, None, ALU.mult))
                for i in range(NB):
                    w0 = weights[h % 2][:, Q_OFF[i]:Q_OFF[i] + (i + 1) * P]
                    step.mark(nc.vector.tensor_scalar(w0, w0, linv[:, c0 + i:c0 + i + 1], None, ALU.mult))
                step.last(dve)
                for i in range(NB):
                    w0 = weights[h % 2][:, Q_OFF[i]:Q_OFF[i] + (i + 1) * P]
                    nc.vector.scalar_tensor_tensor(out=w0, in0=probs_1[:, Q_OFF[i]:Q_OFF[i] + (i + 1) * P],
                                                   scalar=linv[:, c0 + 4 + i:c0 + 5 + i], in1=w0,
                                                   op0=ALU.mult, op1=ALU.add).then_inc(diff_weights, 1)
                if h:
                    subln(h - 1)
                if h + 1 < HEADS:
                    row_maxima(h + 1)
                if h:
                    lo_of_tmp(SPLIT["o"] + h - 1, (b_hi, b_lo), h - 1)
            subln(HEADS - 1)
            lo_of_tmp(SPLIT["o"] + 7, (b_hi, b_lo), 7)

        @block.tensor
        def _(pe):
            pe.wait_ge(consts_done, CONSTS)
            pe.wait_ge(param_rows, PARAM_DMAS * 16)
            for at, n in PAR_GROUPS:
                last = nc.tensor.transpose(bank(0, n, at), par_rows[0:n, at:at + P], ident[0:n, 0:n])
            last.then_inc(fill_done, 1)
            pe.wait_ge(x_landed, 16)
            pe.wait_ge(silu_c_done, 1)
            for k in range(KT):
                pe.wait_ge(ada_landed[k % 3], 16 * (k // 3 + 1))
                for j in range(KT):
                    last = nc.tensor.matmul(psum[0:1, 1024 + k * PCOL:1024 + (k + 1) * PCOL], silu_c[:, j:j + 1],
                                            ada[k % 3][:, j * PCOL:(j + 1) * PCOL], start=j == 0, stop=j == KT - 1)
                last.then_inc(ada_acc_done, 1)
                for normalised in range(2):
                    f = FILL["x"] + 2 * k + normalised
                    wait_ring_free(pe, f)
                    if normalised and k == 0:
                        pe.wait_ge(x_diag, NB)
                    for b in range(NB):
                        part = x_tok[:, b * D + k * P:b * D + (k + 1) * P]
                        if normalised:
                            last = nc.tensor.matmul(bank(f % 2, P, b * P), part, diag[:, b * P:(b + 1) * P],
                                                    start=True, stop=True)
                        else:
                            last = nc.tensor.transpose(bank(f % 2, P, b * P), part, ident[:])
                    last.then_inc(fill_done, 1)

            def ada_columns(f, bufs, at):
                for j, buf in enumerate(bufs):
                    for c in range(2):
                        col = at + 2 * j + c
                        last = nc.tensor.matmul(bank(f % 2, 1, col), ada_acc[buf][:, c * P:(c + 1) * P], ones[:, 0:1],
                                                start=True, stop=True)
                return last

            pe.wait_ge(mod_rows, 4)
            for j in range(16):
                last = nc.tensor.matmul(bank(6, 1, j), mod_row[j // 4][0:1, (j % 4) * P:(j % 4 + 1) * P], ones[0:1, 0:1],
                                        start=True, stop=True)
            last.then_inc(mod_columns, 1)

            f = FILL["fl"]
            wait_ring_free(pe, f)
            wait_panel(pe, PANEL["fl"])
            product(bank(f % 2), PANEL["fl"] % 2, 0, 0, range(KT), need=SPLIT["h1"]).then_inc(fill_done, 1)
            linear(pe, "mix", 0, None)
            linear(pe, "qk", 0, None)

            def token_major(n, d, f0, df, src=0, need=None, plus_x=None):
                wait_panel(pe, n, d)
                for g in range(2):
                    f = f0 + g
                    wait_ring_free(pe, f, df)
                    for b in (2 * g, 2 * g + 1):
                        for k in range(KT):
                            if need is not None and b == 0:
                                pe.wait_ge(split_lo, need + k + 1)
                            ah = hi[src][:, k * S + b * P:k * S + (b + 1) * P]
                            al = lo[src][:, k * S + b * P:k * S + (b + 1) * P]
                            wh = w_hi[n % 2][:, k * PCOL:(k + 1) * PCOL]
                            wl = w_lo[n % 2][:, k * PCOL:(k + 1) * PCOL]
                            o = bank(f % 2, PCOL, (b % 2) * PCOL)
                            nc.tensor.matmul(o, ah, wh, start=k == 0, stop=False)
                            nc.tensor.matmul(o, ah, wl, start=False, stop=False)
                            last = nc.tensor.matmul(o, al, wh, start=False, stop=k == KT - 1 and plus_x is None)
                        if plus_x is not None:
                            for c in range(2):
                                last = nc.tensor.matmul(bank(f % 2, P, (b % 2) * PCOL + c * P),
                                                        tile_of(x, plus_x + c)[:, b * P:(b + 1) * P], ident[:],
                                                        start=False, stop=c == 1)
                    last.then_inc(fill_done, 1)

            for s in range(2):
                token_major(PANEL["v"] + s, 0, FILL["v"] + 2 * s, 0)

            for j in range(2):
                f = FILL["pool"] + j
                pe.wait_ge(pooled, j + 1)
                pe.wait_ge(small_landed, SMALL_DMAS * 16)
                wait_ring_free(pe, f)
                nc.tensor.matmul(bank(f % 2), w_pool[:, j * P:(j + 1) * P], tile_of(u, j), start=True, stop=True)\
                  .then_inc(fill_done, 1)

            def head_cum(h):
                f = attn_bc(h)
                wait_ring_free(pe, f)
                if h == 0:
                    pe.wait_ge(cum_done, 1)
                nc.tensor.matmul(bank(f % 2), ident[0:HEADS, h:h + 1].to_broadcast([HEADS, P]), flog[0][0:HEADS],
                                 start=True, stop=True).then_inc(fill_done, 1)

            def head_scores(h):
                p0, base = DH * (h % 2), (2 + 3 * (h % 2)) * 512
                q_t = tile_of(qk, h // 2)[p0:p0 + DH]
                k_t = tile_of(qk, 4 + h // 2)[p0:p0 + DH]
                if h == 0:
                    for b in range(2):
                        pe.wait_ge(ring_free[b], (FILL["v"] + 3) // 2)
                if h >= 2:
                    pe.wait_ge(scores_read, h - 1)
                for i in (3, 2, 0, 1):
                    o = base + Q_OFF[i]
                    last = nc.tensor.matmul(psum[:, o:o + (i + 1) * P], q_t[:, i * P:(i + 1) * P],
                                            k_t[:, 0:(i + 1) * P], start=True, stop=True)
                last.then_inc(scores_done, 1)

            head_cum(0)
            head_scores(0)
            for h in range(HEADS):
                if h + 1 < HEADS:
                    head_cum(h + 1)
                    head_scores(h + 1)
                pe.wait_ge(probs_done, 4 * h + 4)
                for fill, blocks in enumerate(((0,), (1, 3), (2,))):
                    f = attn_pt(h, fill)
                    wait_ring_free(pe, f)
                    for j in blocks:
                        for i in range(j, NB):
                            o = K_OFF[j] - 512 * fill + (i - j) * P
                            sc = scores[h % 2][:, Q_OFF[i] + j * P:Q_OFF[i] + (j + 1) * P]
                            last = nc.tensor.transpose(bank(f % 2, P, o), sc, ident[:])
                    last.then_inc(fill_done, 1)
                f, p0 = attn_o(h), DH * (h % 2)
                wait_ring_free(pe, f)
                wait_ring_read(pe, attn_pt(h, 1))
                wait_ring_read(pe, attn_pt(h, 2))
                for j in range(NB):
                    n = (NB - j) * P
                    last = nc.tensor.matmul(bank(f % 2, n, j * P)[p0:p0 + DH], v[:, j * S + h * DH:j * S + (h + 1) * DH],
                                            probs_tr[:, K_OFF[j]:K_OFF[j] + n], start=j == 0, stop=j == NB - 1)
                    if h == HEADS - 1 and j == 0:
                        last.then_inc(branch_done, 1)
                last.then_inc(fill_done, 1)

            n0, f0 = PANEL["gates"], FILL["gates"]
            with pe.Fori(0, 4) as i:
                for s in range(3):
                    wait_panel(pe, n0 + s, 2 * i)
                    for c in range(2):
                        f = f0 + 3 * s + c
                        wait_ring_free(pe, f, 4 * i)
                        product(bank(f % 2), (n0 + s) % 2, c, 0, range(KT)).then_inc(fill_done, 1)
                    if s < 2:
                        f = f0 + 3 * s + 2
                        pe.wait_ge(ada_acc_done, 10 + 2 * s + 4 * i)
                        wait_ring_free(pe, f, 4 * i)
                        ada_columns(f, [0, 1], 0).then_inc(fill_done, 1)
                wait_panel(pe, n0 + 3, 2 * i)
                pe.wait_ge(split_lo, SPLIT["merged"])
                for c in range(2):
                    pe.wait_ge(branch_read, 2 * i + 1)
                    for b, ks in enumerate((range(0, 4), range(4, 6), range(6, 8))):
                        last = product(bank(2 + 3 * c + b), (n0 + 3) % 2, c, 1, ks)
                    last.then_inc(branch_done, 1)
            linear(pe, "wout", 0, SPLIT["merged"])

            def sum_squares(norm):
                for k in range(KT):
                    q = 8 * NORM[norm] + k
                    if k == 0:
                        if NORM[norm]:
                            pe.wait_ge(rms_done, RMS.get(norm, NORM[norm]))
                        else:
                            pe.wait_ge(branch_read, 9)
                    pe.wait_ge(sq_done, q + 1)
                    nc.tensor.matmul(bank(7), ones[:], sq[q % 2][:], start=k == 0, stop=k == KT - 1).then_inc(sq_read, 1)

            sum_squares("mix_post")
            sum_squares("ff_pre")
            n0, f0 = PANEL["ff"], FILL["ff"]
            with pe.Fori(0, 4) as q:
                for s in range(8):
                    wait_panel(pe, n0 + s, 4 * q)
                    for c in range(2):
                        f = f0 + 2 * s + c
                        wait_ring_free(pe, f, 8 * q)
                        need = {(0, 0): SPLIT["h_ff"], (4, 0): SPLIT["hidden"] + 8 * q}.get((s, c))
                        product(bank(f % 2), (n0 + s) % 2, c, s // 4, range(KT), need=need).then_inc(fill_done, 1)
            sum_squares("ff_post")
            sum_squares("a_norm")
            f = FILL["dt"]
            wait_ring_free(pe, f)
            wait_panel(pe, PANEL["dt"])
            product(bank(f % 2), PANEL["dt"] % 2, 0, 0, range(KT), need=SPLIT["h2"]).then_inc(fill_done, 1)
            linear(pe, "glu", 0, None)
            linear(pe, "xbc", 0, None)
            f = FILL["dtt"]
            wait_ring_free(pe, f)
            pe.wait_ge(cum_chunks, NB)
            for j, src in enumerate((dt_tmp[0], cum)):
                for b in range(NB):
                    last = nc.tensor.transpose(bank(f % 2, 16, 64 * j + 16 * b), src[0:SSD_HEADS, b * P:(b + 1) * P],
                                               ident[0:SSD_HEADS, 0:SSD_HEADS])
            last.then_inc(fill_done, 1)
            f = FILL["dtt"] + 1
            wait_ring_free(pe, f)
            wait_ring_read(pe, FILL["dtt"])
            nc.tensor.matmul(bank(f % 2, 64), ident[:, P - 1:P].to_broadcast([P, P]), ncum_tok, start=True, stop=True)\
              .then_inc(fill_done, 1)
            for b in range(3):
                f = FILL["btok"] + b
                wait_ring_free(pe, f)
                pe.wait_ge(xbc_done, 16)
                for g in range(SSD_GROUPS):
                    last = nc.tensor.transpose(bank(f % 2, P, g * P), tile_of(xbc, 8 + g)[:, b * P:(b + 1) * P], ident[:])
                last.then_inc(fill_done, 1)
            for b in range(NB):
                for half in range(2):
                    f = FILL["xtok"] + 2 * b + half
                    wait_ring_free(pe, f)
                    for j in range(4):
                        last = nc.tensor.transpose(bank(f % 2, P, j * P), tile_of(xbc, 4 * half + j)[:, b * P:(b + 1) * P],
                                                   ident[:])
                    last.then_inc(fill_done, 1)

            def group(g):
                for b in range(NB):
                    blk = slice(b * P, (b + 1) * P)
                    last = nc.tensor.matmul(bank(2 + g % 2, P, b * P), tile_of(xbc, 8 + g)[:, blk],
                                            tile_of(xbc, 12 + g)[:, blk], start=True, stop=True)
                last.then_inc(cb_done, 1)
                pe.wait_ge(xdu_done, g + 1)
                if g == 0:
                    wait_ring_read(pe, FILL["btok"] + 1)
                    wait_ring_read(pe, FILL["btok"] + 2)
                base = (4 + 2 * (g % 2)) * 512
                for b in range(3):
                    last = nc.tensor.matmul(psum[:, base + b * 256:base + (b + 1) * 256],
                                            b_tok[:, b * S + g * P:b * S + (g + 1) * P],
                                            xdu[:, b * 256:(b + 1) * 256], start=True, stop=True)
                last.then_inc(states_summed, 1)

            def head_cum_row(h):
                f = ssd_cum(h)
                wait_ring_free(pe, f)
                nc.tensor.matmul(bank(f % 2), ident[0:SSD_HEADS, h:h + 1].to_broadcast([SSD_HEADS, P]), cum[0:SSD_HEADS],
                                 start=True, stop=True).then_inc(fill_done, 1)

            def z_tile(h):
                n, f = PANEL["z"] + h // 2, ssd_z(h)
                wait_panel(pe, n)
                wait_ring_free(pe, f)
                product(bank(f % 2), n % 2, h % 2, 0, range(KT)).then_inc(fill_done, 1)

            head_cum_row(0)
            head_cum_row(1)
            group(0)
            for h in range(SSD_HEADS):
                f, p0, g = ssd_y(h), DH * (h % 2), h // 4
                wait_ring_free(pe, f)
                pe.wait_ge(masked_scores, h + 1)
                pe.wait_ge(states_done, g + 1)
                for b in range(NB):
                    o = bank(f % 2, P, b * P)[p0:p0 + DH]
                    last = nc.tensor.matmul(o, xd[:, b * D + h * DH:b * D + (h + 1) * DH], masked[:, b * P:(b + 1) * P],
                                            start=True, stop=b == 0)
                    if b:
                        last = nc.tensor.matmul(o, state[:, (b - 1) * 256 + (h % 4) * DH:(b - 1) * 256 + (h % 4 + 1) * DH],
                                                c_scaled[:, b * P:(b + 1) * P], start=False, stop=True)
                last.then_inc(fill_done, 1)
                if h % 4 == 2 and g + 1 < SSD_GROUPS:
                    group(g + 1)
                if h < 14:
                    z_tile(h)
                if h + 2 < SSD_HEADS:
                    head_cum_row(h + 2)
            z_tile(14)
            for g in range(SSD_GROUPS):
                for j in range(2):
                    q = SQ["ya"] + 2 * g + j
                    pe.wait_ge(sq_done, q + 1)
                    nc.tensor.matmul(bank(2 + g), ones[:], sq[q % 2][:], start=j == 0, stop=j == 1).then_inc(sq_read, 1)
            z_tile(15)
            pe.wait_ge(dw_done, 9)
            for k in range(KT):
                last = nc.tensor.matmul(bank(6), ones[:], glu_tile(k), start=k == 0, stop=k == KT - 1)
            last.then_inc(ln_summed, 1)
            n0, f0 = PANEL["out_a"], FILL["out_a"]
            for s in range(4):
                wait_panel(pe, n0 + s)
                for c in range(2):
                    f = f0 + 2 * s + c
                    wait_ring_free(pe, f)
                    product(bank(f % 2), (n0 + s) % 2, c, 1, range(KT), need=SPLIT["ya"] if s + c == 0 else None)\
                      .then_inc(fill_done, 1)
                if s == 0:
                    for k in range(KT):
                        q = SQ["ln"] + k
                        pe.wait_ge(sq_done, q + 1)
                        nc.tensor.matmul(bank(7), ones[:], sq[q % 2][:], start=k == 0, stop=k == KT - 1).then_inc(sq_read, 1)
            linear(pe, "out_b", 0, SPLIT["yb"])
            sum_squares("c_norm")
            for seg in ("dqk", "dv"):
                with pe.Fori(0, dict(SEGMENTS)[seg] // 2) as i:
                    for s in range(2):
                        token_major(PANEL[seg] + s, i, FILL[seg] + 2 * s, 2 * i,
                                    need=SPLIT["h3"] if seg == "dqk" and s == 0 else None)

            def q_and_k_t(h):
                for j in range(2):
                    f = diff_t(h, j)
                    wait_ring_free(pe, f)
                    if h == 0:
                        pe.wait_ge(qk_prepared, 8)
                    for b in range(NB):
                        at = j * 4096 + (h // 2) * 1024 + b * PCOL + (h % 2) * P
                        last = nc.tensor.transpose(bank(f % 2, P, b * P), qkv[:, at:at + P], ident[:])
                    last.then_inc(fill_done, 1)

            def diff_head_scores(h):
                for j in range(2):
                    wait_ring_read(pe, diff_t(h, j))
                if h == 0:
                    pe.wait_ge(halves_done, 1)
                    pe.wait_ge(rms_done, RMS["c_norm"] + 1)
                for m in range(2):
                    base, r = (2 + 3 * m) * 512, slice(DH * m, DH * m + DH)
                    if h:
                        pe.wait_ge(diff_exp, 8 * (h - 1) + 4 * (m + 1))
                    for i in (3, 2, 0, 1):
                        o, q_i = base + Q_OFF[i], q_t[r, i * P:(i + 1) * P]
                        if i:
                            nc.tensor.matmul(psum[:, o:o + i * P], q_i, k_t[r, 0:i * P], start=True, stop=True)
                        o += i * P
                        nc.tensor.matmul(psum[:, o:o + P], q_i, k_t[r, i * P:(i + 1) * P], start=True, stop=False)
                        last = nc.tensor.matmul(psum[:, o:o + P], half_q, half_k, start=False, stop=True)
                    last.then_inc(diff_scores, 1)

            q_and_k_t(0)
            diff_head_scores(0)
            for h in range(HEADS):
                if h + 1 < HEADS:
                    q_and_k_t(h + 1)
                    diff_head_scores(h + 1)
                pe.wait_ge(diff_weights, 4 * h + 4)
                for fill, blocks in enumerate(((0,), (1, 3), (2,))):
                    f = diff_wt(h, fill)
                    wait_ring_free(pe, f)
                    for j in blocks:
                        for i in range(j, NB):
                            o = K_OFF[j] - 512 * fill + (i - j) * P
                            part = weights[h % 2][:, Q_OFF[i] + j * P:Q_OFF[i] + (j + 1) * P]
                            last = nc.tensor.transpose(bank(f % 2, P, o), part, ident[:])
                    last.then_inc(fill_done, 1)
                f = diff_o(h)
                wait_ring_free(pe, f)
                for fill in (1, 2):
                    wait_ring_read(pe, diff_wt(h, fill))
                for j in range(NB):
                    n, at = (NB - j) * P, 8192 + (h // 2) * 1024 + j * PCOL + (h % 2) * P
                    part = weights_tr[K_OFF[j] // 512][:, K_OFF[j] % 512:K_OFF[j] % 512 + n]
                    last = nc.tensor.matmul(bank(f % 2, n, j * P), qkv[:, at:at + P], part,
                                            start=j == 0, stop=j == NB - 1)
                last.then_inc(fill_done, 1)
                f, n = diff_gate(h), PANEL["dgate"] + h // 2
                wait_panel(pe, n)
                wait_ring_free(pe, f)
                product(bank(f % 2), n % 2, h % 2, 0, range(KT)).then_inc(fill_done, 1)
                f = diff_sum(h)
                wait_ring_free(pe, f)
                nc.tensor.matmul(bank(f % 2), ones[:], rb[:], start=True, stop=True).then_inc(fill_done, 1)
            for s in range(4):
                n = PANEL["dout"] + s
                token_major(n, 0, FILL["dout"] + 2 * s, 0, src=1, need=SPLIT["o"] if s == 0 else None, plus_x=2 * s)


def log1p(dve, alone, e, w, l, d):
    nc = dve.bass
    alone(nc.vector.tensor_scalar(d, w, -1.0, None, ALU.add))
    alone(nc.vector.tensor_tensor(l, l, e, ALU.mult))
    alone(nc.vector.tensor_scalar(w, d, 0.0, None, ALU.is_equal))
    alone(nc.vector.tensor_scalar(d, d, 1e-30, None, ALU.max))
    alone(nc.vector.reciprocal(d, d))
    alone(nc.vector.tensor_tensor(l, l, d, ALU.mult))
    alone(nc.vector.tensor_tensor(w, w, e, ALU.mult))
    alone(nc.vector.tensor_tensor(l, l, w, ALU.add))


_INS = (
    "x", "c", "w_ada", "b_ada", "g_mix_pre", "g_mix_post", "g_ff_pre", "g_ff_post", "w_in", "b_f", "w_pool",
    "pool_scale", "conv_w", "w_branch", "w_out", "w_ff1", "w_ff2", "positions_2", "a_norm_w_2", "a_w_in_2",
    "a_conv_w_2", "a_conv_b_2", "a_dt_bias_2", "a_a_log_2", "a_d_skip_2", "a_ssd_norm_w_2", "a_dw_w_2",
    "a_dw_b_2", "a_ln_w_2", "a_ln_b_2", "a_w_out_2", "c_norm_w_2", "c_w_in_2", "c_q_norm_w_2", "c_k_norm_w_2",
    "c_lq1_2", "c_lk1_2", "c_lq2_2", "c_lk2_2", "c_subln_w_2", "c_w_out_2",
)


def kernel(**inputs):
    import concourse.bacc as _bacc
    from concourse.bass_utils import run_bass_kernel_spmd as _run

    nc = _bacc.Bacc("TRN2", target_bir_lowering=False, num_devices=1, dynamic_dma_scratch_size=8192)
    arrays, by_name = {}, {}
    for name in _INS:
        a = np.ascontiguousarray(inputs[name])
        arrays[f"in_{name}_dram"] = a
        by_name[name] = nc.dram_tensor(f"in_{name}_dram", a.shape, mybir.dt.from_np(a.dtype),
                                       kind="ExternalInput").ap()
    out = nc.dram_tensor("out_dram", (1, S, D), F32, kind="ExternalOutput").ap()
    hybrid_program(nc, by_name, out)
    return _run(nc, [arrays], core_ids=[0]).results[0]["out_dram"]
```

```python
from contextlib import ExitStack

import concourse.bass as bass
import numpy as np
from concourse import mybir

ALU = mybir.AluOpType
ACT = mybir.ActivationFunctionType
F32 = mybir.dt.float32
F32R = mybir.dt.float32r
I32 = mybir.dt.int32
AX_X = mybir.AxisListType.X

P = 128
S = 512
D = 1024
KT = D // P
NB = S // P
CONSTS = 5
SMALL_DMAS = 8
PARAM_DMAS = 18
PCOL = 256
EPS = 1e-6
LN_EPS = 1e-5
NEG = -1e30
HEADS = 8
DH = 64
WINDOWS = (2, 4, 8, 16)
SSD_HEADS = 16
SSD_GROUPS = 4
SSD_TAPS = 4
DW_TAPS = 31
ROT_HALF = 8
GLU_W = S + DW_TAPS - 1
ROPE_THETA = 500000.0
LAM_INIT = 0.8 - 0.6 * float(np.exp(-0.3))
CHUNK = 64
TWO_PI = 2.0 * np.pi
TWO_PI_PARTS = (6.28125, 0.0019350051879882812, float(TWO_PI - 6.28125 - 0.0019350051879882812))
ROUNDER = 1.5 * 2.0 ** 23
SIN_MAX = 3.1415925

Q_OFF = {3: 0, 2: 512, 0: 896, 1: 1024}
K_OFF = {0: 0, 1: 512, 3: 896, 2: 1024}
PACKED = 1280

PAR = {}
PAR_ROWS = [
    ("c", 8), ("b_ada", 48), ("g_mix_pre", 8), ("g_mix_post", 8), ("g_ff_pre", 8), ("g_ff_post", 8),
    ("pool_scale", 2), ("conv_w", 6), ("a_norm_w_2", 8), ("a_ln_w_2", 8), ("a_ln_b_2", 8), ("a_ssd_norm_w_2", 8),
    ("a_conv_w_2", 64), ("a_conv_b_2", 16), ("a_dw_b_2", 8), ("c_norm_w_2", 8), ("pad", 32),
    ("a_dw_w_2", 248),
]
at_row = 0
for row_name, row_count in PAR_ROWS:
    PAR[row_name] = at_row
    at_row += row_count
PAR_GROUPS = [(0, 128), (128, 96), (256, 128), (384, 120)]

SEGMENTS = [("fl", 1), ("mix", 4), ("qk", 4), ("v", 2), ("gates", 16), ("wout", 4), ("ff", 32),
            ("dt", 1), ("glu", 8), ("xbc", 8), ("z", 8), ("out_a", 4), ("out_b", 4),
            ("dqk", 8), ("dv", 4), ("dgate", 4), ("dout", 4)]
PANEL = {}
panels_so_far = 0
for seg_name, seg_count in SEGMENTS:
    PANEL[seg_name] = panels_so_far
    panels_so_far += seg_count
N_PANELS = panels_so_far

FILLS = [("par", 1), ("x", 16), ("fl", 1), ("mix", 8), ("qk", 8), ("v", 4), ("pool", 2),
         ("attn", 40), ("gates", 32), ("wout", 8), ("ff", 64),
         ("dt", 1), ("glu", 16), ("xbc", 16), ("dtt", 2), ("btok", 3), ("xtok", 8), ("ssd", 48),
         ("out_a", 8), ("out_b", 8), ("dqk", 16), ("dv", 8),
         ("dattn", 64), ("dout", 8)]
FILL = {}
fills_so_far = 0
for fill_name, fill_count in FILLS:
    FILL[fill_name] = fills_so_far
    fills_so_far += fill_count

SPLITS = [("h1", 8), ("conv", 2), ("pool", 2), ("attn", 8), ("merged", 8), ("h_ff", 8), ("hidden", 32),
          ("h2", 8), ("ya", 8), ("yb", 8), ("h3", 8), ("o", 8)]
SPLIT = {}
splits_so_far = 0
for split_name, split_count in SPLITS:
    SPLIT[split_name] = splits_so_far
    splits_so_far += split_count

NOT_BY_DVE = ("pool", "attn", "merged", "hidden")


def dve_source(q):
    return sum(min(max(q + 1 - SPLIT[name], 0), n) for name, n in SPLITS if name not in NOT_BY_DVE)


SUMS = [("mix_post", 4), ("ff_pre", 2), ("ff_post", 4), ("a_norm", 2), ("ya", 2), ("ln", 4), ("c_norm", 2)]
GROUP, TILE_0, ADD_0, SUM_0 = dict(SUMS), {}, {}, {}
adds_so_far = sums_so_far = 0
for sum_at, (sum_name, sum_group) in enumerate(SUMS):
    TILE_0[sum_name], ADD_0[sum_name], SUM_0[sum_name] = 8 * sum_at, adds_so_far, sums_so_far
    adds_so_far += 8 // sum_group * (sum_group - 1)
    sums_so_far += 8 // sum_group
RMS = {"mix_post": 0, "ff_pre": 1, "ff_post": 2, "a_norm": 3, "ya": 4, "ln": 8, "c_norm": 9}


def adds_until(name, k):
    if k < 0:
        at = [n for n, _ in SUMS].index(name)
        return adds_until(SUMS[at - 1][0], k + 8) if at else 0
    g = GROUP[name]
    return ADD_0[name] + k // g * (g - 1) + max(k % g, 1)


def attn_bc(h):
    return FILL["attn"] + (0 if h == 0 else 1 + 5 * (h - 1))


def attn_pt(h, j):
    return FILL["attn"] + 1 + 5 * h + (1 if h < HEADS - 1 else 0) + j


def attn_o(h):
    return attn_pt(h, 3)



def ssd_cum(h):
    return FILL["ssd"] + max(3 * h - 2, 0)


def ssd_y(h):
    return FILL["ssd"] + min(2 + 3 * h, 45)


def ssd_z(h):
    return FILL["ssd"] + (3 + 3 * h if h < 14 else 32 + h)


def diff_first(h):
    return FILL["dattn"] + 2 + 8 * h - (1 if h else 0)


def diff_t(h, j):
    return (diff_first(h - 1) if h else FILL["dattn"]) + j


def diff_gate(h):
    return diff_first(h) + (2 if h < HEADS - 1 else 0) + (1 if h else 0)


def diff_wt(h, j):
    return diff_gate(h) + 1 + j


def diff_o(h):
    return diff_gate(h) + 4


def diff_sum(h):
    return diff_gate(h + 1) - 1 if h < HEADS - 1 else diff_o(h) + 1


class Tally:

    def __init__(self, sem):
        self.sem, self.n = sem, 0

    def mark(self, instruction):
        instruction.then_inc(self.sem, 1)
        self.n = self.n + 1

    def last(self, engine):
        engine.wait_ge(self.sem, self.n)

    def enter(self, turn, per_turn):
        self.before, self.per_turn = self.n, per_turn
        self.n = turn * per_turn + self.before

    def leave(self, turns):
        self.n = self.before + turns * self.per_turn


def hybrid_program(nc, t, out):
    ctx = ExitStack()
    with ctx:
        def sb(name, shape, dtype=F32):
            return ctx.enter_context(nc.sbuf_tensor(name, shape, dtype))

        def sem(name):
            return ctx.enter_context(nc.semaphore(name))

        def row(ap):
            return ap.rearrange("a n -> (a n)").unsqueeze(0) if len(ap.shape) == 2 else ap.unsqueeze(0)

        raw = [sb(f"raw{i}", [P, KT * PCOL]) for i in range(2)]
        w_hi = [sb(f"w_hi{i}", [P, KT * PCOL], F32R) for i in range(2)]
        w_lo = [sb(f"w_lo{i}", [P, KT * PCOL], F32R) for i in range(2)]
        h_hi = sb("h_hi", [P, KT * S], F32R)
        h_lo = sb("h_lo", [P, KT * S], F32R)
        b_offset = nc.sbuf_base
        b_hi = sb("b_hi", [P, KT * S], F32R)
        b_lo = sb("b_lo", [P, KT * S], F32R)
        b_mem = nc.alloc_sbuf_tensor_at("b_mem", [P, 2 * KT * S], F32, offset=b_offset)
        x = sb("resid", [P, KT * S])
        par = sb("par", [P, 512])
        ident = sb("ident", [P, P])
        ones = sb("ones", [P, P])
        causal_offset = nc.sbuf_base
        causal_qk = sb("causal_qk", [P, P])
        causal_kq = sb("causal_kq", [P, P])
        tmp = [sb(f"tmp{i}", [P, S]) for i in range(2)]
        sq = [sb(f"sq{i}", [P, S]) for i in range(2)]
        rb = sb("rb", [P, S])
        small = sb("small", [P, 672])
        arena_offset = nc.sbuf_base
        arena = sb("arena", [P, 18176])
        arena_r = nc.alloc_sbuf_tensor_at("arena_r", [P, 18176], F32R, offset=arena_offset)
        causal_r = nc.alloc_sbuf_tensor_at("causal_r", [P, 2 * P], F32R, offset=causal_offset)

        small_at = [0]

        def little(n):
            small_at[0] += n
            assert small_at[0] <= 672
            return small[:, small_at[0] - n:small_at[0]]

        def place(at, n):
            assert at + n <= 18176, (at, n)
            return arena[:, at:at + n]

        def place_r(at, n):
            return arena_r[:, at:at + n]

        silu_c, mod = little(8), little(48)
        a_mix, g_mix, a_ff, g_ff = little(8), little(8), little(8), little(8)
        ss_x, r_x = little(4), little(4)
        lmax, lneg, lsum, linv = little(4 * HEADS), little(4 * HEADS), little(4 * HEADS), little(4 * HEADS)
        bias_f = little(1)
        eps_t = little(2)
        win_n, win_inv = little(32), little(32)
        win_i = little(16).bitcast(I32)

        xbc = place(0, 16 * S)
        glu = place(8192, KT * GLU_W)
        z_b = place(12528, 4096)
        z_a = place(16624, 512)
        dw_acc_pool = place(17136, 512)
        cum, cum_r = place(17648, 512), place_r(17648, 512)
        cum_copy_t = sq[0][:]
        taps = [tmp[0][:], tmp[1][:]]
        padded = [b_mem[:, 3600 + 520 * j:4115 + 520 * j] for j in range(4)]
        dt_tmp = [b_mem[:, 1040 + 512 * i:1552 + 512 * i] for i in range(5)]
        xd = b_mem[:, 0:4096]
        b_tok = b_mem[:, 4096:5632]
        xdu = b_mem[:, 5632:6400]
        state = b_mem[:, 6400:7168]
        c_scaled = b_mem[:, 7168:7680]
        masked = tmp[0][:]
        csb = tmp[1][:]
        decay = sq
        from_start = [rb[:], b_mem[:, 7680:8192]]
        y_rms = [place(4096 + 512 * g, 512) for g in range(SSD_GROUPS)]
        out_a = place(0, 4096)
        dw_acc = [sq[0][:], sq[1][:]]
        dw_acc_late = place(8 * S, S)
        dt_bias, a_log, a_rate = little(1), little(1), little(1)
        d_all, d_skip = little(16), little(8)
        dt_tok, ncum_tok, to_end, end_decay = little(64), little(64), little(64), little(64)

        qkv = place(0, 12 * 1024)
        qk_sq = place(12288, 1024)
        qk_w = place(13312, 128)
        lam_in = place(13440, 256)
        position = place(13696, 4)
        pos_f, turns, angle = place(13700, 4), place(13704, 32), place(13736, 32)
        cosines, sines, qk_ms = place(13768, 32), place(13800, 32), place(13832, 16)
        rot = [place(13848 + 128 * j, 128) for j in range(4)]
        lam_prod = place(14360, 128)
        d_gate = [place(12288, 512), place(12800, 512)]
        weights = [place(13312, PACKED), place(14592, PACKED)]
        probs_1 = place(15872, PACKED)
        weights_tr = [place(17152, 512), place(17664, 512), par[:, 0:256]]
        final = place(0, 8 * S)
        lam_e, neg_lam, sub_w = little(2), little(1), little(1)

        def glu_tile(k):
            return glu[:, k * GLU_W + DW_TAPS - 1:(k + 1) * GLU_W]

        psum = ctx.enter_context(nc.psum_tensor("psum", [P, 8 * 512], F32))

        def bank(b, n=512, at=0):
            return psum[:, b * 512 + at:b * 512 + at + n]

        landed = [sem("landed0"), sem("landed1")]
        hi_done = sem("hi_done")
        lo_done = sem("lo_done")
        fill_done = sem("fill_done")
        ring_free = [sem("ring_free0"), sem("ring_free1")]
        split_hi = sem("split_hi")
        split_lo = sem("split_lo")
        split_src = sem("split_src")
        param_rows = sem("param_rows")
        small_landed = sem("small_landed")
        consts_done = sem("consts_done")
        pool_step = sem("pool_step")
        x_landed = sem("x_landed")
        ada_landed = [sem(f"ada_landed{i}") for i in range(3)]
        ada_acc_done = sem("ada_acc_done")
        act_step = sem("act_step")
        dve_step = sem("dve_step")
        par_done = sem("par_done")
        x_sumsq = sem("x_sumsq")
        x_rms = sem("x_rms")
        x_diag = sem("x_diag")
        silu_t = sem("silu_t")
        mod_a = sem("mod_a")
        f_logit = sem("f_logit")
        f_exp_in = sem("f_exp_in")
        f_exp = sem("f_exp")
        f_ln = sem("f_ln")
        cum_done = sem("cum_done")
        qk_hi_done = sem("qk_hi_done")
        qk_lo_done = sem("qk_lo_done")
        scores_done = sem("scores_done")
        scores_read = sem("scores_read")
        cum_row = sem("cum_row")
        neg_max = sem("neg_max")
        exp_done = sem("exp_done")
        probs_done = sem("probs_done")
        probs_t = sem("probs_t")
        branch_done = sem("branch_done")
        branch_read = sem("branch_read")
        pooled = sem("pooled")
        sq_done = sem("sq_done")
        tiles_added = sem("tiles_added")
        sums_done = sem("sums_done")
        rms_done = sem("rms_done")
        rinv_done = sem("rinv_done")
        x_ready = sem("x_ready")
        eps_done = sem("eps_done")
        silu_c_done = sem("silu_c_done")
        mod_rows = sem("mod_rows")
        mod_columns = sem("mod_columns")
        out_landed = sem("out_landed")
        cum_chunks = sem("cum_chunks")
        cum_split = sem("cum_split")
        taps_done = sem("taps_done")
        xbc_done = sem("xbc_done")
        ends_done = sem("ends_done")
        ends_exp = sem("ends_exp")
        xdu_done = sem("xdu_done")
        states_summed = sem("states_summed")
        states_done = sem("states_done")
        cb_done = sem("cb_done")
        decay_in = sem("decay_in")
        decay_done = sem("decay_done")
        from_start_done = sem("from_start_done")
        masked_scores = sem("masked_scores")
        gated_y = sem("gated_y")
        dw_in_done = sem("dw_in_done")
        pool_in_done = sem("pool_in_done")
        pool_moved = sem("pool_moved")
        pool_dw_done = sem("pool_dw_done")
        dw_done = sem("dw_done")
        ln_summed = sem("ln_summed")
        ln_mean = sem("ln_mean")
        centred = sem("centred")
        ln_scaled = sem("ln_scaled")
        ln_silu = sem("ln_silu")

        diff_landed = sem("diff_landed")
        diff_hi = sem("diff_hi")
        angle_in = sem("angle_in")
        lam_in_done = sem("lam_in_done")
        sin_done = sem("sin_done")
        lam_exp = sem("lam_exp")
        qk_squared = sem("qk_squared")
        qk_rms = sem("qk_rms")
        qk_prepared = sem("qk_prepared")
        diff_scores = sem("diff_scores")
        diff_neg_max = sem("diff_neg_max")
        diff_exp = sem("diff_exp")
        diff_weights = sem("diff_weights")
        o_squared = sem("o_squared")
        o_rms = sem("o_rms")
        o_rinv = sem("o_rinv")
        o_normed = sem("o_normed")

        hi = h_hi, b_hi
        lo = h_lo, b_lo

        def tile_of(buffer, k):
            return buffer[:, k * S:(k + 1) * S]

        x_tok, xn = place(4096, 4096), place(8192, 4096)
        x_junk, diag = place(12288, 1024), place(13312, 512)
        ada = [place(0, 2048), place(2048, 2048), raw[1][:]]
        w_pool = place(15616, 256)
        ada_acc = [place(15936, 256), place(16192, 256)]
        par_rows = place(13824, 512)
        mod_row = [rb[:], sq[0][:], sq[1][:], tmp[1][:]]
        u = place(0, 4096)
        qk, v = place(4096, 4096), place(8192, 2048)
        scores = [place(10240, PACKED), place(11520, PACKED)]
        probs_tr = place(12800, PACKED)
        cum_bc, cum_bcm = place(14080, 512), place(14592, 512)
        flog = [place(15104, 512), place(10240, 512), place(10752, 512), place(11264, 512), place(11776, 512)]
        pool_sum = [sq[0][:], sq[1][:]]
        cum_hi, cum_lo, ident_1 = place_r(16448, 512), place_r(16960, 512), place_r(17472, 128)
        q_hi, q_lo, k_hi, k_lo = (place_r(2048 + 512 * j, 512) for j in range(4))
        gate = place(4096, 3072)
        merged, gate_tmp = place(7168, 4096), place(11264, 512)
        y = place(0, 4096)
        relu = [place(4096, 512), place(4608, 512)]
        relu_sq = [place(5120, 512), place(5632, 512)]

        def wait_fill(engine, f, d=0):
            engine.wait_ge(fill_done, f + 1 + 2 * d)

        def wait_ring_free(pe, f, d=0):
            if isinstance(d, int) and f // 2 + d == 0:
                return
            pe.wait_ge(ring_free[f % 2], f // 2 + d)

        def wait_ring_read(engine, f, d=0):
            engine.wait_ge(ring_free[f % 2], f // 2 + 1 + d)

        def split_weights_hi(act, n, filled, slot, landings):
            act.wait_ge(landed[slot], landings)
            if filled is not None:
                act.wait_ge(fill_done, filled)
            nc.scalar.activation(w_hi[slot][:], raw[slot][:], ACT.Copy).then_inc(hi_done, 1)

        def panel_hi(act, n, d, filled):
            split_weights_hi(act, n, filled, n % 2, 16 * (n // 2 + 1) + 16 * d)

        def wait_panel(pe, n, d=0):
            pe.wait_ge(lo_done, n + 1 + 2 * d)

        def product(out_ap, slot, c, src, k_range, need=None, n_done=None, start=True, stop=True):
            ks = list(k_range)
            a_hi, a_lo = hi[src], lo[src]
            last = None
            for k in ks:
                if need is not None:
                    nc.tensor.wait_ge(split_lo, need + k + 1)
                wh = w_hi[slot][:, k * PCOL + c * P:k * PCOL + (c + 1) * P]
                wl = w_lo[slot][:, k * PCOL + c * P:k * PCOL + (c + 1) * P]
                nc.tensor.matmul(out_ap, wh, tile_of(a_hi, k), start=start and k == ks[0], stop=False)
                nc.tensor.matmul(out_ap, wh, tile_of(a_lo, k), start=False, stop=False)
                last = nc.tensor.matmul(out_ap, wl, tile_of(a_hi, k), start=False, stop=stop and k == ks[-1])
            return last

        def linear(pe, seg, src, split, count=None, fill=None):
            n0, f0 = PANEL[seg], FILL[fill or seg]
            with pe.Fori(0, (count or dict(SEGMENTS)[seg]) // 2) as i:
                for s in range(2):
                    wait_panel(pe, n0 + s, i)
                    for c in range(2):
                        f = f0 + 2 * s + c
                        wait_ring_free(pe, f, 2 * i)
                        product(bank(f % 2), (n0 + s) % 2, c, src, range(KT),
                                need=split if s == 0 and c == 0 else None).then_inc(fill_done, 1)

        def panel_load(sp, n, d, source):
            sp.dma_start(raw[n % 2][:].rearrange("p (t n) -> p t n", t=KT), source)\
              .then_inc(landed[n % 2], 16)

        def wait_slot(sp, n, d=0):
            if isinstance(d, int) and n + 2 * d < 2:
                return
            sp.wait_ge(lo_done, n - 1 + 2 * d)

        def load_segment(sp, seg, weight, col0, count=None, first=0):
            w = weight.rearrange("(t p) n -> p t n", p=P)
            n0 = PANEL[seg] + first
            count = count or dict(SEGMENTS)[seg]
            if count == 1:
                wait_slot(sp, n0)
                panel_load(sp, n0, 0, w[:, :, col0:col0 + PCOL])
                return
            for s in range(2):
                wait_slot(sp, n0 + s)
                panel_load(sp, n0 + s, 0, w[:, :, col0 + s * PCOL:col0 + (s + 1) * PCOL])
            if count > 2:
                with sp.Fori(1, count // 2) as i:
                    for s in range(2):
                        wait_slot(sp, n0 + s, i)
                        panel_load(sp, n0 + s, i, w[:, :, bass.ds(i * 2 * PCOL + (col0 + s * PCOL), PCOL)])

        w_ada = t["w_ada"][0].rearrange("(t p) n -> p t n", p=P)

        def ada_load(sp, slot, col):
            sp.dma_start(ada[slot].rearrange("p (t n) -> p t n", t=KT), w_ada[:, :, col])\
              .then_inc(ada_landed[slot], 16)

        block = ctx.enter_context(nc.Block())

        @block.sync
        def _(sp):
            sp.dma_start(x_tok.rearrange("p (b d) -> p b d", b=NB),
                         t["x"][0].rearrange("(b p) d -> p b d", p=P)).then_inc(x_landed, 16)
            for a in range(8):
                if a >= 3:
                    sp.wait_ge(ada_acc_done, a - 2)
                ada_load(sp, a % 3, slice(a * PCOL, (a + 1) * PCOL))
                if a == 3:
                    load_segment(sp, "fl", t["w_in"][0], 1536)
            sp.wait_ge(ada_acc_done, 6)
            load_segment(sp, "mix", t["w_in"][0], 1544)
            load_segment(sp, "qk", t["w_in"][0], 0)
            load_segment(sp, "v", t["w_in"][0], 1024)

            w_in = t["w_in"][0].rearrange("(t p) n -> p t n", p=P)
            w_branch = t["w_branch"][0].rearrange("(t p) n -> p t n", p=P)
            n0 = PANEL["gates"]
            with sp.Fori(1, 5) as i:
                for s in range(4):
                    sp.wait_ge(lo_done, n0 + s - 5 + 4 * i)
                    if s < 3:
                        panel_load(sp, n0 + s, 0, w_in[:, :, bass.ds(i * PCOL + (2568 - PCOL + s * D), PCOL)])
                    else:
                        panel_load(sp, n0 + s, 0, w_branch[:, :, bass.ds(i * PCOL - PCOL, PCOL)])
                    if s == 1:
                        sp.wait_ge(split_lo, SPLIT["attn"])
                        sp.wait_ge(scores_done, HEADS)
                        for a in range(2):
                            sp.wait_ge(ada_acc_done, 3 + a + 4 * i)
                            ada_load(sp, a % 2, bass.ds(i * 4 * PCOL + (4 + a) * PCOL, PCOL))
                for a in range(2, 4):
                    sp.wait_ge(ada_acc_done, 3 + a + 4 * i)
                    ada_load(sp, a % 2, bass.ds(i * 4 * PCOL + (4 + a) * PCOL, PCOL))
            load_segment(sp, "wout", t["w_out"][0], 0)

            w1 = t["w_ff1"][0].rearrange("(t p) n -> p t n", p=P)
            w2 = t["w_ff2"][0].rearrange("(q t p) n -> p (q t) n", p=P, t=KT)
            n0 = PANEL["ff"]
            with sp.Fori(0, 4) as q:
                for s in range(4):
                    sp.wait_ge(lo_done, n0 + s - 1 + 8 * q)
                    panel_load(sp, n0 + s, 4 * q, w1[:, :, bass.ds(q * D + s * PCOL, PCOL)])
                for s in range(4, 8):
                    sp.wait_ge(lo_done, n0 + s - 1 + 8 * q)
                    panel_load(sp, n0 + s, 4 * q, w2[:, bass.ds(q * KT, KT), (s - 4) * PCOL:(s - 3) * PCOL])
            w2in = t["a_w_in_2"][0]
            load_segment(sp, "dt", w2in, 3072)
            w2v = w2in.rearrange("(t p) n -> p t n", p=P)
            n0 = PANEL["glu"]
            with sp.Fori(0, 4) as i:
                for s in range(2):
                    sp.wait_ge(lo_done, n0 + s - 1 + 2 * i)
                    panel_load(sp, n0 + s, i, w2v[:, :, bass.ds(i * PCOL + (3088 + s * D), PCOL)])
            load_segment(sp, "xbc", w2in, 1024)
            n0 = PANEL["z"]
            with sp.Fori(0, 4) as i:
                for s, col in enumerate((0, 5136)):
                    sp.wait_ge(lo_done, n0 + s - 1 + 2 * i)
                    panel_load(sp, n0 + s, i, w2v[:, :, bass.ds(i * PCOL + col, PCOL)])
            load_segment(sp, "out_a", t["a_w_out_2"][0][0:D], 0)
            load_segment(sp, "out_b", t["a_w_out_2"][0][D:2 * D], 0)
            w_c = t["c_w_in_2"][0]
            w_cv = w_c.rearrange("(t p) n -> p t n", p=P)
            n0 = PANEL["dqk"]
            with sp.Fori(0, 4) as i:
                for s in range(2):
                    sp.wait_ge(lo_done, n0 + s - 1 + 2 * i)
                    panel_load(sp, n0 + s, i, w_cv[:, :, bass.ds(i * PCOL + s * D, PCOL)])
            load_segment(sp, "dv", w_c, 2 * D)
            load_segment(sp, "dgate", w_c, 3 * D)
            load_segment(sp, "dout", t["c_w_out_2"][0], 0)
            out_v = out[0].rearrange("(b p) d -> p b d", p=P)
            for j in range(8):
                s, g = j // 2, j % 2
                wait_ring_read(sp, FILL["dout"] + j)
                sp.dma_start(out_v[:, 2 * g:2 * g + 2, s * PCOL:(s + 1) * PCOL],
                             tile_of(final, j).rearrange("p (b n) -> p b n", b=2)).then_inc(out_landed, 16)
            sp.wait_ge(out_landed, 16 * 8)

        @block.gpsimd
        def _(pool):
            step = Tally(pool_step)
            step.mark(nc.gpsimd.memset(ones[:], 1.0))
            step.mark(nc.gpsimd.memset(ident[:], 0.0))
            step.mark(nc.gpsimd.memset(causal_qk[:], 0.0))
            step.mark(nc.gpsimd.memset(causal_kq[:], 0.0))
            step.last(pool)
            nc.gpsimd.affine_select(out=ident[:], in_=ident[:], compare_op=ALU.not_equal, fill=1.0, base=0,
                                    pattern=[[-1, P]], channel_multiplier=1).then_inc(consts_done, 1)
            nc.gpsimd.affine_select(out=causal_qk[:], in_=causal_qk[:], compare_op=ALU.is_ge, fill=NEG * 8, base=0,
                                    pattern=[[-1, P]], channel_multiplier=1).then_inc(consts_done, 1)
            nc.gpsimd.affine_select(out=causal_kq[:], in_=causal_kq[:], compare_op=ALU.is_ge, fill=NEG, base=0,
                                    pattern=[[1, P]], channel_multiplier=-1).then_inc(consts_done, 1)
            nc.gpsimd.memset(w_pool, 0.0).then_inc(consts_done, 1)
            nc.gpsimd.iota(win_i, pattern=[[1, 16]], base=1, channel_multiplier=0).then_inc(consts_done, 1)

            def panel_lo(n, d):
                pool.wait_ge(hi_done, n + 1 + 2 * d)
                nc.gpsimd.tensor_tensor(w_lo[n % 2][:], raw[n % 2][:], w_hi[n % 2][:].bitcast(F32), ALU.subtract)\
                  .then_inc(lo_done, 1)

            first = (PANEL["glu"] + 6) // 2 * 2
            with pool.Fori(0, first // 2) as i:
                for s in range(2):
                    panel_lo(s, i)

            def dw_step(number, scratch):
                if number < 2:
                    k, f = 4 + number, FILL["glu"] + 8 + number
                    wait_ring_read(pool, f)
                    wait_ring_read(pool, f + 2)
                    pool.wait_ge(dw_done, 1)
                    nc.gpsimd.tensor_tensor(glu_tile(k), glu_tile(k), tile_of(z_b, k), ALU.mult).then_inc(pool_in_done, 1)
                    return
                k, tap = 4 + (number - 2) // DW_TAPS, (number - 2) % DW_TAPS
                src = glu[:, k * GLU_W + tap:k * GLU_W + tap + S]
                w_tap = par[:, PAR["a_dw_w_2"] + 8 * tap + k:PAR["a_dw_w_2"] + 8 * tap + k + 1]
                if tap == 0:
                    pool.wait_ge(pool_in_done, 2)
                    if k == 5:
                        pool.wait_ge(pool_dw_done, 1)
                    step.mark(nc.gpsimd.tensor_scalar(dw_acc_pool, src, w_tap,
                                                      par[:, PAR["a_dw_b_2"] + k:PAR["a_dw_b_2"] + k + 1],
                                                      ALU.mult, ALU.add))
                    return
                step.last(pool)
                step.mark(nc.gpsimd.tensor_scalar(scratch, src, w_tap, None, ALU.mult))
                step.last(pool)
                if tap == DW_TAPS - 1:
                    nc.gpsimd.tensor_tensor(src, dw_acc_pool, scratch, ALU.add).then_inc(pool_dw_done, 1)
                else:
                    step.mark(nc.gpsimd.tensor_tensor(dw_acc_pool, dw_acc_pool, scratch, ALU.add))

            steps, n_steps = 0, 2 + 2 * DW_TAPS
            for n in range(first, PANEL["out_a"] + 1):
                panel_lo(n, 0)
                more, scratch = (2, tile_of(z_b, 4)) if n <= PANEL["z"] else (6, tile_of(z_b, 7))
                if n == PANEL["z"] + 1:
                    pool.wait_ge(dw_in_done, 6)
                    step.last(pool)
                    nc.gpsimd.memset(tile_of(z_b, 7)[:, 0:1], 0.0).then_inc(pool_moved, 1)
                    pool.wait_ge(pool_moved, 1)
                for number in range(steps, min(steps + more, n_steps)):
                    dw_step(number, scratch)
                steps = min(steps + more, n_steps)
            assert steps == n_steps
            first = PANEL["out_a"] + 1
            if (N_PANELS - first) % 2:
                panel_lo(first, 0)
                first += 1
            with pool.Fori(0, (N_PANELS - first) // 2) as i:
                for s in range(2):
                    panel_lo(first + s, i)

        @block.scalar
        def _(act):
            step = Tally(act_step)

            def rows_of(name):
                ap = t[name]
                flat = ap.rearrange("a n -> (a n)") if len(ap.shape) == 2 else ap.rearrange("a k n -> (a k n)")
                return flat.rearrange("(r p) -> r p", p=P)

            n_rows = [0]

            def load_rows(name, at, r0, r1):
                g, r = at // P, at % P
                act.dma_start(par_rows[r:r + r1 - r0, g * P:(g + 1) * P], rows_of(name)[r0:r1]).then_inc(param_rows, 16)
                n_rows[0] += 16

            for name, count in PAR_ROWS:
                if name == "pad":
                    continue
                if name == "a_dw_w_2":
                    load_rows(name, 256, 0, 128)
                    load_rows(name, 384, 128, 248)
                    continue
                at, done = PAR[name], 0
                while done < count:
                    k = min(count - done, P - (at + done) % P)
                    load_rows(name, at + done, done, done + k)
                    done += k
            assert n_rows[0] == PARAM_DMAS * 16
            with nc.allow_non_contiguous_dma(reason="eight biases"):
                act.dma_start(bias_f[0:HEADS, :], t["b_f"].rearrange("a n -> n a")).then_inc(small_landed, 16)
            act.wait_ge(consts_done, CONSTS)
            for g in range(len(WINDOWS)):
                r = slice(DH * (g % 2), DH * (g % 2) + DH)
                act.dma_start(w_pool[r, (g // 2) * P + DH * (g % 2):(g // 2) * P + DH * (g % 2) + DH],
                              t["w_pool"][0][g]).then_inc(small_landed, 16)
            with nc.allow_non_contiguous_dma(reason="sixteen biases and rates"):
                act.dma_start(dt_bias[0:SSD_HEADS, :], t["a_dt_bias_2"].rearrange("a n -> n a")).then_inc(small_landed, 16)
                act.dma_start(a_log[0:SSD_HEADS, :], t["a_a_log_2"].rearrange("a n -> n a")).then_inc(small_landed, 16)
            act.dma_start(d_all, t["a_d_skip_2"].to_broadcast([P, SSD_HEADS])).then_inc(small_landed, 16)

            act.wait_ge(fill_done, FILL["par"] + 1)
            for at, n in PAR_GROUPS:
                ins = nc.scalar.activation(par[:, at:at + n], bank(0, n, at), ACT.Copy)
                if at == PAR_GROUPS[-1][0]:
                    ins.then_inc(ring_free[0], 1)
            wait_ring_read(act, FILL["par"])
            nc.scalar.activation(silu_c, par[:, 0:8], ACT.Tanh, scale=0.5).then_inc(silu_t, 1)
            act.wait_ge(eps_done, 1)
            act.wait_ge(x_landed, 16)
            for b in range(NB):
                nc.scalar.activation(x_junk, x_tok[:, b * D:(b + 1) * D], ACT.Square,
                                     accum_out=ss_x[:, b:b + 1]).then_inc(x_sumsq, 1)
                act.wait_ge(x_sumsq, b + 1)
            nc.scalar.activation(r_x, ss_x, ACT.Sqrt, bias=eps_t[:, 0:1], scale=1.0 / D).then_inc(x_rms, 1)
            for k in range(KT):
                f = FILL["x"] + 2 * k
                wait_fill(act, f)
                nc.scalar.activation(tile_of(x, k), bank(f % 2), ACT.Copy).then_inc(ring_free[f % 2], 1)
            act.wait_ge(ada_acc_done, 8)
            for j in range(4):
                nc.scalar.activation(mod_row[j][0:1], bank(2 + j)[0:1], ACT.Copy).then_inc(mod_rows, 1)
            panel_hi(act, 0, 0, None)

            def hi_of_tmp(q, dest, k, scale=1.0, bias=None):
                act.wait_ge(split_src, dve_source(q))
                if bias is None:
                    nc.scalar.activation(tile_of(dest, k), tmp[q % 2][:], ACT.Copy).then_inc(split_hi, 1)
                else:
                    nc.scalar.activation(tile_of(dest, k), tmp[q % 2][:], ACT.Identity, bias=bias).then_inc(split_hi, 1)

            for k in range(KT):
                hi_of_tmp(SPLIT["h1"] + k, h_hi, k)

            def evacuate(seg, emit, count=None, fill=None, first=None):
                n0, f0 = PANEL[seg], FILL[fill or seg]
                with act.Fori(0, (count or dict(SEGMENTS)[seg]) // 2) as i:
                    for s in range(2):
                        panel_hi(act, n0 + s + 1, i, f0 + 2 * s + 4 * i)
                        for c in range(2):
                            f = f0 + 2 * s + c
                            wait_fill(act, f, 2 * i)
                            emit(i, 2 * s + c, f)

            def to(dest):
                def emit(i, j, f):
                    nc.scalar.activation(dest[:, bass.ds(i * 4 * S + j * S, S)], bank(f % 2), ACT.Copy)\
                      .then_inc(ring_free[f % 2], 1)
                return emit

            f = FILL["fl"]
            panel_hi(act, PANEL["fl"] + 1, 0, None)
            wait_fill(act, f)
            act.wait_ge(small_landed, SMALL_DMAS * 16)
            nc.scalar.activation(flog[0][0:HEADS], bank(f % 2)[0:HEADS], ACT.Identity, bias=bias_f[0:HEADS, 0:1])\
              .then_inc(ring_free[f % 2], 1)
            act.wait_ge(f_exp_in, 1)
            nc.scalar.activation(flog[1][0:HEADS], flog[1][0:HEADS], ACT.Exp, scale=-1.0).then_inc(f_exp, 1)
            act.wait_ge(f_exp_in, 2)
            nc.scalar.activation(flog[3][0:HEADS], flog[2][0:HEADS], ACT.Ln).then_inc(f_ln, 1)
            evacuate("mix", to(u))
            evacuate("qk", to(qk))
            n0, f0 = PANEL["v"], FILL["v"]
            for s in range(2):
                panel_hi(act, n0 + s + 1, 0, f0 + 2 * s)
                for g in range(2):
                    f = f0 + 2 * s + g
                    wait_fill(act, f)
                    nc.scalar.activation(
                        v.rearrange("p (b n) -> p b n", b=NB)[:, 2 * g:2 * g + 2, s * PCOL:(s + 1) * PCOL],
                        bank(f % 2).rearrange("p (b n) -> p b n", b=2), ACT.Copy).then_inc(ring_free[f % 2], 1)

            for j in range(2):
                hi_of_tmp(SPLIT["conv"] + j, b_hi, 6 + j)

            def from_psum(q, f, dest, k, rows=slice(0, P), scale=1.0):
                wait_fill(act, f)
                act.wait_ge(split_lo, q - 1)
                nc.scalar.activation(tmp[q % 2][rows], bank(f % 2)[rows], ACT.Copy, scale=scale)\
                  .then_inc(ring_free[f % 2], 1)
                wait_ring_read(act, f)
                nc.scalar.activation(tile_of(dest, k)[rows], tmp[q % 2][rows], ACT.Copy).then_inc(split_hi, 1)

            for j in range(2):
                from_psum(SPLIT["pool"] + j, FILL["pool"] + j, b_hi, 4 + j,
                          scale=par[:, PAR["pool_scale"] + j:PAR["pool_scale"] + j + 1])
            def cum_copy(h):
                wait_fill(act, attn_bc(h))
                if h >= 1:
                    act.wait_ge(scores_read, h)
                nc.scalar.activation(cum_bc, bank(attn_bc(h) % 2), ACT.Copy).then_inc(ring_free[attn_bc(h) % 2], 1)

            def qk_split_hi(pair):
                if pair:
                    act.wait_ge(scores_done, 2 * pair)
                for j, dest in enumerate((q_hi, k_hi)):
                    nc.scalar.activation(dest, tile_of(qk, 4 * j + pair), ACT.Copy).then_inc(qk_hi_done, 1)

            for b in range(2):
                wait_ring_read(act, FILL["qk"] + 6 + b)
            qk_split_hi(0)
            cum_copy(0)
            for h in range(HEADS):
                if h + 1 < HEADS:
                    cum_copy(h + 1)
                act.wait_ge(neg_max, h + 1)
                for i in range(NB):
                    sc = scores[h % 2][:, Q_OFF[i]:Q_OFF[i] + (i + 1) * P]
                    nc.scalar.activation(sc, sc, ACT.Exp, bias=lneg[:, 4 * h + i:4 * h + i + 1], scale=DH ** -0.5,
                                         accum_out=lsum[:, 4 * h + i:4 * h + i + 1]).then_inc(exp_done, 1)
                if h % 2 == 0 and h + 2 < HEADS:
                    qk_split_hi(h // 2 + 1)
                for j in range(3):
                    f = attn_pt(h, j)
                    wait_fill(act, f)
                    if j == 0 and h >= 1:
                        wait_fill(act, attn_o(h - 1))
                    n = 256 if j == 2 else 512
                    nc.scalar.activation(probs_tr[:, j * 512:j * 512 + n], bank(f % 2, n), ACT.Copy)\
                      .then_inc(ring_free[f % 2], 1)
                from_psum(SPLIT["attn"] + h, attn_o(h), b_hi, h // 2, slice(DH * (h % 2), DH * (h % 2) + DH))

            n0, f0 = PANEL["gates"], FILL["gates"]
            with act.Fori(0, 4) as i:
                for s in range(4):
                    if s == 0:
                        act.wait_ge(branch_done, 2 * i + 1)
                    panel_hi(act, n0 + s + 1, 2 * i, f0 + (0, 2, 5, 8)[s] + 8 * i)
                    if s == 3:
                        continue
                    for c in range(2):
                        f = f0 + 3 * s + c
                        wait_fill(act, f, 4 * i)
                        if s == 0 and c == 0:
                            act.wait_ge(branch_read, 2 * i + 1)
                        nc.scalar.activation(gate[:, (2 * s + c) * S:(2 * s + c + 1) * S], bank(f % 2), ACT.Tanh,
                                             scale=0.5).then_inc(ring_free[f % 2], 1)
            for k in range(KT):
                q = SPLIT["merged"] + k
                act.wait_ge(branch_read, k + 2)
                wait_fill(act, FILL["wout"] - 1)
                nc.scalar.activation(tile_of(h_hi, k), tile_of(merged, k), ACT.Copy, scale=0.5).then_inc(split_hi, 1)
            n0, f0 = PANEL["wout"], FILL["wout"]

            def square(name, k, tile):
                if adds_until(name, k - 2):
                    act.wait_ge(tiles_added, adds_until(name, k - 2))
                nc.scalar.activation(sq[k % 2][:], tile, ACT.Square).then_inc(sq_done, 1)

            def root(name, n_sums, dest, source, n, eps=0):
                act.wait_ge(sums_done, SUM_0[name] + n_sums)
                nc.scalar.activation(dest, source, ACT.Sqrt, bias=eps_t[:, eps:eps + 1], scale=1.0 / n)\
                  .then_inc(rms_done, 1)

            def squares(norm, source, ready=None):
                for k in range(KT):
                    if ready is not None:
                        act.wait_ge(*ready(k))
                    square(norm, k, tile_of(source, k))
                root(norm, 8 // GROUP[norm], rb[:], bank(7), D)

            for s in range(4):
                panel_hi(act, n0 + s + 1, 0, f0 + 2 * s)
                for c in range(2):
                    k = 2 * s + c
                    wait_fill(act, f0 + k)
                    nc.scalar.activation(tile_of(y, k), bank((f0 + k) % 2), ACT.Copy).then_inc(ring_free[(f0 + k) % 2], 1)
                    wait_ring_read(act, f0 + k)
                    square("mix_post", k, tile_of(y, k))
            root("mix_post", 8 // GROUP["mix_post"], rb[:], bank(7), D)
            squares("ff_pre", x, lambda k: (x_ready, k + 1))
            for k in range(KT):
                hi_of_tmp(SPLIT["h_ff"] + k, h_hi, k, bias=mod[:, 24 + k:25 + k])

            n0, f0 = PANEL["ff"], FILL["ff"]
            def ff_quarter(q):
                for s in range(8):
                    panel_hi(act, n0 + s + 1, 4 * q, f0 + 2 * s + 16 * q)
                    if s >= 4:
                        if isinstance(q, int) and s >= 5:
                            for k in (2 * s - 10, 2 * s - 9):
                                wait_ring_read(act, f0 + 56 + k)
                                square("ff_post", k, tile_of(y, k))
                        continue
                    for c in range(2):
                        j = 2 * s + c
                        f = f0 + j
                        wait_fill(act, f, 8 * q)
                        act.wait_ge(split_lo, SPLIT["hidden"] + j - 1 + 8 * q)
                        nc.scalar.activation(relu[j % 2], bank(f % 2), ACT.Relu).then_inc(ring_free[f % 2], 1)
                        wait_ring_read(act, f, 8 * q)
                        nc.scalar.activation(tile_of(b_hi, j), relu[j % 2], ACT.Square).then_inc(split_hi, 1)

            with act.Fori(0, 3) as q:
                ff_quarter(q)
            ff_quarter(3)
            for k in (6, 7):
                wait_ring_read(act, f0 + 56 + k)
                square("ff_post", k, tile_of(y, k))
            root("ff_post", 8 // GROUP["ff_post"], rb[:], bank(7), D)
            squares("a_norm", x, lambda k: (x_ready, KT + k + 1))
            for k in range(KT):
                hi_of_tmp(SPLIT["h2"] + k, h_hi, k)
            f = FILL["dt"]
            panel_hi(act, PANEL["dt"] + 1, 0, f)
            wait_fill(act, f)
            nc.scalar.activation(dt_tmp[0][0:SSD_HEADS], bank(f % 2)[0:SSD_HEADS], ACT.Identity,
                                 bias=dt_bias[0:SSD_HEADS, 0:1]).then_inc(ring_free[f % 2], 1)
            nc.scalar.activation(a_rate[0:SSD_HEADS], a_log[0:SSD_HEADS], ACT.Exp).then_inc(xbc_done, 1)
            nc.scalar.activation(lam_e[:, 0:1], eps_t[:, 0:1], ACT.Copy).then_inc(xbc_done, 1)
            act.wait_ge(f_exp_in, 3)
            nc.scalar.activation(dt_tmp[1][0:SSD_HEADS], dt_tmp[1][0:SSD_HEADS], ACT.Exp, scale=-1.0).then_inc(f_exp, 1)
            act.wait_ge(f_exp_in, 4)
            nc.scalar.activation(dt_tmp[3][0:SSD_HEADS], dt_tmp[2][0:SSD_HEADS], ACT.Ln).then_inc(f_ln, 1)

            n0, f0 = PANEL["glu"], FILL["glu"]
            with act.Fori(0, 4) as i:
                for s in range(2):
                    panel_hi(act, n0 + s + 1, i, f0 + 2 * s + 4 * i)
                    for c in range(2):
                        f = f0 + 2 * s + c
                        wait_fill(act, f, 2 * i)
                        if s == 0:
                            nc.scalar.activation(glu[:, bass.ds(i * 2 * GLU_W + (c * GLU_W + DW_TAPS - 1), S)], bank(f % 2),
                                                 ACT.Copy).then_inc(ring_free[f % 2], 1)
                        else:
                            nc.scalar.activation(z_b[:, bass.ds(i * 2 * S + c * S, S)], bank(f % 2), ACT.Sigmoid)\
                              .then_inc(ring_free[f % 2], 1)
            n0, f0 = PANEL["xbc"], FILL["xbc"]
            for j in range(16 + 3):
                if j < 16:
                    if j % 2 == 0:
                        panel_hi(act, n0 + j // 2 + 1, 0, f0 + j)
                    f = f0 + j
                    wait_fill(act, f)
                    act.wait_ge(taps_done, j + 1)
                    nc.scalar.activation(padded[j % 4][:, 3:3 + S], bank(f % 2), ACT.Copy).then_inc(ring_free[f % 2], 1)
                if j >= 3:
                    k, bias = j - 3, PAR["a_conv_b_2"] + j - 3
                    act.wait_ge(taps_done, k + 1 + 4)
                    nc.scalar.activation(tile_of(xbc, k), taps[k % 2], ACT.Silu, bias=par[:, bias:bias + 1])\
                      .then_inc(xbc_done, 1)
            act.wait_ge(ends_done, 1)
            nc.scalar.activation(to_end, to_end, ACT.Exp).then_inc(ends_exp, 1)
            nc.scalar.activation(end_decay, end_decay, ACT.Exp).then_inc(ends_exp, 1)
            for b in range(3):
                f = FILL["btok"] + b
                wait_fill(act, f)
                nc.scalar.activation(b_tok[:, b * S:(b + 1) * S], bank(f % 2), ACT.Copy).then_inc(ring_free[f % 2], 1)

            def head_decay(h):
                f = ssd_cum(h)
                wait_fill(act, f)
                if h >= 1:
                    act.wait_ge(decay_in, h)
                    act.wait_ge(from_start_done, h)
                nc.scalar.activation(csb, bank(f % 2), ACT.Copy).then_inc(ring_free[f % 2], 1)
                wait_ring_read(act, f)
                if h >= 2:
                    act.wait_ge(masked_scores, h - 1)
                nc.scalar.activation(from_start[h % 2], csb, ACT.Exp).then_inc(from_start_done, 1)

            def decay_exp(h):
                act.wait_ge(decay_in, h + 1)
                nc.scalar.activation(decay[h % 2][:], decay[h % 2][:], ACT.Exp).then_inc(decay_done, 1)

            def z_silu(h):
                f, k = ssd_z(h), 2 * (h // 4) + h % 2
                wait_fill(act, f)
                if h % 4 < 2 and k:
                    act.wait_ge(gated_y, k)
                if h == 2:
                    act.wait_ge(dw_in_done, 6)
                    act.wait_ge(pool_moved, 1)
                if h == 15:
                    act.wait_ge(pool_dw_done, 2)
                nc.scalar.activation(z_a if h % 4 < 2 else tile_of(z_b, k), bank(f % 2), ACT.Silu)\
                  .then_inc(ring_free[f % 2], 1)

            head_decay(0)
            decay_exp(0)
            for h in range(SSD_HEADS):
                if h + 1 < SSD_HEADS:
                    head_decay(h + 1)
                    decay_exp(h + 1)
                if h % 2 == 0:
                    panel_hi(act, PANEL["z"] + h // 2 + 1, 0, ssd_z(h - 1) + 1 if h else FILL["xbc"] + 16)
                if h < 14:
                    z_silu(h)

            for g in range(SSD_GROUPS):
                for j in range(2):
                    act.wait_ge(gated_y, 2 * g + j + 1)
                    act.wait_ge(masked_scores, SSD_HEADS)
                    square("ya", 2 * g + j, tile_of(xbc, 2 * g + j))
            z_silu(14)
            for g in range(SSD_GROUPS):
                root("ya", g + 1, y_rms[g], bank(2 + g), 256)
            for k in range(KT):
                hi_of_tmp(SPLIT["ya"] + k, b_hi, k)
                if k == 3:
                    z_silu(15)
            act.wait_ge(ln_summed, 1)
            nc.scalar.activation(rb[:], bank(6), ACT.Copy, scale=1.0 / D).then_inc(ln_mean, 1)

            def ln_activation(k):
                act.wait_ge(ln_scaled, k + 1)
                nc.scalar.activation(glu_tile(k), glu_tile(k), ACT.Silu, bias=par[:, PAR["a_ln_b_2"] + k:PAR["a_ln_b_2"] + k + 1],
                                     scale=par[:, PAR["a_ln_w_2"] + k:PAR["a_ln_w_2"] + k + 1]).then_inc(ln_silu, 1)

            n0, f0 = PANEL["out_a"], FILL["out_a"]
            for s in range(4):
                panel_hi(act, n0 + s + 1, 0, f0 + 2 * s)
                for c in range(2):
                    f = f0 + 2 * s + c
                    wait_fill(act, f)
                    nc.scalar.activation(tile_of(out_a, 2 * s + c), bank(f % 2), ACT.Copy).then_inc(ring_free[f % 2], 1)
                if s == 0:
                    for k in range(KT):
                        act.wait_ge(centred, k + 1)
                        square("ln", k, glu_tile(k))
                    root("ln", 8 // GROUP["ln"], rb[:], bank(7), D, 1)
                if s in (1, 2):
                    for k in range(4 * s - 4, 4 * s):
                        ln_activation(k)
            for k in range(KT):
                hi_of_tmp(SPLIT["yb"] + k, h_hi, k)
            panel_hi(act, PANEL["out_b"] + 1, 0, FILL["out_b"])
            act.wait_ge(split_lo, SPLIT["yb"] + KT)
            with nc.allow_non_contiguous_dma(reason="positions and a weight column"):
                act.dma_start(position.bitcast(I32), t["positions_2"].rearrange("a (b p) -> p (a b)", p=P))\
                  .then_inc(diff_landed, 16)
                act.dma_start(sub_w, t["c_subln_w_2"].rearrange("a n -> n a")).then_inc(diff_landed, 16)
            for j, name in enumerate(("c_lq1_2", "c_lq2_2", "c_lk1_2", "c_lk2_2")):
                act.dma_start(lam_in[:, 64 * j:64 * j + 64], t[name].to_broadcast([P, DH])).then_inc(diff_landed, 16)
            for j, name in enumerate(("c_q_norm_w_2", "c_k_norm_w_2")):
                act.dma_start(qk_w[:, 64 * j:64 * j + 64], t[name].to_broadcast([P, DH])).then_inc(diff_landed, 16)
            act.wait_ge(angle_in, 2)
            nc.scalar.activation(sines, sines, ACT.Sin).then_inc(sin_done, 1)
            nc.scalar.activation(cosines, cosines, ACT.Sin).then_inc(sin_done, 1)
            act.wait_ge(lam_in_done, 1)
            nc.scalar.activation(lam_e, lam_e, ACT.Exp).then_inc(lam_exp, 1)
            n0, f0 = PANEL["out_b"], FILL["out_b"]
            for s in range(1, 5):
                if s < 4:
                    panel_hi(act, n0 + s + 1, 0, f0 + 2 * s)
                for k in (2 * s - 2, 2 * s - 1):
                    wait_ring_read(act, f0 + k)
                    square("c_norm", k, tile_of(x, k))
            root("c_norm", 8 // GROUP["c_norm"], rb[:], bank(7), D)
            for k in range(KT):
                hi_of_tmp(SPLIT["h3"] + k, h_hi, k)
            n0, f0 = PANEL["dqk"], FILL["dqk"]
            with act.Fori(0, 4) as i:
                for s in range(2):
                    panel_hi(act, n0 + s + 1, i, f0 + 2 * s + 4 * i)
                    for c in range(2):
                        f = f0 + 2 * s + c
                        wait_fill(act, f, 2 * i)
                        nc.scalar.activation(qkv[:, bass.ds(i * 2 * S + (s * 8 + c) * S, S)], bank(f % 2), ACT.Copy)\
                          .then_inc(ring_free[f % 2], 1)
                    act.wait_ge(qk_squared, 2 * i + s + 1)
                    nc.scalar.activation(qk_ms, qk_ms, ACT.Sqrt, bias=eps_t[:, 0:1], scale=1.0 / DH).then_inc(qk_rms, 1)
            evacuate("dv", to(qkv[:, 8192:12288]))

            def diff_qk_hi(h):
                for j in range(2):
                    f = diff_t(h, j)
                    wait_fill(act, f)
                    nc.scalar.activation(tile_of(b_hi, 6 + j), bank(f % 2), ACT.Copy).then_inc(diff_hi, 1)

            def diff_root(h):
                f = diff_sum(h)
                wait_fill(act, f)
                nc.scalar.activation(rb[:], bank(f % 2), ACT.Sqrt, bias=eps_t[:, 0:1], scale=1.0 / P)\
                  .then_inc(ring_free[f % 2], 1)

            def diff_exps(h):
                for m in range(2):
                    act.wait_ge(diff_neg_max, 2 * h + m + 1)
                    if m == 1 and h:
                        act.wait_ge(diff_weights, 4 * h)
                    if m == 0 and h >= 2:
                        wait_fill(act, diff_wt(h - 2, 2))
                    for i in range(NB):
                        o, n, col = Q_OFF[i], (i + 1) * P, 8 * (h % 2) + 4 * m + i
                        dest = (weights[h % 2], probs_1)[m]
                        nc.scalar.activation(dest[:, o:o + n], psum[:, (2 + 3 * m) * 512 + o:(2 + 3 * m) * 512 + o + n],
                                             ACT.Exp, bias=lneg[:, col:col + 1], scale=DH ** -0.5,
                                             accum_out=lsum[:, col:col + 1]).then_inc(diff_exp, 1)

            diff_qk_hi(0)
            for h in range(HEADS):
                q = SPLIT["o"] + h
                if h + 1 < HEADS:
                    diff_qk_hi(h + 1)
                diff_exps(h)
                if h:
                    diff_root(h - 1)
                if h % 2 == 0:
                    panel_hi(act, PANEL["dgate"] + h // 2 + 1, 0, diff_gate(h - 1) + 1 if h else FILL["dattn"])
                f = diff_gate(h)
                wait_fill(act, f)
                if h >= 2:
                    act.wait_ge(split_src, dve_source(q - 2))
                nc.scalar.activation(d_gate[h % 2], bank(f % 2), ACT.Silu).then_inc(ring_free[f % 2], 1)
                for j in range(3):
                    f, n = diff_wt(h, j), 256 if j == 2 else 512
                    wait_fill(act, f)
                    if j == 0 and h:
                        wait_fill(act, diff_o(h - 1))
                    nc.scalar.activation(weights_tr[j], bank(f % 2, n), ACT.Copy).then_inc(ring_free[f % 2], 1)
                f = diff_o(h)
                wait_fill(act, f)
                act.wait_ge(split_lo, q - 1)
                if h:
                    act.wait_ge(o_normed, h)
                step.mark(nc.scalar.activation(tmp[q % 2][:], bank(f % 2), ACT.Copy))
                nc.scalar.activation(rb[:], bank(f % 2), ACT.Square).then_inc(ring_free[f % 2], 1)
                if h:
                    hi_of_tmp(SPLIT["o"] + h - 1, b_hi, h - 1)
            diff_root(HEADS - 1)
            hi_of_tmp(SPLIT["o"] + 7, b_hi, 7)
            n0, f0 = PANEL["dout"], FILL["dout"]
            for s in range(4):
                if s < 3:
                    panel_hi(act, n0 + s + 1, 0, f0 + 2 * s if s else diff_gate(HEADS - 1) + 1)
                for g in range(2):
                    f = f0 + 2 * s + g
                    wait_fill(act, f)
                    nc.scalar.activation(tile_of(final, 2 * s + g), bank(f % 2), ACT.Copy)\
                      .then_inc(ring_free[f % 2], 1)

        @block.vector
        def _(dve):
            step = Tally(dve_step)

            def alone(instruction):
                step.mark(instruction)
                step.last(dve)

            def ada_panel(a, d, buf):
                for k in range(KT):
                    w = ada[a % 2][:, k * PCOL:(k + 1) * PCOL]
                    if k == 0:
                        ins = nc.vector.tensor_scalar(ada_acc[buf], w, silu_c[:, 0:1], None, ALU.mult)
                    else:
                        ins = nc.vector.scalar_tensor_tensor(out=ada_acc[buf], in0=w, scalar=silu_c[:, k:k + 1],
                                                             in1=ada_acc[buf], op0=ALU.mult, op1=ALU.add)
                    if k == KT - 1:
                        ins.then_inc(ada_acc_done, 1)
                    else:
                        ins.then_inc(dve_step, 1)
                        dve.wait_ge(dve_step, step.n + k + 1)
                step.n = step.n + KT - 1

            alone(nc.vector.memset(eps_t[:, 0:1], EPS))
            nc.vector.memset(eps_t[:, 1:2], LN_EPS).then_inc(eps_done, 1)
            dve.wait_ge(silu_t, 1)
            alone(nc.vector.scalar_tensor_tensor(out=silu_c, in0=silu_c, scalar=1.0, in1=par[:, 0:8],
                                                 op0=ALU.add, op1=ALU.mult))
            nc.vector.tensor_scalar(silu_c, silu_c, 0.5, None, ALU.mult).then_inc(silu_c_done, 1)
            dve.wait_ge(silu_c_done, 1)
            dve.wait_ge(consts_done, CONSTS)
            dve.wait_ge(x_rms, 1)
            alone(nc.vector.reciprocal(r_x, r_x))
            for b in range(NB):
                nc.vector.tensor_scalar(diag[:, b * P:(b + 1) * P], ident[:], r_x[:, b:b + 1], None, ALU.mult)\
                  .then_inc(x_diag, 1)
            for k in range(KT):
                f = FILL["x"] + 2 * k + 1
                wait_fill(dve, f)
                nc.vector.tensor_copy(tile_of(xn, k), bank(f % 2)).then_inc(ring_free[f % 2], 1)
            dve.wait_ge(mod_columns, 1)
            alone(nc.vector.tensor_tensor(mod[:, 0:16], bank(6, 16), par[:, PAR["b_ada"]:PAR["b_ada"] + 16], ALU.add))
            alone(nc.vector.scalar_tensor_tensor(out=a_mix, in0=mod[:, 8:16], scalar=1.0,
                                                 in1=par[:, PAR["g_mix_pre"]:PAR["g_mix_pre"] + 8],
                                                 op0=ALU.add, op1=ALU.mult))

            def lo_of_tmp(q, dest, k, bias=None):
                dve.wait_ge(split_hi, q + 1)
                if bias is None:
                    nc.vector.tensor_tensor(tile_of(dest[1], k), tmp[q % 2][:], tile_of(dest[0], k).bitcast(F32),
                                            ALU.subtract).then_inc(split_lo, 1)
                else:
                    nc.vector.scalar_tensor_tensor(out=tile_of(dest[1], k), in0=tmp[q % 2][:], scalar=bias,
                                                   in1=tile_of(dest[0], k).bitcast(F32),
                                                   op0=ALU.add, op1=ALU.subtract).then_inc(split_lo, 1)

            def split_tiles(q0, dest, source, bias=lambda k: None):
                def src(k):
                    if q0 + k >= 2:
                        dve.wait_ge(split_lo, q0 + k - 1)
                    source(k, tmp[(q0 + k) % 2][:]).then_inc(split_src, 1)
                src(0)
                for k in range(KT):
                    if k + 1 < KT:
                        src(k + 1)
                    lo_of_tmp(q0 + k, dest, k, bias(k))

            split_tiles(SPLIT["h1"], (h_hi, h_lo),
                        lambda k, o: nc.vector.tensor_scalar(o, tile_of(xn, k), a_mix[:, k:k + 1], mod[:, k:k + 1],
                                                             ALU.mult, ALU.add))

            z, e, w, l, d = (b[0:HEADS] for b in flog)
            f = FILL["fl"]
            wait_ring_read(dve, f)
            nc.vector.scalar_tensor_tensor(out=e, in0=z, scalar=-1.0, in1=z, op0=ALU.mult, op1=ALU.max)\
              .then_inc(f_exp_in, 1)
            dve.wait_ge(f_exp, 1)
            nc.vector.tensor_scalar(w, e, 1.0, None, ALU.add).then_inc(f_exp_in, 1)
            dve.wait_ge(f_ln, 1)
            log1p(dve, alone, e, w, l, d)
            alone(nc.vector.scalar_tensor_tensor(out=l, in0=z, scalar=0.0, in1=l, op0=ALU.min, op1=ALU.subtract))
            alone(nc.vector.memset(w, 1.0))
            alone(nc.vector.tensor_tensor_scan(z, w, l, 0.0, ALU.mult, ALU.add))
            alone(nc.vector.tensor_scalar(z, z, -float(DH ** 0.5), None, ALU.mult))
            alone(nc.vector.tensor_copy(cum_hi[0:HEADS], z))
            alone(nc.vector.tensor_copy(ident_1, ident[:]))
            nc.vector.tensor_tensor(cum_lo[0:HEADS], z, cum_hi[0:HEADS].bitcast(F32), ALU.subtract).then_inc(cum_done, 1)

            f0 = FILL["mix"]
            for b in range(2):
                wait_ring_read(dve, f0 + 6 + b)
            alone(nc.vector.memset(win_n, 2.0))
            for j in range(2):
                for half in range(2):
                    r = slice(DH * half, DH * half + DH)
                    win = float(WINDOWS[2 * j + half])
                    alone(nc.vector.tensor_scalar(win_n[r, 16 * j:16 * j + 16], win_i[r], win, None, ALU.min))
            alone(nc.vector.reciprocal(win_inv, win_n))
            for j in range(2):
                value = tile_of(u, j)
                have, reach = value, 1
                for level in range(2 * j + 2):
                    rows = slice(DH, P) if level == 2 * j + 1 else slice(0, P)
                    o = pool_sum[level % 2] if have is not pool_sum[level % 2] else pool_sum[1 - level % 2]
                    if level == 2 * j + 1:
                        alone(nc.vector.tensor_copy(o[0:DH], have[0:DH]))
                    alone(nc.vector.tensor_copy(o[rows, 0:reach], have[rows, 0:reach]))
                    alone(nc.vector.tensor_tensor(o[rows, reach:S], have[rows, reach:S], have[rows, 0:S - reach],
                                                  ALU.add))
                    have, reach = o, 2 * reach
                first = win_n[:, 16 * j:16 * j + 16]
                alone(nc.vector.tensor_tensor(first, have[:, 0:16], win_inv[:, 16 * j:16 * j + 16], ALU.mult))
                alone(nc.vector.tensor_tensor(first, first, value[:, 0:16], ALU.subtract))
                alone(nc.vector.scalar_tensor_tensor(out=value, in0=have, scalar=win_inv[:, 16 * j + 15:16 * j + 16],
                                                     in1=value, op0=ALU.mult, op1=ALU.subtract))
                nc.vector.tensor_copy(value[:, 0:16], first).then_inc(pooled, 1)
            ch, cb, cc = 2, 4, 6
            conv_w = PAR["conv_w"]
            for j in range(2):
                q = SPLIT["conv"] + j
                value, o = tile_of(u, ch + j), tmp[q % 2][:]
                alone(nc.vector.tensor_tensor(value, value, tile_of(u, cc + j), ALU.mult))
                alone(nc.vector.tensor_scalar(o, value, par[:, conv_w + 4 + j:conv_w + 5 + j], None, ALU.mult))
                for lag in (1, 2):
                    col = conv_w + 2 * (2 - lag) + j
                    alone(nc.vector.scalar_tensor_tensor(out=o[:, lag:S], in0=value[:, 0:S - lag],
                                                         scalar=par[:, col:col + 1], in1=o[:, lag:S],
                                                         op0=ALU.mult, op1=ALU.add))
                nc.vector.tensor_tensor(o, o, tile_of(u, cb + j), ALU.mult).then_inc(split_src, 1)
            for j in range(2):
                lo_of_tmp(SPLIT["conv"] + j, (b_hi, b_lo), 6 + j)
            for j in range(2):
                lo_of_tmp(SPLIT["pool"] + j, (b_hi, b_lo), 4 + j)

            def add_bias(h):
                wait_ring_read(dve, attn_bc(h))
                alone(nc.vector.tensor_tensor(cum_bcm.rearrange("p (b n) -> p b n", b=NB),
                                              cum_bc.rearrange("p (b n) -> p b n", b=NB),
                                              causal_qk[:].unsqueeze(1).to_broadcast([P, NB, P]), ALU.add))
                dve.wait_ge(scores_done, h + 1)
                if h >= 2:
                    wait_fill(dve, attn_pt(h - 2, 2))
                sc = scores[h % 2]
                base = (2 + 3 * (h % 2)) * 512
                for i in (3, 2, 0, 1):
                    o = Q_OFF[i]
                    if i:
                        nc.vector.tensor_tensor(sc[:, o:o + i * P], psum[:, base + o:base + o + i * P],
                                                cum_bc[:, 0:i * P], ALU.add).then_inc(dve_step, 1)
                        step.n = step.n + 1
                    o += i * P
                    ins = nc.vector.tensor_tensor(sc[:, o:o + P], psum[:, base + o:base + o + P],
                                                  cum_bcm[:, i * P:(i + 1) * P], ALU.add)
                    if i == 1:
                        step.last(dve)
                        ins.then_inc(scores_read, 1)
                    else:
                        step.mark(ins)
                dve.wait_ge(scores_read, h + 1)
                for i in range(NB):
                    step.mark(nc.vector.tensor_reduce(lmax[:, 4 * h + i:4 * h + i + 1],
                                                      sc[:, Q_OFF[i]:Q_OFF[i] + (i + 1) * P], AX_X, ALU.max))
                step.last(dve)
                nc.vector.tensor_scalar(lneg[:, 4 * h:4 * h + 4], lmax[:, 4 * h:4 * h + 4], -(DH ** -0.5), None,
                                        ALU.mult).then_inc(neg_max, 1)

            def qk_split_lo(pair):
                for j, (high, low) in enumerate(((q_hi, q_lo), (k_hi, k_lo))):
                    dve.wait_ge(qk_hi_done, 2 * pair + j + 1)
                    nc.vector.tensor_tensor(low, tile_of(qk, 4 * j + pair), high.bitcast(F32), ALU.subtract)\
                      .then_inc(qk_lo_done, 1)

            qk_split_lo(0)
            add_bias(0)
            for h in range(HEADS):
                dve.wait_ge(exp_done, 4 * h + 4)
                alone(nc.vector.reciprocal(linv[:, 4 * h:4 * h + 4], lsum[:, 4 * h:4 * h + 4]))
                for i in range(NB):
                    sc = scores[h % 2][:, Q_OFF[i]:Q_OFF[i] + (i + 1) * P]
                    nc.vector.tensor_scalar(sc, sc, linv[:, 4 * h + i:4 * h + i + 1], None, ALU.mult)\
                      .then_inc(probs_done, 1)
                if h + 1 < HEADS:
                    add_bias(h + 1)
                if h % 2 == 0 and h + 2 < HEADS:
                    qk_split_lo(h // 2 + 1)
                p0, q = DH * (h % 2), SPLIT["attn"] + h
                dve.wait_ge(split_hi, q + 1)
                nc.vector.tensor_tensor(tile_of(b_lo, h // 2)[p0:p0 + DH], tmp[q % 2][p0:p0 + DH],
                                        tile_of(b_hi, h // 2)[p0:p0 + DH].bitcast(F32), ALU.subtract)\
                  .then_inc(split_lo, 1)

            nc.vector.memset(gate_tmp, 0.0).then_inc(branch_read, 1)
            per_turn = 4 * (KT - 1) + 2 * 4
            f0 = FILL["gates"]
            with dve.Fori(0, 4) as i:
                step.enter(i, per_turn)
                for g in range(2):
                    for a in (2 * g, 2 * g + 1):
                        dve.wait_ge(ada_landed[a % 2], 16 * (4 + a // 2) + 32 * i)
                        dve.wait_ge(fill_done, f0 + 8 * i + (0 if g == 0 else 3))
                        ada_panel(a, i, a % 2)
                    f = f0 + 2 + 3 * g
                    wait_fill(dve, f, 4 * i)
                    nc.vector.tensor_tensor(mod[:, bass.ds(i * 8 + (16 + 4 * g), 4)], bank(f % 2, 4),
                                            par[:, bass.ds(i * 8 + (PAR["b_ada"] + 16 + 4 * g), 4)], ALU.add)\
                      .then_inc(ring_free[f % 2], 1)
                for c in range(2):
                    wait_ring_read(dve, f0 + 6 + c, 4 * i)
                for c in range(2):
                    dve.wait_ge(branch_done, 2 * i + c + 2)
                    total = merged[:, bass.ds(i * 2 * S + c * S, S)]

                    def gated(b, o):
                        return nc.vector.scalar_tensor_tensor(
                            out=o, in0=gate[:, (2 * b + c) * S:(2 * b + c + 1) * S], scalar=1.0,
                            in1=bank(2 + 3 * c + b), op0=ALU.add, op1=ALU.mult)
                    alone(gated(0, total))
                    alone(gated(1, gate_tmp))
                    alone(nc.vector.tensor_tensor(total, total, gate_tmp, ALU.add))
                    alone(gated(2, gate_tmp))
                    nc.vector.tensor_tensor(total, total, gate_tmp, ALU.add).then_inc(branch_read, 1)
            step.leave(4)
            wait_ring_read(dve, f0 + 26)
            wait_ring_read(dve, f0 + 29)
            alone(nc.vector.tensor_tensor(g_mix, mod[:, 16:24], par[:, PAR["g_mix_post"]:PAR["g_mix_post"] + 8], ALU.mult))
            alone(nc.vector.scalar_tensor_tensor(out=a_ff, in0=mod[:, 32:40], scalar=1.0,
                                                 in1=par[:, PAR["g_ff_pre"]:PAR["g_ff_pre"] + 8],
                                                 op0=ALU.add, op1=ALU.mult))
            alone(nc.vector.tensor_tensor(g_ff, mod[:, 40:48], par[:, PAR["g_ff_post"]:PAR["g_ff_post"] + 8], ALU.mult))
            for k in range(KT):
                q = SPLIT["merged"] + k
                dve.wait_ge(split_hi, q + 1)
                nc.vector.scalar_tensor_tensor(out=tile_of(h_lo, k), in0=tile_of(merged, k), scalar=0.5,
                                               in1=tile_of(h_hi, k).bitcast(F32), op0=ALU.mult, op1=ALU.subtract)\
                  .then_inc(split_lo, 1)

            def add_square(name, k, acc=None):
                g = GROUP[name]
                group, j = k // g, k % g
                if j == 0:
                    return
                acc = acc if acc is not None else tmp[group % 2][:]
                dve.wait_ge(sq_done, TILE_0[name] + k + 1)
                if j == 1 and group >= 2:
                    dve.wait_ge(sums_done, SUM_0[name] + group - 1)
                if j > 1:
                    dve.wait_ge(tiles_added, adds_until(name, k - 1))
                nc.vector.tensor_tensor(acc, sq[(k - 1) % 2][:] if j == 1 else acc, sq[k % 2][:], ALU.add)\
                  .then_inc(tiles_added, 1)

            def add_squares(name):
                for k in range(KT):
                    add_square(name, k)

            def reciprocal_rms(norm):
                n = RMS[norm] + 1
                dve.wait_ge(rms_done, n)
                nc.vector.reciprocal(rb[:], rb[:]).then_inc(rinv_done, 1)
                dve.wait_ge(rinv_done, n)

            def add_normed(gain, next_norm):
                step.mark(nc.vector.tensor_tensor(tile_of(y, 0), tile_of(y, 0), rb[:], ALU.mult))
                for k in range(KT):
                    if k + 1 < KT:
                        step.mark(nc.vector.tensor_tensor(tile_of(y, k + 1), tile_of(y, k + 1), rb[:], ALU.mult))
                    dve.wait_ge(dve_step, step.n - (1 if k + 1 < KT else 0))
                    nc.vector.scalar_tensor_tensor(out=tile_of(x, k), in0=tile_of(y, k), scalar=gain[:, k:k + 1],
                                                   in1=tile_of(x, k), op0=ALU.mult, op1=ALU.add).then_inc(x_ready, 1)
                    if k >= 1:
                        add_square(next_norm, k - 1)
                add_square(next_norm, KT - 1)

            def normed(gain):
                return lambda k, o: nc.vector.scalar_tensor_tensor(out=o, in0=tile_of(x, k), scalar=gain[:, k:k + 1],
                                                                   in1=rb[:], op0=ALU.mult, op1=ALU.mult)

            add_squares("mix_post")
            reciprocal_rms("mix_post")
            add_normed(g_mix, "ff_pre")
            reciprocal_rms("ff_pre")
            split_tiles(SPLIT["h_ff"], (h_hi, h_lo), normed(a_ff), lambda k: mod[:, 24 + k:25 + k])
            alone(nc.vector.memset(y, 0.0))

            f0 = FILL["ff"]
            steps_before = step.n

            def ff_quarter(q):
                step.n = q * 8 + steps_before
                for j in range(KT):
                    f = f0 + j
                    wait_ring_read(dve, f, 8 * q)
                    alone(nc.vector.tensor_tensor(relu_sq[j % 2], relu[j % 2], relu[j % 2], ALU.mult))
                    dve.wait_ge(split_hi, SPLIT["hidden"] + j + 1 + 8 * q)
                    nc.vector.tensor_tensor(tile_of(b_lo, j), relu_sq[j % 2], tile_of(b_hi, j).bitcast(F32),
                                            ALU.subtract).then_inc(split_lo, 1)
                for j in range(KT):
                    f = f0 + 8 + j
                    wait_fill(dve, f, 8 * q)
                    nc.vector.tensor_tensor(tile_of(y, j), tile_of(y, j), bank(f % 2), ALU.add)\
                      .then_inc(ring_free[f % 2], 1)
                    if isinstance(q, int) and j:
                        add_square("ff_post", j - 1)

            with dve.Fori(0, 3) as q:
                ff_quarter(q)
            ff_quarter(3)
            add_square("ff_post", KT - 1)
            reciprocal_rms("ff_post")
            add_normed(g_ff, "a_norm")
            reciprocal_rms("a_norm")
            split_tiles(SPLIT["h2"], (h_hi, h_lo), normed(par[:, PAR["a_norm_w_2"]:PAR["a_norm_w_2"] + 8]))
            for j in range(4):
                nc.vector.memset(padded[j][:, 0:3], 0.0).then_inc(taps_done, 1)
            for half in range(2):
                r = slice(DH * half, DH * half + DH)
                alone(nc.vector.tensor_copy(d_skip[r], d_all[r].rearrange("p (j b) -> p b j", b=2)[:, half]))
            dt, e, w, l, d = (b[0:SSD_HEADS] for b in dt_tmp)
            f = FILL["dt"]
            wait_ring_read(dve, f)
            nc.vector.scalar_tensor_tensor(out=e, in0=dt, scalar=-1.0, in1=dt, op0=ALU.mult, op1=ALU.max)\
              .then_inc(f_exp_in, 1)
            dve.wait_ge(f_exp, 2)
            nc.vector.tensor_scalar(w, e, 1.0, None, ALU.add).then_inc(f_exp_in, 1)
            dve.wait_ge(f_ln, 2)
            log1p(dve, alone, e, w, l, d)
            alone(nc.vector.scalar_tensor_tensor(out=dt, in0=dt, scalar=0.0, in1=l, op0=ALU.max, op1=ALU.add))
            dve.wait_ge(xbc_done, 1)
            alone(nc.vector.tensor_scalar(l, dt, a_rate[0:SSD_HEADS], -1.0, ALU.mult, ALU.mult))
            alone(nc.vector.memset(w, 1.0))
            for b in range(NB):
                nc.vector.tensor_tensor_scan(cum[0:SSD_HEADS, b * P:(b + 1) * P], w[:, b * P:(b + 1) * P],
                                             l[:, b * P:(b + 1) * P], 0.0, ALU.mult, ALU.add).then_inc(cum_chunks, 1)

            nc.vector.memset(glu.rearrange("p (k n) -> p k n", k=KT)[:, :, 0:DW_TAPS - 1], 0.0).then_inc(dw_done, 1)
            f0 = FILL["glu"]
            with dve.Fori(0, 2) as i:
                step.enter(i, 2 * (DW_TAPS - 1))
                dve.wait_ge(dw_done, 2 * i + 1)
                for c in range(2):
                    wait_ring_read(dve, f0 + c, 2 * i)
                    wait_ring_read(dve, f0 + 2 + c, 2 * i)
                    value = glu[:, bass.ds(i * 2 * GLU_W + (c * GLU_W + DW_TAPS - 1), S)]
                    nc.vector.tensor_tensor(value, value, z_b[:, bass.ds(i * 2 * S + c * S, S)], ALU.mult)\
                      .then_inc(dw_in_done, 1)
                dve.wait_ge(dw_in_done, 2 * i + 2)
                for tap in range(DW_TAPS):
                    last = tap == DW_TAPS - 1
                    for c in range(2):
                        if tap:
                            dve.wait_ge(dve_step, step.n - (0 if last and c else 1))
                        src = glu[:, bass.ds(i * 2 * GLU_W + (c * GLU_W + tap), S)]
                        w_tap = par[:, bass.ds(i * 2 + (PAR["a_dw_w_2"] + 8 * tap + c), 1)]
                        if tap == 0:
                            ins = nc.vector.tensor_scalar(dw_acc[c], src, w_tap,
                                                          par[:, bass.ds(i * 2 + (PAR["a_dw_b_2"] + c), 1)],
                                                          ALU.mult, ALU.add)
                        else:
                            ins = nc.vector.scalar_tensor_tensor(out=src if last else dw_acc[c], in0=src, scalar=w_tap,
                                                                 in1=dw_acc[c], op0=ALU.mult, op1=ALU.add)
                        if last:
                            ins.then_inc(dw_done, 1)
                        else:
                            step.mark(ins)
            step.leave(2)
            for k in (6, 7):
                wait_ring_read(dve, f0 + 4 * (k // 2) + k % 2)
                wait_ring_read(dve, f0 + 4 * (k // 2) + 2 + k % 2)
                nc.vector.tensor_tensor(glu_tile(k), glu_tile(k), tile_of(z_b, k), ALU.mult).then_inc(dw_in_done, 1)
            dve.wait_ge(dw_in_done, 6)
            dve.wait_ge(dw_done, 5)

            def dw_taps(k, t0, t1, acc):
                for tap in range(t0, min(t1, DW_TAPS)):
                    src = glu[:, k * GLU_W + tap:k * GLU_W + tap + S]
                    w_tap = par[:, PAR["a_dw_w_2"] + 8 * tap + k:PAR["a_dw_w_2"] + 8 * tap + k + 1]
                    if tap == 0:
                        dve.wait_ge(dw_done, k - 1)
                        alone(nc.vector.tensor_scalar(acc, src, w_tap, par[:, PAR["a_dw_b_2"] + k:PAR["a_dw_b_2"] + k + 1],
                                                      ALU.mult, ALU.add))
                    elif tap < DW_TAPS - 1:
                        alone(nc.vector.scalar_tensor_tensor(out=acc, in0=src, scalar=w_tap, in1=acc,
                                                             op0=ALU.mult, op1=ALU.add))
                    else:
                        nc.vector.scalar_tensor_tensor(out=src, in0=src, scalar=w_tap, in1=acc,
                                                       op0=ALU.mult, op1=ALU.add).then_inc(dw_done, 1)

            f0 = FILL["xbc"]
            with dve.Fori(0, 4) as i:
                step.enter(i, 4 * (SSD_TAPS - 1))
                for j in range(4):
                    f = f0 + j
                    wait_ring_read(dve, f, 2 * i)
                    dve.wait_ge(xbc_done, 4 * i + j + 1)
                    for tap in range(SSD_TAPS):
                        src = padded[j][:, tap:tap + S]
                        w_tap = par[:, bass.ds(i * 4 + (PAR["a_conv_w_2"] + 16 * tap + j), 1)]
                        if tap == 0:
                            alone(nc.vector.tensor_scalar(taps[j % 2], src, w_tap, None, ALU.mult))
                            continue
                        ins = nc.vector.scalar_tensor_tensor(out=taps[j % 2], in0=src, scalar=w_tap, in1=taps[j % 2],
                                                             op0=ALU.mult, op1=ALU.add)
                        if tap == SSD_TAPS - 1:
                            ins.then_inc(taps_done, 1)
                        else:
                            alone(ins)
            step.leave(4)

            f = FILL["dtt"]
            wait_fill(dve, f)
            step.mark(nc.vector.tensor_copy(dt_tok, bank(f % 2, 64)))
            nc.vector.tensor_scalar(ncum_tok, bank(f % 2, 64, 64), -1.0, None, ALU.mult).then_inc(ring_free[f % 2], 1)
            wait_ring_read(dve, f)
            f = FILL["dtt"] + 1
            wait_fill(dve, f)
            step.mark(nc.vector.tensor_scalar(end_decay, bank(f % 2, 64), -1.0, None, ALU.mult))
            step.last(dve)
            nc.vector.tensor_copy(to_end, bank(f % 2, 64)).then_inc(ring_free[f % 2], 1)
            wait_ring_read(dve, f)
            nc.vector.tensor_tensor(to_end, ncum_tok, to_end, ALU.subtract).then_inc(ends_done, 1)
            alone(nc.vector.tensor_copy(cum_copy_t[0:SSD_HEADS], cum[0:SSD_HEADS]))
            alone(nc.vector.tensor_tensor(causal_r[:, 0:SSD_HEADS], ident[:, 0:SSD_HEADS], ident[:, 32:32 + SSD_HEADS],
                                          ALU.add))
            alone(nc.vector.tensor_scalar(cum_r[0:64], ones[0:64, 0:1].to_broadcast([64, S]), 0.0, None, ALU.mult))
            alone(nc.vector.tensor_copy(cum_r[0:SSD_HEADS], cum_copy_t[0:SSD_HEADS]))
            nc.vector.tensor_tensor(cum_r[32:32 + SSD_HEADS], cum_copy_t[0:SSD_HEADS], cum_r[0:SSD_HEADS].bitcast(F32),
                                    ALU.subtract).then_inc(cum_split, 1)
            for b in range(NB):
                for half in range(2):
                    f = FILL["xtok"] + 2 * b + half
                    wait_fill(dve, f)
                    nc.vector.tensor_tensor(
                        xd[:, b * D + half * S:b * D + (half + 1) * S].rearrange("p (h c) -> p h c", h=8),
                        bank(f % 2).rearrange("p (h c) -> p h c", h=8),
                        dt_tok[:, b * 16 + half * 8:b * 16 + half * 8 + 8].unsqueeze(2).to_broadcast([P, 8, DH]),
                        ALU.mult).then_inc(ring_free[f % 2], 1)
            for b in range(2):
                wait_ring_read(dve, FILL["xtok"] + 6 + b)
            dve.wait_ge(ends_exp, 2)

            def end_weighted(g):
                nc.vector.tensor_tensor(
                    xdu.rearrange("p (b h c) -> p b h c", b=3, h=4),
                    xd.rearrange("p (b g h c) -> p b g h c", b=NB, g=SSD_GROUPS, h=4)[:, 0:3, g],
                    to_end.rearrange("p (b g h) -> p b g h", b=NB, g=SSD_GROUPS)[:, 0:3, g].unsqueeze(3)
                    .to_broadcast([P, 3, 4, DH]), ALU.mult).then_inc(xdu_done, 1)

            def states(g):
                dve.wait_ge(states_summed, g + 1)
                if g:
                    wait_fill(dve, ssd_y(4 * g - 1))
                base = (4 + 2 * (g % 2)) * 512
                alone(nc.vector.tensor_copy(state[:, 0:256], psum[:, base:base + 256]))
                for b in (1, 2):
                    here = state[:, b * 256:(b + 1) * 256]
                    alone(nc.vector.tensor_tensor(
                        here.rearrange("p (h c) -> p h c", h=4),
                        state[:, (b - 1) * 256:b * 256].rearrange("p (h c) -> p h c", h=4),
                        end_decay[:, b * 16 + 4 * g:b * 16 + 4 * g + 4].unsqueeze(2).to_broadcast([P, 4, DH]), ALU.mult))
                    ins = nc.vector.tensor_tensor(here, here, psum[:, base + b * 256:base + (b + 1) * 256], ALU.add)
                    if b == 1:
                        alone(ins)
                    else:
                        ins.then_inc(states_done, 1)

            def decay_exponent(h):
                wait_ring_read(dve, ssd_cum(h))
                for b in range(NB):
                    ins = nc.vector.scalar_tensor_tensor(out=decay[h % 2][:, b * P:(b + 1) * P], in0=csb[:, b * P:(b + 1) * P],
                                                         scalar=ncum_tok[:, b * 16 + h:b * 16 + h + 1], in1=causal_kq[:],
                                                         op0=ALU.add, op1=ALU.add)
                    if b < NB - 1:
                        step.mark(ins)
                    else:
                        ins.then_inc(decay_in, 1)

            def head_out(h):
                f, r = ssd_y(h), slice(DH * (h % 2), DH * (h % 2) + DH)
                wait_fill(dve, f)
                part = tile_of(xbc, h // 2)[r]
                nc.vector.scalar_tensor_tensor(out=part, in0=part, scalar=d_skip[r, h // 2:h // 2 + 1], in1=bank(f % 2)[r],
                                               op0=ALU.mult, op1=ALU.add).then_inc(ring_free[f % 2], 1)

            end_weighted(0)
            decay_exponent(0)
            for h in range(SSD_HEADS):
                g = h // 4
                if h >= 1:
                    wait_fill(dve, ssd_y(h - 1))
                dve.wait_ge(from_start_done, h + 1)
                step.mark(nc.vector.tensor_tensor(c_scaled[:, P:S], tile_of(xbc, 12 + g)[:, P:S], from_start[h % 2][:, P:S],
                                                  ALU.mult))
                dve.wait_ge(decay_done, h + 1)
                dve.wait_ge(cb_done, g + 1)
                step.last(dve)
                nc.vector.tensor_tensor(masked, bank(2 + g % 2), decay[h % 2][:], ALU.mult).then_inc(masked_scores, 1)
                if h % 4 == 0:
                    states(g)
                if h + 1 < SSD_HEADS:
                    decay_exponent(h + 1)
                if h % 4 == 0 and g + 1 < SSD_GROUPS:
                    end_weighted(g + 1)
                first, end = 4 * h, 4 * h + 4
                for k in (6, 7):
                    base = DW_TAPS * (k - 6)
                    if first < base + DW_TAPS and end > base:
                        dw_taps(k, max(first - base, 0), end - base, dw_acc_late)
                head_out(h)
                if h % 2:
                    k = h // 2
                    wait_ring_read(dve, ssd_z(4 * (k // 2) + k % 2))
                    wait_ring_read(dve, ssd_y(h))
                    wait_ring_read(dve, ssd_y(h - 1))
                    nc.vector.tensor_tensor(tile_of(xbc, k), tile_of(xbc, k), z_a, ALU.mult).then_inc(gated_y, 1)

            for k in range(KT):
                add_square("ya", k, y_rms[k // 2])

            def ya_src(k):
                g, q, w = k // 2, SPLIT["ya"] + k, PAR["a_ssd_norm_w_2"] + k
                if k % 2 == 0:
                    dve.wait_ge(rms_done, RMS["ya"] + g + 1)
                    nc.vector.reciprocal(y_rms[g], y_rms[g]).then_inc(rinv_done, 1)
                    dve.wait_ge(rinv_done, RMS["ya"] + g + 1)
                dve.wait_ge(split_lo, q - 1)
                nc.vector.scalar_tensor_tensor(out=tmp[q % 2][:], in0=tile_of(xbc, k), scalar=par[:, w:w + 1], in1=y_rms[g],
                                               op0=ALU.mult, op1=ALU.mult).then_inc(split_src, 1)

            ya_src(0)
            for k in range(KT):
                if k + 1 < KT:
                    ya_src(k + 1)
                lo_of_tmp(SPLIT["ya"] + k, (b_hi, b_lo), k)
            dve.wait_ge(ln_mean, 1)
            for k in range(KT):
                nc.vector.tensor_tensor(glu_tile(k), glu_tile(k), rb[:], ALU.subtract).then_inc(centred, 1)
                if k >= 1:
                    add_square("ln", k - 1)
            add_square("ln", KT - 1)
            dve.wait_ge(rms_done, RMS["ln"] + 1)
            nc.vector.reciprocal(rb[:], rb[:]).then_inc(rinv_done, 1)
            dve.wait_ge(rinv_done, RMS["ln"] + 1)
            for k in range(KT):
                nc.vector.tensor_tensor(glu_tile(k), glu_tile(k), rb[:], ALU.mult).then_inc(ln_scaled, 1)

            def yb_src(k):
                q = SPLIT["yb"] + k
                dve.wait_ge(ln_silu, k + 1)
                dve.wait_ge(split_lo, q - 1)
                nc.vector.tensor_tensor(tmp[q % 2][:], glu_tile(k), tile_of(z_b, k), ALU.mult).then_inc(split_src, 1)

            yb_src(0)
            for k in range(KT):
                if k + 1 < KT:
                    yb_src(k + 1)
                lo_of_tmp(SPLIT["yb"] + k, (h_hi, h_lo), k)
            for b in range(2):
                wait_ring_read(dve, FILL["out_a"] + 6 + b)
            for k in range(KT):
                step.mark(nc.vector.tensor_tensor(tile_of(x, k), tile_of(x, k), tile_of(out_a, k), ALU.add))
            dve.wait_ge(diff_landed, 16 * 8)
            alone(nc.vector.tensor_copy(pos_f, position.bitcast(I32)))
            angle_v = angle.rearrange("p (b j) -> p b j", b=NB)
            for j in range(ROT_HALF):
                rate = float(np.float32(ROPE_THETA ** (-2.0 * j / (2 * ROT_HALF))))
                step.mark(nc.vector.tensor_scalar(angle_v[:, :, j], pos_f, rate, None, ALU.mult))
            step.last(dve)
            alone(nc.vector.tensor_scalar(turns, angle, 1.0 / TWO_PI, ROUNDER, ALU.mult, ALU.add))
            alone(nc.vector.tensor_scalar(turns, turns, -ROUNDER, None, ALU.add))
            for part in TWO_PI_PARTS:
                alone(nc.vector.scalar_tensor_tensor(out=angle, in0=turns, scalar=-part, in1=angle,
                                                     op0=ALU.mult, op1=ALU.add))
            alone(nc.vector.tensor_scalar(angle, angle, SIN_MAX, -SIN_MAX, ALU.min, ALU.max))
            nc.vector.tensor_copy(sines, angle).then_inc(angle_in, 1)
            alone(nc.vector.scalar_tensor_tensor(out=turns, in0=angle, scalar=-1.0, in1=angle, op0=ALU.mult, op1=ALU.max))
            nc.vector.tensor_scalar(cosines, turns, -1.0, TWO_PI / 4, ALU.mult, ALU.add).then_inc(angle_in, 1)
            alone(nc.vector.tensor_tensor(lam_prod, lam_in[:, 0:128], lam_in[:, 128:256], ALU.mult))
            nc.vector.tensor_reduce(lam_e, lam_prod.rearrange("p (g c) -> p g c", g=2), AX_X, ALU.add)\
              .then_inc(lam_in_done, 1)
            for k in range(KT):
                f = FILL["out_b"] + k
                wait_fill(dve, f)
                nc.vector.tensor_tensor(tile_of(x, k), tile_of(x, k), bank(f % 2), ALU.add).then_inc(ring_free[f % 2], 1)
                if k >= 1:
                    add_square("c_norm", k - 1)
            add_square("c_norm", KT - 1)
            for b in range(2):
                wait_ring_read(dve, FILL["out_b"] + 6 + b)
            reciprocal_rms("c_norm")
            split_tiles(SPLIT["h3"], (h_hi, h_lo), normed(par[:, PAR["c_norm_w_2"]:PAR["c_norm_w_2"] + 8]))
            f0 = FILL["dqk"]
            dve.wait_ge(sin_done, 2)
            dve.wait_ge(lam_exp, 1)
            alone(nc.vector.tensor_tensor(neg_lam, lam_e[:, 1:2], lam_e[:, 0:1], ALU.subtract))
            alone(nc.vector.tensor_scalar(neg_lam, neg_lam, -LAM_INIT, None, ALU.add))
            by_head = "p (b h c) -> p b h c"
            cos_b = cosines.rearrange("p (b j) -> p b j", b=NB).unsqueeze(2).to_broadcast([P, NB, 4, ROT_HALF])
            sin_b = sines.rearrange("p (b j) -> p b j", b=NB).unsqueeze(2).to_broadcast([P, NB, 4, ROT_HALF])
            rot_v = [r.rearrange(by_head, b=NB, h=4) for r in rot]
            with dve.Fori(0, 4) as i:
                step.enter(i, 2 * 9)
                for s in range(2):
                    panel = qkv[:, bass.ds(i * 2 * S + s * 8 * S, 2 * S)]
                    for c in range(2):
                        wait_ring_read(dve, f0 + 2 * s + c, 2 * i)
                    alone(nc.vector.tensor_tensor(qk_sq, panel, panel, ALU.mult))
                    nc.vector.tensor_reduce(qk_ms, qk_sq.rearrange("p (g c) -> p g c", c=DH), AX_X, ALU.add)\
                      .then_inc(qk_squared, 1)
                    dve.wait_ge(qk_rms, 2 * i + s + 1)
                    alone(nc.vector.reciprocal(qk_ms, qk_ms))
                    v3 = panel.rearrange("p (g c) -> p g c", c=DH)
                    alone(nc.vector.tensor_tensor(v3, v3, qk_ms.unsqueeze(2).to_broadcast([P, 16, DH]), ALU.mult))
                    alone(nc.vector.tensor_tensor(v3, v3, qk_w[:, 64 * s:64 * s + 64].unsqueeze(1)
                                                  .to_broadcast([P, 16, DH]), ALU.mult))
                    v4 = panel.rearrange(by_head, b=NB, h=4)
                    t1, t2 = v4[:, :, :, 0:ROT_HALF], v4[:, :, :, ROT_HALF:2 * ROT_HALF]
                    for r, (part, turn) in enumerate(((t1, cos_b), (t2, sin_b), (t2, cos_b), (t1, sin_b))):
                        step.mark(nc.vector.tensor_tensor(rot_v[r], part, turn, ALU.mult))
                    step.last(dve)
                    step.mark(nc.vector.tensor_tensor(t1, rot_v[0], rot_v[1], ALU.subtract))
                    nc.vector.tensor_tensor(t2, rot_v[2], rot_v[3], ALU.add).then_inc(qk_prepared, 1)
                    dve.wait_ge(qk_prepared, 2 * i + s + 1)
            step.leave(4)
            dve.wait_ge(diff_landed, 16 * 8)
            alone(nc.vector.tensor_scalar(sub_w, sub_w, 1.0 - LAM_INIT, None, ALU.mult))

            def diff_qk_lo(h):
                for j in range(2):
                    f = diff_t(h, j)
                    dve.wait_ge(diff_hi, 2 * h + j + 1)
                    nc.vector.tensor_tensor(tile_of(b_lo, 6 + j), bank(f % 2), tile_of(b_hi, 6 + j).bitcast(F32),
                                            ALU.subtract).then_inc(ring_free[f % 2], 1)

            def row_maxima(h):
                for m in range(2):
                    dve.wait_ge(diff_scores, 2 * h + m + 1)
                    c0, base = 8 * (h % 2) + 4 * m, (2 + 3 * m) * 512
                    for i in range(NB):
                        o = base + Q_OFF[i] + i * P + CHUNK
                        step.mark(nc.vector.memset(psum[0:CHUNK, o:o + CHUNK], NEG))
                    step.last(dve)
                    for i in range(NB):
                        o = base + Q_OFF[i]
                        step.mark(nc.vector.tensor_reduce(lmax[:, c0 + i:c0 + i + 1], psum[:, o:o + (i + 1) * P],
                                                          AX_X, ALU.max))
                    step.last(dve)
                    nc.vector.tensor_scalar(lneg[:, c0:c0 + 4], lmax[:, c0:c0 + 4], -(DH ** -0.5), None, ALU.mult)\
                      .then_inc(diff_neg_max, 1)

            def subln(h):
                q = SPLIT["o"] + h
                wait_ring_read(dve, diff_sum(h))
                alone(nc.vector.reciprocal(rb[:], rb[:]))
                nc.vector.scalar_tensor_tensor(out=tmp[q % 2][:], in0=tmp[q % 2][:], scalar=sub_w, in1=rb[:],
                                               op0=ALU.mult, op1=ALU.mult).then_inc(o_normed, 1)
                wait_ring_read(dve, diff_gate(h))
                dve.wait_ge(o_normed, h + 1)
                nc.vector.tensor_tensor(tmp[q % 2][:], tmp[q % 2][:], d_gate[h % 2], ALU.mult).then_inc(split_src, 1)

            def combine(h):
                dve.wait_ge(diff_exp, 8 * h + 8)
                c0 = 8 * (h % 2)
                alone(nc.vector.reciprocal(linv[:, c0:c0 + 8], lsum[:, c0:c0 + 8]))
                alone(nc.vector.tensor_scalar(linv[:, c0 + 4:c0 + 8], linv[:, c0 + 4:c0 + 8], neg_lam, None, ALU.mult))
                for i in range(NB):
                    w0 = weights[h % 2][:, Q_OFF[i]:Q_OFF[i] + (i + 1) * P]
                    step.mark(nc.vector.tensor_scalar(w0, w0, linv[:, c0 + i:c0 + i + 1], None, ALU.mult))
                step.last(dve)
                for i in range(NB):
                    w0 = weights[h % 2][:, Q_OFF[i]:Q_OFF[i] + (i + 1) * P]
                    nc.vector.scalar_tensor_tensor(out=w0, in0=probs_1[:, Q_OFF[i]:Q_OFF[i] + (i + 1) * P],
                                                   scalar=linv[:, c0 + 4 + i:c0 + 5 + i], in1=w0,
                                                   op0=ALU.mult, op1=ALU.add).then_inc(diff_weights, 1)

            diff_qk_lo(0)
            row_maxima(0)
            for h in range(HEADS):
                if h + 1 < HEADS:
                    diff_qk_lo(h + 1)
                combine(h)
                if h:
                    subln(h - 1)
                if h + 1 < HEADS:
                    row_maxima(h + 1)
                if h:
                    lo_of_tmp(SPLIT["o"] + h - 1, (b_hi, b_lo), h - 1)
            subln(HEADS - 1)
            lo_of_tmp(SPLIT["o"] + 7, (b_hi, b_lo), 7)

        @block.tensor
        def _(pe):
            pe.wait_ge(consts_done, CONSTS)
            pe.wait_ge(param_rows, PARAM_DMAS * 16)
            for at, n in PAR_GROUPS:
                last = nc.tensor.transpose(bank(0, n, at), par_rows[0:n, at:at + P], ident[0:n, 0:n])
            last.then_inc(fill_done, 1)
            pe.wait_ge(x_landed, 16)
            pe.wait_ge(silu_c_done, 1)
            for k in range(KT):
                pe.wait_ge(ada_landed[k % 3], 16 * (k // 3 + 1))
                for j in range(KT):
                    last = nc.tensor.matmul(psum[0:1, 1024 + k * PCOL:1024 + (k + 1) * PCOL], silu_c[:, j:j + 1],
                                            ada[k % 3][:, j * PCOL:(j + 1) * PCOL], start=j == 0, stop=j == KT - 1)
                last.then_inc(ada_acc_done, 1)
                for normalised in range(2):
                    f = FILL["x"] + 2 * k + normalised
                    wait_ring_free(pe, f)
                    if normalised and k == 0:
                        pe.wait_ge(x_diag, NB)
                    for b in range(NB):
                        part = x_tok[:, b * D + k * P:b * D + (k + 1) * P]
                        if normalised:
                            last = nc.tensor.matmul(bank(f % 2, P, b * P), part, diag[:, b * P:(b + 1) * P],
                                                    start=True, stop=True)
                        else:
                            last = nc.tensor.transpose(bank(f % 2, P, b * P), part, ident[:])
                    last.then_inc(fill_done, 1)

            def ada_columns(f, bufs, at):
                for j, buf in enumerate(bufs):
                    for c in range(2):
                        col = at + 2 * j + c
                        last = nc.tensor.matmul(bank(f % 2, 1, col), ada_acc[buf][:, c * P:(c + 1) * P], ones[:, 0:1],
                                                start=True, stop=True)
                return last

            pe.wait_ge(mod_rows, 4)
            for j in range(16):
                last = nc.tensor.matmul(bank(6, 1, j), mod_row[j // 4][0:1, (j % 4) * P:(j % 4 + 1) * P], ones[0:1, 0:1],
                                        start=True, stop=True)
            last.then_inc(mod_columns, 1)

            f = FILL["fl"]
            wait_ring_free(pe, f)
            wait_panel(pe, PANEL["fl"])
            product(bank(f % 2), PANEL["fl"] % 2, 0, 0, range(KT), need=SPLIT["h1"]).then_inc(fill_done, 1)
            linear(pe, "mix", 0, None)
            linear(pe, "qk", 0, None)

            def token_major(n, d, f0, df, src=0, need=None, plus_x=None):
                wait_panel(pe, n, d)
                for g in range(2):
                    f = f0 + g
                    wait_ring_free(pe, f, df)
                    for b in (2 * g, 2 * g + 1):
                        for k in range(KT):
                            if need is not None and b == 0:
                                pe.wait_ge(split_lo, need + k + 1)
                            ah = hi[src][:, k * S + b * P:k * S + (b + 1) * P]
                            al = lo[src][:, k * S + b * P:k * S + (b + 1) * P]
                            wh = w_hi[n % 2][:, k * PCOL:(k + 1) * PCOL]
                            wl = w_lo[n % 2][:, k * PCOL:(k + 1) * PCOL]
                            o = bank(f % 2, PCOL, (b % 2) * PCOL)
                            nc.tensor.matmul(o, ah, wh, start=k == 0, stop=False)
                            nc.tensor.matmul(o, ah, wl, start=False, stop=False)
                            last = nc.tensor.matmul(o, al, wh, start=False, stop=k == KT - 1 and plus_x is None)
                        if plus_x is not None:
                            for c in range(2):
                                last = nc.tensor.matmul(bank(f % 2, P, (b % 2) * PCOL + c * P),
                                                        tile_of(x, plus_x + c)[:, b * P:(b + 1) * P], ident[:],
                                                        start=False, stop=c == 1)
                    last.then_inc(fill_done, 1)

            for s in range(2):
                token_major(PANEL["v"] + s, 0, FILL["v"] + 2 * s, 0)

            for j in range(2):
                f = FILL["pool"] + j
                pe.wait_ge(pooled, j + 1)
                pe.wait_ge(small_landed, SMALL_DMAS * 16)
                wait_ring_free(pe, f)
                nc.tensor.matmul(bank(f % 2), w_pool[:, j * P:(j + 1) * P], tile_of(u, j), start=True, stop=True)\
                  .then_inc(fill_done, 1)

            def head_cum(h):
                f = attn_bc(h)
                wait_ring_free(pe, f)
                if h == 0:
                    pe.wait_ge(cum_done, 1)
                row = ident_1[0:HEADS, h:h + 1].to_broadcast([HEADS, P])
                nc.tensor.matmul(bank(f % 2), row, cum_hi[0:HEADS], start=True, stop=False)
                nc.tensor.matmul(bank(f % 2), row, cum_lo[0:HEADS], start=False, stop=True).then_inc(fill_done, 1)

            def head_scores(h):
                p0, base = DH * (h % 2), (2 + 3 * (h % 2)) * 512
                r = slice(p0, p0 + DH)
                if h == 0:
                    for b in range(2):
                        pe.wait_ge(ring_free[b], (FILL["v"] + 3) // 2)
                if h >= 2:
                    pe.wait_ge(scores_read, h - 1)
                pe.wait_ge(qk_lo_done, 2 * (h // 2) + 2)
                for i in (3, 2, 0, 1):
                    o = base + Q_OFF[i]
                    for number, (q_part, k_part) in enumerate(((q_hi, k_hi), (q_hi, k_lo), (q_lo, k_hi))):
                        last = nc.tensor.matmul(psum[:, o:o + (i + 1) * P], q_part[r, i * P:(i + 1) * P],
                                                k_part[r, 0:(i + 1) * P], start=number == 0, stop=number == 2)
                last.then_inc(scores_done, 1)

            head_cum(0)
            head_scores(0)
            for h in range(HEADS):
                if h + 1 < HEADS:
                    head_cum(h + 1)
                    head_scores(h + 1)
                pe.wait_ge(probs_done, 4 * h + 4)
                for fill, blocks in enumerate(((0,), (1, 3), (2,))):
                    f = attn_pt(h, fill)
                    wait_ring_free(pe, f)
                    for j in blocks:
                        for i in range(j, NB):
                            o = K_OFF[j] - 512 * fill + (i - j) * P
                            sc = scores[h % 2][:, Q_OFF[i] + j * P:Q_OFF[i] + (j + 1) * P]
                            last = nc.tensor.transpose(bank(f % 2, P, o), sc, ident[:])
                    last.then_inc(fill_done, 1)
                f, p0 = attn_o(h), DH * (h % 2)
                wait_ring_free(pe, f)
                wait_ring_read(pe, attn_pt(h, 1))
                wait_ring_read(pe, attn_pt(h, 2))
                for j in range(NB):
                    n = (NB - j) * P
                    last = nc.tensor.matmul(bank(f % 2, n, j * P)[p0:p0 + DH], v[:, j * S + h * DH:j * S + (h + 1) * DH],
                                            probs_tr[:, K_OFF[j]:K_OFF[j] + n], start=j == 0, stop=j == NB - 1)
                    if h == HEADS - 1 and j == 0:
                        last.then_inc(branch_done, 1)
                last.then_inc(fill_done, 1)

            n0, f0 = PANEL["gates"], FILL["gates"]
            with pe.Fori(0, 4) as i:
                for s in range(3):
                    wait_panel(pe, n0 + s, 2 * i)
                    for c in range(2):
                        f = f0 + 3 * s + c
                        wait_ring_free(pe, f, 4 * i)
                        product(bank(f % 2), (n0 + s) % 2, c, 0, range(KT)).then_inc(fill_done, 1)
                    if s < 2:
                        f = f0 + 3 * s + 2
                        pe.wait_ge(ada_acc_done, 10 + 2 * s + 4 * i)
                        wait_ring_free(pe, f, 4 * i)
                        ada_columns(f, [0, 1], 0).then_inc(fill_done, 1)
                wait_panel(pe, n0 + 3, 2 * i)
                pe.wait_ge(split_lo, SPLIT["merged"])
                for c in range(2):
                    pe.wait_ge(branch_read, 2 * i + 1)
                    for b, ks in enumerate((range(0, 4), range(4, 6), range(6, 8))):
                        last = product(bank(2 + 3 * c + b), (n0 + 3) % 2, c, 1, ks)
                    last.then_inc(branch_done, 1)
            linear(pe, "wout", 0, SPLIT["merged"])

            def sum_group(name, group, target, first, last, acc=None):
                g = GROUP[name]
                pe.wait_ge(tiles_added, ADD_0[name] + (group + 1) * (g - 1))
                nc.tensor.matmul(target, ones[:], acc if acc is not None else tmp[group % 2][:], start=first, stop=last)\
                  .then_inc(sums_done, 1)

            def sum_squares(name):
                if RMS[name]:
                    pe.wait_ge(rms_done, RMS[name])
                else:
                    pe.wait_ge(branch_read, 9)
                groups = KT // GROUP[name]
                for group in range(groups):
                    sum_group(name, group, bank(7), group == 0, group == groups - 1)

            sum_squares("mix_post")
            sum_squares("ff_pre")
            n0, f0 = PANEL["ff"], FILL["ff"]
            with pe.Fori(0, 4) as q:
                for s in range(8):
                    wait_panel(pe, n0 + s, 4 * q)
                    for c in range(2):
                        f = f0 + 2 * s + c
                        wait_ring_free(pe, f, 8 * q)
                        need = {(0, 0): SPLIT["h_ff"], (4, 0): SPLIT["hidden"] + 8 * q}.get((s, c))
                        product(bank(f % 2), (n0 + s) % 2, c, s // 4, range(KT), need=need).then_inc(fill_done, 1)
            sum_squares("ff_post")
            sum_squares("a_norm")
            f = FILL["dt"]
            wait_ring_free(pe, f)
            wait_panel(pe, PANEL["dt"])
            product(bank(f % 2), PANEL["dt"] % 2, 0, 0, range(KT), need=SPLIT["h2"]).then_inc(fill_done, 1)
            linear(pe, "glu", 0, None)
            linear(pe, "xbc", 0, None)
            f = FILL["dtt"]
            wait_ring_free(pe, f)
            pe.wait_ge(cum_chunks, NB)
            for j, src in enumerate((dt_tmp[0], cum)):
                for b in range(NB):
                    last = nc.tensor.transpose(bank(f % 2, 16, 64 * j + 16 * b), src[0:SSD_HEADS, b * P:(b + 1) * P],
                                               ident[0:SSD_HEADS, 0:SSD_HEADS])
            last.then_inc(fill_done, 1)
            f = FILL["dtt"] + 1
            wait_ring_free(pe, f)
            wait_ring_read(pe, FILL["dtt"])
            nc.tensor.matmul(bank(f % 2, 64), ident[:, P - 1:P].to_broadcast([P, P]), ncum_tok, start=True, stop=True)\
              .then_inc(fill_done, 1)
            for b in range(3):
                f = FILL["btok"] + b
                wait_ring_free(pe, f)
                pe.wait_ge(xbc_done, 18)
                for g in range(SSD_GROUPS):
                    last = nc.tensor.transpose(bank(f % 2, P, g * P), tile_of(xbc, 8 + g)[:, b * P:(b + 1) * P], ident[:])
                last.then_inc(fill_done, 1)
            for b in range(NB):
                for half in range(2):
                    f = FILL["xtok"] + 2 * b + half
                    wait_ring_free(pe, f)
                    for j in range(4):
                        last = nc.tensor.transpose(bank(f % 2, P, j * P), tile_of(xbc, 4 * half + j)[:, b * P:(b + 1) * P],
                                                   ident[:])
                    last.then_inc(fill_done, 1)

            def group(g):
                for b in range(NB):
                    blk = slice(b * P, (b + 1) * P)
                    last = nc.tensor.matmul(bank(2 + g % 2, P, b * P), tile_of(xbc, 8 + g)[:, blk],
                                            tile_of(xbc, 12 + g)[:, blk], start=True, stop=True)
                last.then_inc(cb_done, 1)
                pe.wait_ge(xdu_done, g + 1)
                if g == 0:
                    wait_ring_read(pe, FILL["btok"] + 1)
                    wait_ring_read(pe, FILL["btok"] + 2)
                base = (4 + 2 * (g % 2)) * 512
                for b in range(3):
                    last = nc.tensor.matmul(psum[:, base + b * 256:base + (b + 1) * 256],
                                            b_tok[:, b * S + g * P:b * S + (g + 1) * P],
                                            xdu[:, b * 256:(b + 1) * 256], start=True, stop=True)
                last.then_inc(states_summed, 1)

            def head_cum_row(h):
                f = ssd_cum(h)
                wait_ring_free(pe, f)
                if h == 0:
                    pe.wait_ge(cum_split, 1)
                nc.tensor.matmul(bank(f % 2), causal_r[0:64, h:h + 1].to_broadcast([64, P]), cum_r[0:64],
                                 start=True, stop=True).then_inc(fill_done, 1)

            def z_tile(h):
                n, f = PANEL["z"] + h // 2, ssd_z(h)
                wait_panel(pe, n)
                wait_ring_free(pe, f)
                product(bank(f % 2), n % 2, h % 2, 0, range(KT)).then_inc(fill_done, 1)

            head_cum_row(0)
            head_cum_row(1)
            group(0)
            for h in range(SSD_HEADS):
                f, p0, g = ssd_y(h), DH * (h % 2), h // 4
                wait_ring_free(pe, f)
                pe.wait_ge(masked_scores, h + 1)
                pe.wait_ge(states_done, g + 1)
                for b in range(NB):
                    o = bank(f % 2, P, b * P)[p0:p0 + DH]
                    last = nc.tensor.matmul(o, xd[:, b * D + h * DH:b * D + (h + 1) * DH], masked[:, b * P:(b + 1) * P],
                                            start=True, stop=b == 0)
                    if b:
                        last = nc.tensor.matmul(o, state[:, (b - 1) * 256 + (h % 4) * DH:(b - 1) * 256 + (h % 4 + 1) * DH],
                                                c_scaled[:, b * P:(b + 1) * P], start=False, stop=True)
                last.then_inc(fill_done, 1)
                if h % 4 == 2 and g + 1 < SSD_GROUPS:
                    group(g + 1)
                if h < 14:
                    z_tile(h)
                if h + 2 < SSD_HEADS:
                    head_cum_row(h + 2)
            z_tile(14)
            for g in range(SSD_GROUPS):
                sum_group("ya", g, bank(2 + g), True, True, y_rms[g])
            z_tile(15)
            pe.wait_ge(dw_done, 7)
            pe.wait_ge(pool_dw_done, 2)
            for k in range(KT):
                last = nc.tensor.matmul(bank(6), ones[:], glu_tile(k), start=k == 0, stop=k == KT - 1)
            last.then_inc(ln_summed, 1)
            n0, f0 = PANEL["out_a"], FILL["out_a"]
            for s in range(4):
                wait_panel(pe, n0 + s)
                for c in range(2):
                    f = f0 + 2 * s + c
                    wait_ring_free(pe, f)
                    product(bank(f % 2), (n0 + s) % 2, c, 1, range(KT), need=SPLIT["ya"] if s + c == 0 else None)\
                      .then_inc(fill_done, 1)
                if s == 0:
                    sum_squares("ln")
            linear(pe, "out_b", 0, SPLIT["yb"])
            sum_squares("c_norm")
            for seg in ("dqk", "dv"):
                with pe.Fori(0, dict(SEGMENTS)[seg] // 2) as i:
                    for s in range(2):
                        token_major(PANEL[seg] + s, i, FILL[seg] + 2 * s, 2 * i,
                                    need=SPLIT["h3"] if seg == "dqk" and s == 0 else None)

            def q_and_k_t(h):
                for j in range(2):
                    f = diff_t(h, j)
                    wait_ring_free(pe, f)
                    if h == 0:
                        pe.wait_ge(qk_prepared, 8)
                    for b in range(NB):
                        at = j * 4096 + (h // 2) * 1024 + b * PCOL + (h % 2) * P
                        last = nc.tensor.transpose(bank(f % 2, P, b * P), qkv[:, at:at + P], ident[:])
                    last.then_inc(fill_done, 1)

            def diff_head_scores(h):
                for j in range(2):
                    wait_ring_read(pe, diff_t(h, j))
                if h == 0:
                    pe.wait_ge(rms_done, RMS["c_norm"] + 1)
                for m in range(2):
                    base, r = (2 + 3 * m) * 512, slice(DH * m, DH * m + DH)
                    if h:
                        pe.wait_ge(diff_exp, 8 * (h - 1) + 4 * (m + 1))
                    for i in (3, 2, 0, 1):
                        o = base + Q_OFF[i]
                        for number, (q_part, k_part) in enumerate(((b_hi, b_hi), (b_hi, b_lo), (b_lo, b_hi))):
                            last = nc.tensor.matmul(psum[:, o:o + (i + 1) * P], q_part[r, 6 * S + i * P:6 * S + (i + 1) * P],
                                                    k_part[r, 7 * S:7 * S + (i + 1) * P], start=number == 0, stop=number == 2)
                    last.then_inc(diff_scores, 1)

            def square_sum(h):
                f = diff_sum(h)
                wait_ring_free(pe, f)
                wait_ring_read(pe, diff_o(h))
                nc.tensor.matmul(bank(f % 2), ones[:], rb[:], start=True, stop=True).then_inc(fill_done, 1)

            q_and_k_t(0)
            diff_head_scores(0)
            for h in range(HEADS):
                if h + 1 < HEADS:
                    q_and_k_t(h + 1)
                if h:
                    square_sum(h - 1)
                f, n = diff_gate(h), PANEL["dgate"] + h // 2
                wait_panel(pe, n)
                wait_ring_free(pe, f)
                product(bank(f % 2), n % 2, h % 2, 0, range(KT)).then_inc(fill_done, 1)
                if h + 1 < HEADS:
                    diff_head_scores(h + 1)
                pe.wait_ge(diff_weights, 4 * h + 4)
                for fill, blocks in enumerate(((0,), (1, 3), (2,))):
                    f = diff_wt(h, fill)
                    wait_ring_free(pe, f)
                    for j in blocks:
                        for i in range(j, NB):
                            o = K_OFF[j] - 512 * fill + (i - j) * P
                            part = weights[h % 2][:, Q_OFF[i] + j * P:Q_OFF[i] + (j + 1) * P]
                            last = nc.tensor.transpose(bank(f % 2, P, o), part, ident[:])
                    last.then_inc(fill_done, 1)
                f = diff_o(h)
                wait_ring_free(pe, f)
                for fill in (1, 2):
                    wait_ring_read(pe, diff_wt(h, fill))
                for j in range(NB):
                    n, at = (NB - j) * P, 8192 + (h // 2) * 1024 + j * PCOL + (h % 2) * P
                    part = weights_tr[K_OFF[j] // 512][:, K_OFF[j] % 512:K_OFF[j] % 512 + n]
                    last = nc.tensor.matmul(bank(f % 2, n, j * P), qkv[:, at:at + P], part,
                                            start=j == 0, stop=j == NB - 1)
                last.then_inc(fill_done, 1)
            square_sum(HEADS - 1)
            for s in range(4):
                n = PANEL["dout"] + s
                token_major(n, 0, FILL["dout"] + 2 * s, 0, src=1, need=SPLIT["o"] if s == 0 else None, plus_x=2 * s)


def log1p(dve, alone, e, w, l, d):
    nc = dve.bass
    alone(nc.vector.tensor_scalar(d, w, -1.0, None, ALU.add))
    alone(nc.vector.tensor_tensor(l, l, e, ALU.mult))
    alone(nc.vector.tensor_scalar(w, d, 0.0, None, ALU.is_equal))
    alone(nc.vector.tensor_scalar(d, d, 1e-30, None, ALU.max))
    alone(nc.vector.reciprocal(d, d))
    alone(nc.vector.tensor_tensor(l, l, d, ALU.mult))
    alone(nc.vector.tensor_tensor(w, w, e, ALU.mult))
    alone(nc.vector.tensor_tensor(l, l, w, ALU.add))


_INS = (
    "x", "c", "w_ada", "b_ada", "g_mix_pre", "g_mix_post", "g_ff_pre", "g_ff_post", "w_in", "b_f", "w_pool",
    "pool_scale", "conv_w", "w_branch", "w_out", "w_ff1", "w_ff2", "positions_2", "a_norm_w_2", "a_w_in_2",
    "a_conv_w_2", "a_conv_b_2", "a_dt_bias_2", "a_a_log_2", "a_d_skip_2", "a_ssd_norm_w_2", "a_dw_w_2",
    "a_dw_b_2", "a_ln_w_2", "a_ln_b_2", "a_w_out_2", "c_norm_w_2", "c_w_in_2", "c_q_norm_w_2", "c_k_norm_w_2",
    "c_lq1_2", "c_lk1_2", "c_lq2_2", "c_lk2_2", "c_subln_w_2", "c_w_out_2",
)


def kernel(**inputs):
    import concourse.bacc as _bacc
    from concourse.bass_utils import run_bass_kernel_spmd as _run

    nc = _bacc.Bacc("TRN2", target_bir_lowering=False, num_devices=1, dynamic_dma_scratch_size=8192)
    arrays, by_name = {}, {}
    for name in _INS:
        a = np.ascontiguousarray(inputs[name])
        arrays[f"in_{name}_dram"] = a
        by_name[name] = nc.dram_tensor(f"in_{name}_dram", a.shape, mybir.dt.from_np(a.dtype),
                                       kind="ExternalInput").ap()
    out = nc.dram_tensor("out_dram", (1, S, D), F32, kind="ExternalOutput").ap()
    hybrid_program(nc, by_name, out)
    return _run(nc, [arrays], core_ids=[0]).results[0]["out_dram"]
```
